# Optimizing a Trainium2 kernel written in Bass

```python
import math
import jax, jax.numpy as jnp
from jax import lax
import numpy as np

D_MODEL = 1024
BATCH = 1
SEQ = 256
DEPTH = 2

CHUNK = 64
Q_BLOCK = 128
N_A_LAYERS = DEPTH // 2
N_B_LAYERS = DEPTH - N_A_LAYERS
RWKV_HEAD = 64
RWKV_HEADS = D_MODEL // RWKV_HEAD
DECAY_LORA = 64
ICLR_LORA = 64
GATE_LORA = 160
LNX_EPS = 64e-5
MLA_HEADS = 16
QK_NOPE = 64
QK_ROPE = 32
V_HEAD = 64
Q_LORA = 384
KV_LORA = 256
ROPE_THETA = 10000.0
NEG_INF = -1e30
D_FF = 2816
CONV_W = 3
NORM_EPS = 1e-6


def rmsnorm(x, g):
    xf = x.astype(jnp.float32)
    y = xf * lax.rsqrt(jnp.mean(xf * xf, axis=-1, keepdims=True) + NORM_EPS)
    return (y * g.astype(jnp.float32)).astype(x.dtype)

def conv_ffn(x, w_in, conv_w, conv_b, w_out):
    T = x.shape[1]
    gate, up = jnp.split(x @ w_in, 2, axis=-1)
    gp = jnp.pad(gate, ((0, 0), (CONV_W - 1, 0), (0, 0)))
    gc = conv_b
    for j in range(CONV_W):
        gc = gc + gp[:, j:j + T, :] * conv_w[j]
    h = jax.nn.gelu(gc) * up
    return h @ w_out

def _rwkv7_step(S, inp):
    r, w, k, v, a, b = inp
    sa = jnp.einsum('bhvk,bhk->bhv', S, a)
    S = S * w[:, :, None, :] + sa[..., None] * b[:, :, None, :] + v[..., None] * k[:, :, None, :]
    y = jnp.einsum('bhvk,bhk->bhv', S, r)
    return S, y

def rwkv7_time_mix(x, mu, w_rkv, w0, w1, w2, a0, a1, a2, g1, g2, k_k, k_a, r_k, lnx_w, lnx_b, w_o):
    B, T, D = x.shape
    H, N = RWKV_HEADS, RWKV_HEAD
    f32 = jnp.float32
    x_prev = jnp.pad(x, ((0, 0), (1, 0), (0, 0)))[:, :T]
    xx = x_prev - x
    xs = x[None] + xx[None] * mu[:, None, None, :]
    rkv = jnp.einsum('nbtd,nde->nbte', xs[:3], w_rkv)
    r, k, v = rkv[0], rkv[1], rkv[2]
    xw, xa, xg = xs[3], xs[4], xs[5]
    w_log = -jax.nn.softplus(-(w0 + jnp.tanh(xw @ w1) @ w2)) - 0.5
    decay = jnp.exp(-jnp.exp(w_log.astype(f32)))
    a = jax.nn.sigmoid(a0 + (xa @ a1) @ a2)
    g = jax.nn.sigmoid(xg @ g1) @ g2
    kk = (k * k_k).reshape(B, T, H, N).astype(f32)
    kk = kk / jnp.maximum(jnp.sqrt(jnp.sum(kk * kk, axis=-1, keepdims=True)), 1e-12)
    k = k * (1.0 + (a - 1.0) * k_a)
    heads = lambda t: t.reshape(B, T, H, N).astype(f32)
    rh, kh, vh, wh, ah = heads(r), heads(k), heads(v), heads(decay), heads(a)
    seq = tuple(jnp.moveaxis(t, 1, 0) for t in (rh, wh, kh, vh, -kk, kk * ah))
    S0 = jnp.zeros((B, H, N, N), f32)
    _, y = lax.scan(_rwkv7_step, S0, seq)
    y = jnp.moveaxis(y, 0, 1)
    mean = jnp.mean(y, axis=-1, keepdims=True)
    var = jnp.mean(jnp.square(y - mean), axis=-1, keepdims=True)
    yn = ((y - mean) * lax.rsqrt(var + LNX_EPS)).reshape(B, T, D) * lnx_w + lnx_b
    bonus = (jnp.sum(rh * kh * r_k, axis=-1, keepdims=True) * vh).reshape(B, T, D)
    out = ((yn + bonus) * g).astype(x.dtype)
    return out @ w_o

def rope_tables(T):
    inv = 1.0 / (ROPE_THETA ** (jnp.arange(0, QK_ROPE, 2, dtype=jnp.float32) / QK_ROPE))
    ang = jnp.arange(T, dtype=jnp.float32)[:, None] * inv[None, :]
    return jnp.cos(ang), jnp.sin(ang)

def apply_rope(x, cos, sin):
    half = x.shape[-1] // 2
    xf = x.astype(jnp.float32)
    x1, x2 = xf[..., :half], xf[..., half:]
    return jnp.concatenate([x1 * cos - x2 * sin, x1 * sin + x2 * cos], axis=-1).astype(x.dtype)

def mla_attend(q_nope, q_rope, k_nope, k_rope, v):
    B, T, H, _ = q_nope.shape
    nb = T // Q_BLOCK
    scale = 1.0 / math.sqrt(QK_NOPE + QK_ROPE)
    k_chunk = jnp.arange(T) // CHUNK

    def blocks(t):
        return jnp.moveaxis(t.reshape((B, nb, Q_BLOCK) + t.shape[2:]), 1, 0)

    def one_block(args):
        qn, qr, bi = args
        s = jnp.einsum('bqhd,bkhd->bhqk', qn, k_nope) + jnp.einsum('bqhr,bkr->bhqk', qr, k_rope)
        s = s.astype(jnp.float32) * scale
        q_chunk = (bi * Q_BLOCK + jnp.arange(Q_BLOCK)) // CHUNK
        mask = k_chunk[None, :] <= q_chunk[:, None]
        s = jnp.where(mask[None, None], s, NEG_INF)
        p = jax.nn.softmax(s, axis=-1)
        return jnp.einsum('bhqk,bkhd->bqhd', p.astype(v.dtype), v)

    out = lax.map(one_block, (blocks(q_nope), blocks(q_rope), jnp.arange(nb)))
    return jnp.moveaxis(out, 0, 1).reshape(B, T, H, V_HEAD)

def first_inputs(seed: int = 0) -> dict:
    key = jax.random.key(seed)
    ks = jax.random.split(key, 32)
    D, F, H, N = D_MODEL, D_FF, RWKV_HEADS, RWKV_HEAD
    nA, nB = N_A_LAYERS, N_B_LAYERS
    nrm = lambda k, shape, s: jax.random.normal(k, shape, jnp.float32) * s
    return {
        'x': nrm(ks[0], (BATCH, SEQ, D), 1.0),
        'norm_g': 1.0 + nrm(ks[1], (DEPTH, 4, D), 0.05),
        'ffn_w_in': nrm(ks[2], (DEPTH, D, 2 * F), D ** -0.5),
        'ffn_conv_w': nrm(ks[3], (DEPTH, CONV_W, F), CONV_W ** -0.5),
        'ffn_conv_b': nrm(ks[4], (DEPTH, F), 0.01),
        'ffn_w_out': nrm(ks[5], (DEPTH, F, D), F ** -0.5),
        'a_mu': jax.random.uniform(ks[6], (nA, 6, D), jnp.float32),
        'a_w_rkv': nrm(ks[7], (nA, 3, D, D), D ** -0.5),
        'a_w0': jax.random.uniform(ks[8], (nA, D), jnp.float32, minval=-6.5, maxval=-1.5),
        'a_w1': nrm(ks[9], (nA, D, DECAY_LORA), 0.1 * D ** -0.5),
        'a_w2': nrm(ks[10], (nA, DECAY_LORA, D), DECAY_LORA ** -0.5),
        'a_a0': nrm(ks[11], (nA, D), 0.1),
        'a_a1': nrm(ks[12], (nA, D, ICLR_LORA), 0.1 * D ** -0.5),
        'a_a2': nrm(ks[13], (nA, ICLR_LORA, D), ICLR_LORA ** -0.5),
        'a_g1': nrm(ks[14], (nA, D, GATE_LORA), D ** -0.5),
        'a_g2': nrm(ks[15], (nA, GATE_LORA, D), GATE_LORA ** -0.5),
        'a_k_k': 0.85 + nrm(ks[16], (nA, D), 0.05),
        'a_k_a': 1.0 + nrm(ks[17], (nA, D), 0.05),
        'a_r_k': nrm(ks[18], (nA, H, N), 0.1),
        'a_lnx_w': 1.0 + nrm(ks[19], (nA, D), 0.05),
        'a_lnx_b': nrm(ks[20], (nA, D), 0.01),
        'a_w_o': nrm(ks[21], (nA, D, D), D ** -0.5),
        'kv_norm_g': 1.0 + nrm(ks[22], (D,), 0.05),
        'kv_w_down': nrm(ks[23], (D, KV_LORA + QK_ROPE), D ** -0.5),
        'kv_a_norm_g': 1.0 + nrm(ks[24], (KV_LORA,), 0.05),
        'kv_w_up': nrm(ks[25], (KV_LORA, MLA_HEADS * (QK_NOPE + V_HEAD)), KV_LORA ** -0.5),
        'q_w_down': nrm(ks[26], (nB, D, Q_LORA), D ** -0.5),
        'q_norm_g': 1.0 + nrm(ks[27], (nB, Q_LORA), 0.05),
        'q_w_up': nrm(ks[28], (nB, Q_LORA, MLA_HEADS * (QK_NOPE + QK_ROPE)), Q_LORA ** -0.5),
        'o_w': nrm(ks[29], (nB, MLA_HEADS * V_HEAD, D), (MLA_HEADS * V_HEAD) ** -0.5),
    }

def first_block(x, norm_g, ffn_w_in, ffn_conv_w, ffn_conv_b, ffn_w_out,
              a_mu, a_w_rkv, a_w0, a_w1, a_w2, a_a0, a_a1, a_a2, a_g1, a_g2,
              a_k_k, a_k_a, a_r_k, a_lnx_w, a_lnx_b, a_w_o,
              kv_norm_g, kv_w_down, kv_a_norm_g, kv_w_up,
              q_w_down, q_norm_g, q_w_up, o_w):
    B, T, _ = x.shape
    cos, sin = rope_tables(T)
    k_nope = k_rope = v_sh = None
    for layer in range(DEPTH):
        h = rmsnorm(x, norm_g[layer, 0])
        if layer < N_A_LAYERS:
            i = layer
            m = rwkv7_time_mix(h, a_mu[i], a_w_rkv[i], a_w0[i], a_w1[i], a_w2[i],
                               a_a0[i], a_a1[i], a_a2[i], a_g1[i], a_g2[i],
                               a_k_k[i], a_k_a[i], a_r_k[i], a_lnx_w[i], a_lnx_b[i], a_w_o[i])
        else:
            if layer == N_A_LAYERS:
                down = rmsnorm(x, kv_norm_g) @ kv_w_down
                c_kv = rmsnorm(down[..., :KV_LORA], kv_a_norm_g)
                k_rope = apply_rope(down[..., KV_LORA:], cos, sin)
                up = (c_kv @ kv_w_up).reshape(B, T, MLA_HEADS, QK_NOPE + V_HEAD)
                k_nope, v_sh = up[..., :QK_NOPE], up[..., QK_NOPE:]
            j = layer - N_A_LAYERS
            c_q = rmsnorm(h @ q_w_down[j], q_norm_g[j])
            q = (c_q @ q_w_up[j]).reshape(B, T, MLA_HEADS, QK_NOPE + QK_ROPE)
            q_nope = q[..., :QK_NOPE]
            q_rope = apply_rope(q[..., QK_NOPE:], cos[:, None, :], sin[:, None, :])
            o = mla_attend(q_nope, q_rope, k_nope, k_rope, v_sh)
            m = o.reshape(B, T, MLA_HEADS * V_HEAD) @ o_w[j]
        x = x + rmsnorm(m, norm_g[layer, 1])
        f = conv_ffn(rmsnorm(x, norm_g[layer, 2]), ffn_w_in[layer], ffn_conv_w[layer],
                     ffn_conv_b[layer], ffn_w_out[layer])
        x = x + rmsnorm(f, norm_g[layer, 3])
    return x


DEPTH_2 = 1

GRID_W = 64
HEAD_DIM = 64
N_Q_HEADS = 8
N_KV_HEADS = 2
Q_PER_KV = N_Q_HEADS // N_KV_HEADS
ATTN_WIDTH = N_Q_HEADS * HEAD_DIM
KV_WIDTH = N_KV_HEADS * HEAD_DIM
AXIAL_DIM = HEAD_DIM // 2
SSD_D_INNER = D_MODEL
SSD_HEADDIM = 64
SSD_HEADS = SSD_D_INNER // SSD_HEADDIM
SSD_GROUPS = 2
SSD_HEADS_PER_GROUP = SSD_HEADS // SSD_GROUPS
SSD_STATE = 128
CONV_K = 5
CHUNK_2 = 128
CONV_CH = SSD_D_INNER + 2 * SSD_GROUPS * SSD_STATE
N_BRANCH = 2
D_FF_2 = ((8 * D_MODEL // 3 + 255) // 256) * 256
EPS = 1e-6
IN_SPLITS = (ATTN_WIDTH, KV_WIDTH, KV_WIDTH, SSD_D_INNER, CONV_CH, 2 * SSD_HEADS, N_BRANCH * D_MODEL)
D_IN_PROJ = sum(IN_SPLITS)


def rms_norm(x, g):
    xf = x.astype(jnp.float32)
    xf = xf * lax.rsqrt(jnp.mean(xf * xf, axis=-1, keepdims=True) + EPS)
    return (xf * g.astype(jnp.float32)).astype(x.dtype)

def split_cols(h, sizes):
    idx = np.cumsum(np.array(sizes[:-1]))
    return jnp.split(h, [int(i) for i in idx], axis=-1)

def axial_angles(seq_len):
    rows = seq_len // GRID_W
    row_idx = jnp.repeat(jnp.arange(rows, dtype=jnp.float32), GRID_W)
    col_idx = jnp.tile(jnp.arange(GRID_W, dtype=jnp.float32), rows)
    inv_freq = ROPE_THETA ** (-jnp.arange(0, AXIAL_DIM, 2, dtype=jnp.float32) / AXIAL_DIM)
    ang_row = row_idx[:, None] * inv_freq[None, :]
    ang_col = col_idx[:, None] * inv_freq[None, :]
    return ang_row, ang_col

def rotate(xh, ang):
    half = xh.shape[-1] // 2
    x1, x2 = xh[..., :half], xh[..., half:]
    cos, sin = jnp.cos(ang).astype(xh.dtype), jnp.sin(ang).astype(xh.dtype)
    return jnp.concatenate([x1 * cos - x2 * sin, x2 * cos + x1 * sin], axis=-1)

def axial_rope(x, ang_row, ang_col):
    shp = (1, x.shape[1]) + (1,) * (x.ndim - 3) + (AXIAL_DIM // 2,)
    xr = rotate(x[..., :AXIAL_DIM], ang_row.reshape(shp))
    xc = rotate(x[..., AXIAL_DIM:], ang_col.reshape(shp))
    return jnp.concatenate([xr, xc], axis=-1)

def gqa_attention(q, k, v):
    b, s = q.shape[0], q.shape[1]
    nblk = s // Q_BLOCK
    scale = 1.0 / math.sqrt(HEAD_DIM)
    qb = jnp.moveaxis(q.reshape(b, nblk, Q_BLOCK, N_KV_HEADS, Q_PER_KV, HEAD_DIM), 1, 0)

    def block(q_blk):
        sc = jnp.einsum("bqkgd,bskd->bkgqs", q_blk, k).astype(jnp.float32) * scale
        p = jax.nn.softmax(sc, axis=-1).astype(v.dtype)
        return jnp.einsum("bkgqs,bskd->bqkgd", p, v)

    out = lax.map(block, qb)
    return jnp.moveaxis(out, 0, 1).reshape(b, s, ATTN_WIDTH)

def ssd_chunked(xs, dt, a, bm, cm):
    b, l, g, r, p = xs.shape
    n = bm.shape[-1]
    c = l // CHUNK_2
    xd = (xs * dt[..., None]).reshape(b, c, CHUNK_2, g, r, p)
    adt = jnp.moveaxis((dt * a).reshape(b, c, CHUNK_2, g, r), 2, -1)
    bc = bm.reshape(b, c, CHUNK_2, g, n)
    cc = cm.reshape(b, c, CHUNK_2, g, n)
    a_cs = jnp.cumsum(adt, axis=-1)
    tri = jnp.tril(jnp.ones((CHUNK_2, CHUNK_2), dtype=bool))
    seg = a_cs[..., :, None] - a_cs[..., None, :]
    decay_in = jnp.exp(jnp.where(tri, seg, -jnp.inf))
    cb = jnp.einsum("bclgn,bcsgn->bcgls", cc, bc)
    y_diag = jnp.einsum("bcgls,bcgrls,bcsgrp->bclgrp", cb, decay_in, xd)
    decay_states = jnp.exp(a_cs[..., -1:] - a_cs)
    states = jnp.einsum("bclgn,bcgrl,bclgrp->bcgrpn", bc, decay_states, xd)
    chunk_decay = jnp.exp(a_cs[..., -1])

    def step(h, inp):
        st, dec = inp
        return h * dec[..., None, None] + st, h

    h0 = jnp.zeros((b, g, r, p, n), dtype=xs.dtype)
    _, prev = lax.scan(step, h0, (jnp.moveaxis(states, 1, 0), jnp.moveaxis(chunk_decay, 1, 0)))
    prev = jnp.moveaxis(prev, 0, 1)
    y_off = jnp.einsum("bclgn,bcgrpn,bcgrl->bclgrp", cc, prev, jnp.exp(a_cs))
    return (y_diag + y_off).reshape(b, l, g, r, p)

def centred_depthwise_conv(u, w, bias):
    pad = (CONV_K - 1) // 2
    out = lax.conv_general_dilated(
        u, w[:, None, :].astype(u.dtype), window_strides=(1,), padding=[(pad, pad)],
        dimension_numbers=("NWC", "WIO", "NWC"), feature_group_count=u.shape[-1])
    return out + bias

def ssd_branch(z, xbc, dt_raw, conv_w, conv_b, dt_bias_f, dt_bias_b, a_log_f, a_log_b, d_skip, ssd_norm):
    b, l, _ = z.shape
    xbc = jax.nn.silu(centred_depthwise_conv(xbc, conv_w, conv_b))
    xs, bm, cm = split_cols(xbc, (SSD_D_INNER, SSD_GROUPS * SSD_STATE, SSD_GROUPS * SSD_STATE))
    f32 = jnp.float32
    xs = xs.astype(f32).reshape(b, l, SSD_GROUPS, SSD_HEADS_PER_GROUP, SSD_HEADDIM)
    bm = bm.astype(f32).reshape(b, l, SSD_GROUPS, SSD_STATE)
    cm = cm.astype(f32).reshape(b, l, SSD_GROUPS, SSD_STATE)
    dt_raw = dt_raw.astype(f32)
    shp = (SSD_GROUPS, SSD_HEADS_PER_GROUP)
    dt_f = jax.nn.softplus(dt_raw[..., :SSD_HEADS] + dt_bias_f.astype(f32)).reshape(b, l, *shp)
    dt_b = jax.nn.softplus(dt_raw[..., SSD_HEADS:] + dt_bias_b.astype(f32)).reshape(b, l, *shp)
    a_f = -jnp.exp(a_log_f.astype(f32)).reshape(shp)
    a_b = -jnp.exp(a_log_b.astype(f32)).reshape(shp)
    y_fwd = ssd_chunked(xs, dt_f, a_f, bm, cm)
    flip = lambda t: jnp.flip(t, axis=1)
    y_bwd = flip(ssd_chunked(flip(xs), flip(dt_b), a_b, flip(bm), flip(cm)))
    y = y_fwd + y_bwd + d_skip.astype(f32).reshape(shp)[..., None] * xs
    y = y.reshape(b, l, SSD_D_INNER).astype(z.dtype)
    return rms_norm(y * jax.nn.silu(z), ssd_norm)

def second_inputs(seed: int = 0) -> dict:
    key = jax.random.key(seed)
    ks = jax.random.split(key, 24)
    L = DEPTH_2
    nrm = lambda k, shape, fan_in: jax.random.normal(k, shape, jnp.float32) * fan_in ** -0.5
    gain = lambda k, shape: 1.0 + 0.05 * jax.random.normal(k, shape, jnp.float32)
    dt0 = jnp.exp(jax.random.uniform(ks[6], (2, L, SSD_HEADS), jnp.float32, math.log(1e-3), math.log(1e-1)))
    dt_bias = dt0 + jnp.log(-jnp.expm1(-dt0))
    a_log = jnp.log(jax.random.uniform(ks[7], (2, L, SSD_HEADS), jnp.float32, 1.0, 16.0))
    return {
        "x": jax.random.normal(ks[0], (BATCH, SEQ, D_MODEL), jnp.float32),
        "w_in": nrm(ks[1], (L, D_MODEL, D_IN_PROJ), D_MODEL),
        "q_norm": gain(ks[2], (L, HEAD_DIM)),
        "k_norm": gain(ks[3], (L, HEAD_DIM)),
        "conv_w": nrm(ks[4], (L, CONV_K, CONV_CH), CONV_K),
        "conv_b": 0.02 * jax.random.normal(ks[5], (L, CONV_CH), jnp.float32),
        "dt_bias_f": dt_bias[0],
        "dt_bias_b": dt_bias[1],
        "a_log_f": a_log[0],
        "a_log_b": a_log[1],
        "d_skip": 1.0 + 0.1 * jax.random.normal(ks[8], (L, SSD_HEADS), jnp.float32),
        "ssd_norm": gain(ks[9], (L, SSD_D_INNER)),
        "w_attn_proj": nrm(ks[10], (L, ATTN_WIDTH, D_MODEL), ATTN_WIDTH),
        "w_ssd_proj": nrm(ks[11], (L, SSD_D_INNER, D_MODEL), SSD_D_INNER),
        "w_out": nrm(ks[12], (L, D_MODEL, D_MODEL), D_MODEL),
        "norm1_pre": gain(ks[13], (L, D_MODEL)),
        "norm1_post": gain(ks[14], (L, D_MODEL)),
        "norm2_pre": gain(ks[15], (L, D_MODEL)),
        "norm2_post": gain(ks[16], (L, D_MODEL)),
        "w_gate_up": nrm(ks[17], (L, D_MODEL, 2 * D_FF_2), D_MODEL),
        "w_down": nrm(ks[18], (L, D_FF_2, D_MODEL), D_FF_2),
    }

def second_block(x, w_in, q_norm, k_norm, conv_w, conv_b, dt_bias_f, dt_bias_b, a_log_f, a_log_b,
              d_skip, ssd_norm, w_attn_proj, w_ssd_proj, w_out, norm1_pre, norm1_post,
              norm2_pre, norm2_post, w_gate_up, w_down):
    b, s, _ = x.shape
    ang_row, ang_col = axial_angles(s)
    for i in range(DEPTH_2):
        h = rms_norm(x, norm1_pre[i])
        proj = h @ w_in[i]
        q, k, v, z, xbc, dt_raw, gates = split_cols(proj, IN_SPLITS)
        q = rms_norm(q.reshape(b, s, N_KV_HEADS, Q_PER_KV, HEAD_DIM), q_norm[i])
        k = rms_norm(k.reshape(b, s, N_KV_HEADS, HEAD_DIM), k_norm[i])
        v = v.reshape(b, s, N_KV_HEADS, HEAD_DIM)
        q = axial_rope(q, ang_row, ang_col)
        k = axial_rope(k, ang_row, ang_col)
        attn_out = gqa_attention(q, k, v) @ w_attn_proj[i]
        ssd_y = ssd_branch(z, xbc, dt_raw, conv_w[i], conv_b[i], dt_bias_f[i], dt_bias_b[i],
                           a_log_f[i], a_log_b[i], d_skip[i], ssd_norm[i])
        ssd_out = ssd_y @ w_ssd_proj[i]
        g_attn, g_ssd = jnp.split(jax.nn.sigmoid(gates), N_BRANCH, axis=-1)
        mixed = (g_attn * attn_out + g_ssd * ssd_out) @ w_out[i]
        x = x + rms_norm(mixed, norm1_post[i])
        h2 = rms_norm(x, norm2_pre[i])
        gate, up = jnp.split(h2 @ w_gate_up[i], 2, axis=-1)
        ffn = (jax.nn.silu(gate) * up) @ w_down[i]
        x = x + rms_norm(ffn, norm2_post[i])
    return x


def setup_inputs(seed=0):
    out = dict(first_inputs(seed))
    for name, value in second_inputs(seed + 1).items():
        if name != "x":
            out[name + "_2"] = value
    return out


def reference(
    x, norm_g, ffn_w_in, ffn_conv_w, ffn_conv_b, ffn_w_out, a_mu, a_w_rkv, a_w0, a_w1, a_w2,
    a_a0, a_a1, a_a2, a_g1, a_g2, a_k_k, a_k_a, a_r_k, a_lnx_w, a_lnx_b, a_w_o, kv_norm_g,
    kv_w_down, kv_a_norm_g, kv_w_up, q_w_down, q_norm_g, q_w_up, o_w, w_in_2, q_norm_2,
    k_norm_2, conv_w_2, conv_b_2, dt_bias_f_2, dt_bias_b_2, a_log_f_2, a_log_b_2, d_skip_2,
    ssd_norm_2, w_attn_proj_2, w_ssd_proj_2, w_out_2, norm1_pre_2, norm1_post_2, norm2_pre_2,
    norm2_post_2, w_gate_up_2, w_down_2,
):
    x = first_block(
        x, norm_g, ffn_w_in, ffn_conv_w, ffn_conv_b, ffn_w_out, a_mu, a_w_rkv, a_w0, a_w1, a_w2,
        a_a0, a_a1, a_a2, a_g1, a_g2, a_k_k, a_k_a, a_r_k, a_lnx_w, a_lnx_b, a_w_o, kv_norm_g,
        kv_w_down, kv_a_norm_g, kv_w_up, q_w_down, q_norm_g, q_w_up, o_w,
    )
    return second_block(
        x, w_in_2, q_norm_2, k_norm_2, conv_w_2, conv_b_2, dt_bias_f_2, dt_bias_b_2, a_log_f_2,
        a_log_b_2, d_skip_2, ssd_norm_2, w_attn_proj_2, w_ssd_proj_2, w_out_2, norm1_pre_2,
        norm1_post_2, norm2_pre_2, norm2_post_2, w_gate_up_2, w_down_2,
    )


_drawn_inputs = setup_inputs


def setup_inputs(seed=0):
    import zlib

    import numpy as np

    out = dict(_drawn_inputs(seed))
    spreads = {}
    factors = {'ffn_conv_b': 5.386,
     'a_w1': 7.915,
     'a_w2': 8.0,
     'q_norm_2': 8.0,
     'k_norm_2': 8.0,
     'conv_b_2': 4.352,
     'd_skip_2': 2.769,
     'norm2_post_2': 2.875,
     'ssd_norm_2': 2.872}
    for name, (base, spread) in spreads.items():
        noise = np.random.default_rng([zlib.crc32(name.encode()), seed]).standard_normal(out[name].shape)
        drawn = base * np.exp(spread * noise) if base else spread * noise
        out[name] = __import__('jax').numpy.asarray(drawn.astype(out[name].dtype))
    for name, factor in factors.items():
        out[name] = (out[name] * factor).astype(out[name].dtype)
    return out
```

```python
from contextlib import ExitStack

import numpy as np

import concourse.bass as bass
from concourse import mybir

F32 = mybir.dt.float32
ALU = mybir.AluOpType
ACT = mybir.ActivationFunctionType
AX = mybir.AxisListType.X

P = 128
T = 256
NT = T // P
D = 1024
DC = D // P
HALF = 512
F = 2816
FC = F // P
H = 16
N = 64
HP = H // 2
NOPE, ROPE = 64, 32
QK = NOPE + ROPE
Q_LORA, KV_LORA = 384, 256
GATE_LORA = 160
GH, GKV, GJ = 8, 2, 4
XC = 12
EPS = 1e-6
LNX_EPS = 64e-5
KAPPA = float(np.exp(-0.5))
BS = 32
NB = P // BS
MLA_SCALE = float(QK) ** -0.5
GQA_SCALE = float(N) ** -0.5
NEG = -1e30

RING = 4
SLOT = 2048

PLAN = [("lora_wa", 1, 2), ("w_k", 4, 1), ("lora_wa2", 1, 2), ("lora_g", 1, 1), ("w_r", 4, 1), ("lora_g2", 1, 2),
        ("w_v", 4, 1), ("w_o", 4, 1), ("ffn_in0", FC, 2), ("ffn_out0", FC // 2, 1),
        ("kv_down", 2, 1), ("q_down", 2, 1), ("kv_up", 2, 1), ("q_up", 4, 1), ("o_w", 4, 1),
        ("ffn_in1", FC, 2), ("ffn_out1", FC // 2, 1),
        ("kvdt", 2, 2), ("xbc", 6, 1), ("q", 2, 1), ("z", 4, 1), ("gates", 8, 1),
        ("attn_proj", 2, 2), ("ssd_proj", 4, 1), ("w_out", 4, 1), ("ffn_in2", FC, 2), ("ffn_out2", FC // 2, 1)]
FIRST = {}
LANDED = []
_count = [0] * RING
for _name, _n, _dmas in PLAN:
    FIRST[_name] = len(LANDED)
    for _ in range(_n):
        _r = len(LANDED) % RING
        _count[_r] += 16 * _dmas
        LANDED.append(_count[_r])

ROW_TILES = [[("norm_g", 64), ("a_mu", 48), ("a_w0", 8), ("a_a0", 8)],
             [("a_k_k", 8), ("a_k_a", 8), ("a_r_k", 8), ("kv_norm_g", 8), ("kv_a_norm_g", 2), ("q_norm_g", 3),
              ("norm1_pre_2", 8), ("norm2_pre_2", 8), ("ssd_norm_2", 8), ("conv_w_2", 60)],
             [("conv_b_2", 12), ("ffn_conv_w0", 66), ("ffn_conv_b", 44)],
             [("ffn_conv_w1", 66)]]
COL = {}
for _q, _tile in enumerate(ROW_TILES):
    _at = 0
    for _name, _n in _tile:
        COL[_name] = _q * P + _at
        _at += _n
PARAM_DMAS = sum(len(t) for t in ROW_TILES)


def constants():
    s, t = np.arange(P)[:, None], np.arange(P)[None, :]
    tok = np.arange(T, dtype=np.float32)
    inv = (1.0 / (10000.0 ** (np.arange(0, ROPE, 2, dtype=np.float32) / ROPE))).astype(np.float32)
    ang = tok[:, None] * inv[None, :]
    c, sn = np.cos(ang), np.sin(ang)
    perm = np.zeros((P, QK))
    cosT, sinT = np.zeros((P, T)), np.zeros((P, T))
    half = ROPE // 2
    for i in range(half):
        perm[NOPE + half + i, NOPE + i] = 1
        perm[NOPE + i, NOPE + half + i] = 1
        cosT[NOPE + i] = cosT[NOPE + half + i] = c[:, i]
        sinT[NOPE + i], sinT[NOPE + half + i] = -sn[:, i], sn[:, i]
    ktok = lambda a: a.reshape(NT, P, half).transpose(1, 0, 2).reshape(P, -1)
    maskb = np.where((t // 64) <= (s // 64), 0.0, NEG)
    inv2 = (10000.0 ** (-np.arange(0, 32, 2, dtype=np.float32) / 32)).astype(np.float32)
    a2 = np.stack([(tok // 64)[:, None] * inv2, (tok % 64)[:, None] * inv2], 1)
    axial = lambda a: a.reshape(NT, P, 32).transpose(1, 0, 2).reshape(P, -1)
    return {
        "ident": s == t, "before": s < t, "upto": s <= t, "after": s > t, "from": s >= t,
        "off": (s < t) & (s // BS != t // BS), "same_head": s // N == t // N, "ones": np.ones((P, P)),
        "head_of": s // N == np.arange(2)[None, :], "perm": perm, "cosT": cosT, "sinT": sinT,
        "kcos": ktok(c), "ksin": ktok(sn), "maskb": np.concatenate([maskb, maskb, 0 * maskb], 1),
        "acos": axial(np.cos(a2)), "asin": axial(np.sin(a2)),
    }


CONSTANTS = {k: np.asarray(v, np.float32) for k, v in constants().items()}
CONST_AT, _at = {}, 0
for _k, _v in CONSTANTS.items():
    CONST_AT[_k] = _at
    _at += _v.shape[1]
CONST_W = _at


def build(nc, A, const_dram, out):
    with ExitStack() as ctx:
        def sb(name, shape):
            return ctx.enter_context(nc.sbuf_tensor(name, shape, F32))

        def sem(name):
            return ctx.enter_context(nc.semaphore(name))

        ring = sb("ring", [P, RING, SLOT])
        arena = sb("arena", [P, 18, SLOT])
        x_sb = sb("x_sb", [P, NT, D])
        cst = sb("cst", [P, CONST_W])
        cols = sb("cols", [P, 4 * P])
        gpost = sb("gpost", [P, 2, D])
        stat = sb("stat", [P, 640])
        bank = [ctx.enter_context(nc.psum_tensor(f"bank{i}", [P, HALF], F32)) for i in range(8)]

        stat_used = [0]

        def small(n):
            stat_used[0] += n
            assert stat_used[0] <= 640
            return stat[:, stat_used[0] - n:stat_used[0]]

        def const(name, lo=0, hi=None):
            w = CONSTANTS[name].shape[1]
            return cst[:, CONST_AT[name] + lo:CONST_AT[name] + (w if hi is None else hi)]

        def col(name, i):
            return cols[:, COL[name] + i:COL[name] + i + 1]

        def buf(i, lo=0, hi=SLOT):
            return arena[:, i, lo:hi]

        def chan(i):
            return arena[:, i, :].rearrange("p (c t) -> p c t", t=T)

        def toks(i):
            return arena[:, i, :].rearrange("p (a d) -> p a d", a=NT)

        def heads(i):
            return arena[:, i, :].rearrange("p (h t) -> p h t", t=P)

        def spread(ap, shape):
            return ap.broadcast_to(shape)

        ident = const("ident")
        ss2, var2, rstd2 = small(2), small(2), small(2)
        ss4, po_ss, po_var, po_rstd = small(4), small(2), small(2), small(2)
        minus_half = small(32)

        landed = [sem(f"landed{r}") for r in range(RING)]
        slot_done = sem("slot_done")
        x_landed, const_landed, rows_zeroed, rows_landed = (
            sem(n) for n in ("x_landed", "const_landed", "rows_zeroed", "rows_landed"))
        cols_turned, cols_ready, consts_set = sem("cols_turned"), sem("cols_ready"), sem("consts_set")
        gpost_landed = [sem("gpost_landed0"), sem("gpost_landed1")]
        x_updated, out_stored = sem("x_updated"), sem("out_stored")
        dve_step = sem("dve_step")
        pre_ss, pre_var, pre_rstd, pre_xn_a, pre_xn_v = (
            sem(n) for n in ("pre_ss", "pre_var", "pre_rstd", "pre_xn_a", "pre_xn_v"))
        turned, turn_a, turn_v = sem("turned"), sem("turn_a"), sem("turn_v")
        post_ss, post_var, post_rstd = sem("post_ss"), sem("post_var"), sem("post_rstd")
        conv_step, act_done, ffn_done = sem("conv_step"), sem("ffn_act_done"), sem("ffn_done")

        (TURN_PRE0, TURN_RWKV, TURN_PRE1, TURN_PRE2, TURN_PRE3, TURN_PRE4, TURN_SSD, TURN_MIX, TURN_PRE5) = range(9)
        PRE_TURN = [TURN_PRE0, TURN_PRE1, TURN_PRE2, TURN_PRE3, TURN_PRE4, TURN_PRE5]
        XN, SQ, TMP = 17, 16, 15

        def after_slots(eng, name, n=None):
            count = {k: c for k, c, _ in PLAN}[name]
            eng.wait_ge(slot_done, FIRST[name] + (count if n is None else n))

        def weights(pe, n):
            pe.wait_ge(landed[n % RING], LANDED[n])
            return ring[:, n % RING, :]

        def wide(pe, name, nslots, stationary, base):
            for s in range(nslots):
                w = weights(pe, FIRST[name] + s)
                for kk in range(2):
                    k = 2 * s + kk
                    for a in range(NT):
                        for half in range(2):
                            mm = nc.tensor.matmul(bank[base + 2 * a + half][:, :], stationary(k, a),
                                                  w[:, kk * D + half * HALF:kk * D + (half + 1) * HALF],
                                                  start=(k == 0), stop=(k == 2 * nslots - 1))
                mm.then_inc(slot_done, 1)

        def turn_pe(src, base):
            for j in range(4):
                for c in (2 * j, 2 * j + 1):
                    for a in range(NT):
                        at = (c % 2) * T + a * P
                        mm = nc.tensor.transpose(bank[base + j][:, at:at + P], src[:, a, c * P:(c + 1) * P], ident)
                mm.then_inc(turned, 1)

        def pre_norm_pe(pe, i):
            pe.wait_ge(pre_xn_a, i + 1)
            pe.wait_ge(pre_xn_v, i + 1)
            turn_pe(toks(XN), 4)

        def turned_in(eng, n):
            eng.wait_ge(turn_a, 2 * (n + 1))
            eng.wait_ge(turn_v, 2 * (n + 1))

        def turn_act(act, n, base, dsts):
            for j in (0, 2):
                act.wait_ge(turned, 4 * n + j + 1)
                for gain, dst in dsts:
                    for c in (2 * j, 2 * j + 1):
                        src = bank[base + j][:, (c % 2) * T:(c % 2 + 1) * T]
                        if gain is None:
                            op = nc.scalar.activation(chan(dst)[:, c, :], src, ACT.Copy)
                        else:
                            op = nc.scalar.activation(chan(dst)[:, c, :], src, ACT.Copy, scale=col(gain[0], gain[1] + c))
                op.then_inc(turn_a, 1)

        def x_wait(eng, i, a):
            if i == 0:
                eng.wait_ge(x_landed, 16 * NT)
            else:
                eng.wait_ge(x_updated, NT * (i - 1) + a + 1)

        def pre_norm_act(act, i, dsts):
            for a in range(NT):
                x_wait(act, i, a)
                nc.scalar.activation(buf(SQ, a * D, (a + 1) * D), x_sb[:, a, :], ACT.Square,
                                     accum_out=ss2[:, a:a + 1]).then_inc(pre_ss, 1)
            act.wait_ge(pre_rstd, i + 1)
            nc.scalar.activation(buf(XN, 0, D), x_sb[:, 0, :], ACT.Copy, scale=rstd2[:, 0:1]).then_inc(pre_xn_a, 1)
            turn_act(act, PRE_TURN[i], 4, dsts)

        def post_norm_act(act, i, ready):
            ready(act)
            for a in range(NT):
                for half in range(2):
                    n = 2 * a + half
                    nc.scalar.activation(buf(SQ, n * HALF, (n + 1) * HALF), bank[4 + n][:, :], ACT.Square,
                                         accum_out=ss4[:, n:n + 1]).then_inc(post_ss, 1)

        steps = [0]

        def step(ins):
            steps[0] += 1
            ins.then_inc(dve_step, 1)
            return steps[0]

        def link(dve, ins):
            dve.wait_ge(dve_step, step(ins))

        def turn_dve(dve, n, base, dsts):
            for j in (1, 3):
                dve.wait_ge(turned, 4 * n + j + 1)
                for gain, dst in dsts:
                    for c in (2 * j, 2 * j + 1):
                        src = bank[base + j][:, (c % 2) * T:(c % 2 + 1) * T]
                        if gain is None:
                            op = nc.vector.tensor_copy(chan(dst)[:, c, :], src)
                        else:
                            op = nc.vector.tensor_scalar(chan(dst)[:, c, :], src, col(gain[0], gain[1] + c), None, ALU.mult)
                op.then_inc(turn_v, 1)

        def pre_norm_dve(dve, i, dsts):
            dve.wait_ge(pre_ss, NT * (i + 1))
            nc.vector.tensor_scalar(var2, ss2, 1.0 / D, EPS, ALU.mult, ALU.add).then_inc(pre_var, 1)
            dve.wait_ge(pre_rstd, i + 1)
            nc.vector.tensor_scalar(buf(XN, D, 2 * D), x_sb[:, 1, :], rstd2[:, 1:2], None, ALU.mult).then_inc(pre_xn_v, 1)
            turn_dve(dve, PRE_TURN[i], 4, dsts)

        def post_norm_dve(dve, i):
            dve.wait_ge(post_ss, 4 * (i + 1))
            link(dve, nc.vector.tensor_tensor(po_ss, ss4[:, 0:4:2], ss4[:, 1:4:2], ALU.add))
            nc.vector.tensor_scalar(po_var, po_ss, 1.0 / D, EPS, ALU.mult, ALU.add).then_inc(post_var, 1)
            dve.wait_ge(gpost_landed[i % 2], 16 * (i // 2 + 1))
            dve.wait_ge(post_rstd, i + 1)
            scaled = []
            for a in range(NT):
                for half in range(2):
                    n = 2 * a + half
                    scaled.append(step(nc.vector.scalar_tensor_tensor(
                        buf(TMP, n * HALF, (n + 1) * HALF), bank[4 + n][:, :], po_rstd[:, a:a + 1],
                        gpost[:, i % 2, half * HALF:(half + 1) * HALF], ALU.mult, ALU.mult)))
            for a in range(NT):
                dve.wait_ge(dve_step, scaled[2 * a + 1])
                nc.vector.tensor_tensor(x_sb[:, a, :], x_sb[:, a, :], buf(TMP, a * D, (a + 1) * D),
                                        ALU.add).then_inc(x_updated, 1)

        def pre_norm_pool(pool, i):
            pool.wait_ge(pre_var, i + 1)
            nc.gpsimd.tensor_tensor(rstd2, var2, minus_half[:, 0:2], ALU.pow).then_inc(pre_rstd, 1)

        def post_norm_pool(pool, i):
            pool.wait_ge(post_var, i + 1)
            nc.gpsimd.tensor_tensor(po_rstd, po_var, minus_half[:, 0:2], ALU.pow).then_inc(post_rstd, 1)

        def load_gain(pool, i, row):
            if i >= 2:
                pool.wait_ge(x_updated, NT * (i - 1))
            pool.dma_start(gpost[:, i % 2, :], row.partition_broadcast(P)).then_inc(gpost_landed[i % 2], 16)

        FFN_H, FFN_F = 0, 1
        fT = arena[:, FFN_F:FFN_F + 3, :].rearrange("p b s -> p (b s)")
        conv_acc = [buf(4, j * T, (j + 1) * T) for j in range(RING)]
        gate_act = [buf(4, (RING + j) * T, (RING + j + 1) * T) for j in range(RING)]
        LOOPS = FC // RING
        CONV = (2 * FC)

        def rounds(eng, tile):
            for j in range(RING):
                tile(0, j)
            with eng.Fori(1, LOOPS) as it:
                for j in range(RING):
                    tile(it, j)
            for j in range(FC - LOOPS * RING):
                tile(LOOPS, j)

        def ffn_pe(pe, f, turn):
            first = FIRST[f"ffn_in{f}"]
            hT = chan(FFN_H)
            turned_in(pe, turn)

            def tile(it, j):
                r = (first + j) % RING
                pe.wait_ge(landed[r], LANDED[first + j] + it * 32)
                if not (isinstance(it, int) and it == 0):
                    pe.wait_ge(ffn_done, f * FC + it * RING + (j - RING + 1))
                w = ring[:, r, :].rearrange("p (k g n) -> p k g n", k=DC, g=2)
                for g in range(2):
                    for k in range(DC):
                        mm = nc.tensor.matmul(bank[j][:, g * T:(g + 1) * T], w[:, k, g, :], hT[:, k, :],
                                              start=(k == 0), stop=(k == DC - 1))
                mm.then_inc(slot_done, 1)

            rounds(pe, tile)
            for k in range(FC):
                s = FIRST[f"ffn_out{f}"] + k // 2
                if k % 2 == 0:
                    w = weights(pe, s)
                pe.wait_ge(ffn_done, f * FC + k + 1)
                for a in range(NT):
                    for half in range(2):
                        mm = nc.tensor.matmul(bank[4 + 2 * a + half][:, :], fT[:, k * T + a * P:k * T + (a + 1) * P],
                                              w[:, (k % 2) * D + half * HALF:(k % 2) * D + (half + 1) * HALF],
                                              start=(k == 0), stop=(k == FC - 1))
                if k % 2 == 1:
                    mm.then_inc(slot_done, 1)

        def ffn_act(act, f):
            def tile(it, j):
                if f < 2:
                    act.wait_ge(conv_step, 3 * f * FC + it * (3 * RING) + 3 * (j + 1))
                    nc.scalar.activation(gate_act[j], conv_acc[j], ACT.Gelu_apprx_tanh).then_inc(act_done, 1)
                else:
                    act.wait_ge(slot_done, FIRST[f"ffn_in{f}"] + it * RING + (j + 1))
                    nc.scalar.activation(gate_act[j], bank[j][:, 0:T], ACT.Silu).then_inc(act_done, 1)

            rounds(act, tile)

        def ffn_dve(dve, f):
            def at(it, j, name):
                if isinstance(it, int):
                    return col(name[0], name[1] + it * RING + j)
                return cols[:, bass.ds(it * RING + (COL[name[0]] + name[1] + j), 1)]

            def tile(it, j):
                gate, up = bank[j][:, 0:T], bank[j][:, T:2 * T]
                if f < 2:
                    tap = [(f"ffn_conv_w{f}", i * FC) for i in range(3)]
                    dve.wait_ge(slot_done, FIRST[f"ffn_in{f}"] + it * RING + (j + 1))
                    nc.vector.tensor_scalar(conv_acc[j], gate, at(it, j, tap[2]), at(it, j, ("ffn_conv_b", f * FC)),
                                            ALU.mult, ALU.add).then_inc(conv_step, 1)
                    for i in (1, 0):
                        back = 2 - i
                        dve.wait_ge(conv_step, 3 * f * FC + it * (3 * RING) + 3 * j + back)
                        nc.vector.scalar_tensor_tensor(conv_acc[j][:, back:T], gate[:, 0:T - back], at(it, j, tap[i]),
                                                       conv_acc[j][:, back:T], ALU.mult, ALU.add).then_inc(conv_step, 1)
                dve.wait_ge(act_done, f * FC + it * RING + (j + 1))
                dst = (fT[:, (it * RING + j) * T:(it * RING + j + 1) * T] if isinstance(it, int)
                       else fT[:, bass.ds(it * (RING * T) + j * T, T)])
                nc.vector.tensor_tensor(dst, gate_act[j], up, ALU.mult).then_inc(ffn_done, 1)

            rounds(dve, tile)

        def ffn_ready(f):
            return lambda eng: after_slots(eng, f"ffn_out{f}")

        ROWS = 15
        rows = buf(ROWS, 0, 4 * P).rearrange("p (q n) -> p q n", n=P)

        def row_view(name):
            if name[-1] in "01" and name.startswith("ffn_conv_w"):
                return A["ffn_conv_w"][int(name[-1])].rearrange("j (c p) -> (j c) p", p=P)
            a = A[name]
            if name == "a_r_k":
                return a.rearrange("o (c g) n -> (o c) (g n)", g=2)
            if len(a.shape) == 1:
                return a.rearrange("(c p) -> c p", p=P)
            if len(a.shape) == 2:
                return a.rearrange("o (c p) -> (o c) p", p=P)
            return a.rearrange("o j (c p) -> (o j c) p", p=P)

        def start_act(act):
            for a in range(NT):
                act.dma_start(x_sb[:, a, :], A["x"][0, a * P:(a + 1) * P, :]).then_inc(x_landed, 16)
            act.dma_start(cst[:, :], const_dram).then_inc(const_landed, 16)
            act.wait_ge(rows_zeroed, 1)
            for q, tile in enumerate(ROW_TILES):
                for name, n in tile:
                    lo = COL[name] - q * P
                    act.dma_start(rows[lo:lo + n, q, :], row_view(name)).then_inc(rows_landed, 16)

        def start_pool(pool):
            nc.gpsimd.memset(minus_half, -0.5).then_inc(consts_set, 1)
            load_gain(pool, 0, A["norm_g"][0, 1])
            load_gain(pool, 1, A["norm_g"][0, 3])
            pool.wait_ge(consts_set, 1)

        def start_pe(pe):
            pe.wait_ge(const_landed, 16)
            pe.wait_ge(rows_landed, 16 * PARAM_DMAS)
            for q in range(4):
                mm = nc.tensor.transpose(bank[0][:, q * P:(q + 1) * P], rows[:, q, :], ident)
            mm.then_inc(cols_turned, 1)

        def start_dve(dve):
            nc.vector.memset(buf(ROWS, 0, 4 * P), 0.0).then_inc(rows_zeroed, 1)
            dve.wait_ge(cols_turned, 1)
            nc.vector.tensor_copy(cols[:, :], bank[0][:, :]).then_inc(cols_ready, 1)
            dve.wait_ge(const_landed, 16)

        W_HT, W_DX = 0, 1
        W_XS = {"w": 3, "a": 13, "k": 2, "g": 15, "r": 14, "v": 16}
        MIXES = [("w", 3), ("a", 4), ("k", 1), ("g", 5), ("r", 0), ("v", 2)]
        MIXED = {name: i + 1 for i, (name, _) in enumerate(MIXES)}
        W_K, W_SIG, W_CUM, W_A, W_EP, W_EM, W_KK, W_LORA, W_G, W_R = 4, 5, 6, 7, 8, 9, 10, 11, 12, 17
        W_RINV, W_T1, W_V = 0, 1, 11
        W_REMOVE, W_ADD, W_KEY, W_QUERY = W_SIG, W_A, W_EM, W_EP
        W_N, W_Z, W_LK, W_RB, W_RK = (13, 14), (15, 16), (0, 1), (2, 3), (6, 10)
        W_SOLVE = W_TOK = 17
        W_RHS, W_U, W_S0 = 9, 7, 4
        W_LNX, W_YC, W_YSQ, W_BV, W_OT = 13, 0, 1, 2, 3
        nd = buf(W_SOLVE, 0, BS * BS).rearrange("p (s t) -> p s t", t=BS)
        yd = buf(W_SOLVE, BS * BS, 2 * BS * BS).rearrange("p (s t) -> p s t", t=BS)
        n_dram = nc.dram_tensor("n_blocks", (NT, H, NB, BS, BS), F32, kind="Internal").ap()
        y_dram = nc.dram_tensor("y_blocks", (NT, H, NB, BS, BS), F32, kind="Internal").ap()
        mid, last_e, s_scale = small(16), small(8), small(8)
        solve_tmp = small(256)
        bon, y_sum, y_mean, y_sq, y_var, y_rstd = (small(32) for _ in range(6))

        (mix_done, lora_hidden, gate_hidden, k_evac, decay_sig, iclr_sig, r_evac, g_evac, v_evac) = (
            sem(n) for n in ("mix_done", "lora_hidden", "gate_hidden", "k_evac", "decay_sig", "iclr_sig", "r_evac",
                             "g_evac", "v_evac"))
        (kk_ready, kk_squared, kk_normed, kk_root, cum_ready, decay_exp, removal_ready, keys_ready, queries_ready,
         bonus_ready, bonus_summed, bonus_copied, n_mm, n_masked, prod_mm, prod_masked) = (
            sem(n) for n in ("kk_ready", "kk_squared", "kk_normed", "kk_root", "cum_ready", "decay_exp",
                             "removal_ready", "keys_ready", "queries_ready", "bonus_ready", "bonus_summed",
                             "bonus_copied", "n_mm", "n_masked", "prod_mm", "prod_masked"))
        (n_saved, nd_landed, solved, y_saved, z_zeroed, z_landed, n_cut, tok_mm, tok_evac, u_mm, u_rhs, u_sol,
         state_mm, state_ready, ymm, lnx_landed, yc_ready, yc_sq, y_var_ready, y_rstd_ready, bv_ready, o_ready) = (
            sem(n) for n in ("n_saved", "nd_landed", "solved", "y_saved", "z_zeroed", "z_landed", "n_cut", "tok_mm",
                             "tok_evac", "u_mm", "u_rhs", "u_sol", "state_mm", "state_ready", "y_mm", "lnx_landed",
                             "yc_ready", "yc_sq", "y_var_ready", "y_rstd_ready", "bv_ready", "o_ready"))

        def rwkv_pe(pe):
            xs = {name: chan(i) for name, i in W_XS.items()}
            lora = buf(W_LORA)

            def columns(name, x):
                for s in range(4):
                    w = weights(pe, FIRST[name] + s).rearrange("p (k n) -> p k n", n=T)
                    for n in range(2):
                        for k in range(DC):
                            mm = nc.tensor.matmul(bank[s][:, n * T:(n + 1) * T], w[:, k, n * P:(n + 1) * P], x[:, k, :],
                                                  start=(k == 0), stop=(k == DC - 1))
                    mm.then_inc(slot_done, 1)

            w = weights(pe, FIRST["lora_wa"])[:, 0:2 * DC * 64].rearrange("p (g k n) -> p g k n", g=2, k=DC)
            for g, name in enumerate(("w", "a")):
                pe.wait_ge(mix_done, MIXED[name])
                for k in range(DC):
                    mm = nc.tensor.matmul(bank[4 + g][0:64, 0:T], w[:, g, k, :], xs[name][:, k, :],
                                          start=(k == 0), stop=(k == DC - 1))
            mm.then_inc(slot_done, 1)
            pe.wait_ge(mix_done, MIXED["k"])
            columns("w_k", xs["k"])
            w = weights(pe, FIRST["lora_wa2"])
            pe.wait_ge(lora_hidden, 2)
            for g in range(2):
                if g == 1:
                    pe.wait_ge(k_evac, 4)
                for c in range(DC):
                    mm = nc.tensor.matmul(bank[(4, 0)[g] + c // 2][:, (c % 2) * T:(c % 2 + 1) * T],
                                          w[0:64, g * D + c * P:g * D + (c + 1) * P], lora[0:64, g * T:(g + 1) * T],
                                          start=True, stop=True)
            mm.then_inc(slot_done, 1)
            w = weights(pe, FIRST["lora_g"])[:, 0:DC * GATE_LORA].rearrange("p (k n) -> p k n", n=GATE_LORA)
            pe.wait_ge(mix_done, MIXED["g"])
            pe.wait_ge(decay_sig, 1)
            for lo, hi in ((0, P), (P, GATE_LORA)):
                at = 0 if lo == 0 else T
                for k in range(DC):
                    mm = nc.tensor.matmul(bank[4][0:hi - lo, at:at + T], w[:, k, lo:hi], xs["g"][:, k, :],
                                          start=(k == 0), stop=(k == DC - 1))
            mm.then_inc(slot_done, 1)
            pe.wait_ge(mix_done, MIXED["r"])
            pe.wait_ge(iclr_sig, 4)
            columns("w_r", xs["r"])
            pe.wait_ge(kk_squared, 1)
            pe.wait_ge(decay_sig, 4)
            pe.wait_ge(gate_hidden, 2)
            for j in range(4):
                nc.tensor.matmul(bank[4 + j][:, :], const("same_head"), buf(W_RINV, j * HALF, (j + 1) * HALF),
                                 start=True, stop=True).then_inc(kk_normed, 1)
            w = weights(pe, FIRST["lora_g2"])
            pe.wait_ge(r_evac, 4)
            for a in range(NT):
                for half in range(2):
                    dst = bank[2 * a + half][:, :]
                    nc.tensor.matmul(dst, lora[:, 2 * T + a * P:2 * T + (a + 1) * P],
                                     w[:, half * HALF:(half + 1) * HALF], start=True, stop=False)
                    mm = nc.tensor.matmul(dst, lora[0:32, 3 * T + a * P:3 * T + (a + 1) * P],
                                          w[0:32, D + half * HALF:D + (half + 1) * HALF], start=False, stop=True)
            mm.then_inc(slot_done, 1)
            pe.wait_ge(mix_done, MIXED["v"])
            pe.wait_ge(kk_root, 4)
            wide(pe, "w_v", 4, lambda k, a: xs["v"][:, k, a * P:(a + 1) * P], 4)

            remove, add, key, query = (chan(i) for i in (W_REMOVE, W_ADD, W_KEY, W_QUERY))

            def pair(dst, left, right, a, q, i):
                h = q % 2 + 2 * (4 * (q // 2) + i)
                lo = (h % 2) * N
                return nc.tensor.matmul(dst, left[lo:lo + N, h // 2, a * P:(a + 1) * P],
                                        right[lo:lo + N, h // 2, a * P:(a + 1) * P], start=True, stop=True)

            pe.wait_ge(removal_ready, 1)
            pe.wait_ge(g_evac, 4)
            for l in range(8):
                if l >= 4:
                    pe.wait_ge(n_masked, l - 3)
                for i in range(4):
                    mm = pair(bank[l % 4][:, i * P:(i + 1) * P], add, remove, l // 4, l % 4, i)
                mm.then_inc(n_mm, 1)
            pe.wait_ge(v_evac, 4)
            pe.wait_ge(keys_ready, 1)
            for l in range(24):
                left, right = ((key, remove), (add, query), (key, query))[l // 8]
                if l == 8:
                    pe.wait_ge(queries_ready, 1)
                if l >= 4:
                    pe.wait_ge(prod_masked, l - 3)
                for i in range(4):
                    mm = pair(bank[4 + l % 4][:, i * P:(i + 1) * P], left, right, l % 8 // 4, l % 4, i)
                mm.then_inc(prod_mm, 1)
            pe.wait_ge(n_masked, 8)
            for j in range(4):
                for i in range(4):
                    c = 4 * (j % 2) + i
                    mm = nc.tensor.transpose(bank[j][:, i * P:(i + 1) * P], (add, key)[j // 2][:, c, 0:P], ident)
                mm.then_inc(tok_mm, 1)
            pe.wait_ge(bonus_ready, 1)
            pe.wait_ge(prod_masked, 21)
            for a in range(NT):
                for c in range(DC):
                    mm = nc.tensor.matmul(bank[4][:, a * H + 2 * c:a * H + 2 * c + 2], chan(W_K)[:, c, a * P:(a + 1) * P],
                                          const("head_of"), start=True, stop=True)
            mm.then_inc(bonus_summed, 1)

            v, rhs, u, s0 = toks(W_V), buf(W_RHS, 0, D), buf(W_U, 0, D), buf(W_S0)
            bh = buf(W_TOK, 0, D)
            kh = buf(W_TOK, D, 2 * D)
            pe.wait_ge(prod_masked, 24)
            pe.wait_ge(tok_evac, 4)
            pe.wait_ge(bonus_copied, 1)
            for a in range(NT):
                z, n_off, lk, rb, rk = (heads(m[a]) for m in (W_Z, W_N, W_LK, W_RB, W_RK))
                if a == 1:
                    pe.wait_ge(state_ready, 1)
                for s in range(2 * NB):
                    for q in range(2):
                        if s == 1:
                            pe.wait_ge(z_landed, 16 * NT * NB)
                        if s == 2:
                            pe.wait_ge(n_cut, NT)
                        if s % 2 == 1:
                            pe.wait_ge(u_rhs, a * 2 * NB + (s - 1) + q + 1)
                        elif s > 0:
                            pe.wait_ge(u_sol, a * 2 * NB + (s - 2) + q + 1)
                        dst = bank[(s % 2) * 2 + q]
                        for i in range(8):
                            h = 2 * i + q
                            cells, hv = dst[:, i * N:(i + 1) * N], slice(h * N, (h + 1) * N)
                            hu = slice(q * HALF + i * N, q * HALF + (i + 1) * N)
                            if s == 0:
                                mm = nc.tensor.matmul(cells, lk[:, h, :], v[:, a, hv], start=True, stop=(a == 0))
                                if a == 1:
                                    lo, c = (h % 2) * N, h // 2
                                    mm = nc.tensor.matmul(cells, remove[lo:lo + N, c, P:2 * P],
                                                          s0[lo:lo + N, c * N:(c + 1) * N], start=False, stop=True)
                            elif s % 2 == 0:
                                mm = nc.tensor.matmul(cells, n_off[:, h, :], u[:, hu], start=True, stop=True)
                            else:
                                mm = nc.tensor.matmul(cells, z[:, h, :],
                                                      (rhs if s == 1 else buf(W_RHS, D, 2 * D))[:, hu], start=True, stop=True)
                        mm.then_inc(u_mm, 1)
                for q in range(2):
                    pe.wait_ge(u_sol, a * 2 * NB + 2 * (NB - 1) + q + 1)
                    for i in range(8):
                        h = 2 * i + q
                        cells, hv = bank[4 + 2 * a + q][:, i * N:(i + 1) * N], slice(h * N, (h + 1) * N)
                        hu = slice(q * HALF + i * N, q * HALF + (i + 1) * N)
                        nc.tensor.matmul(cells, rb[:, h, :], u[:, hu], start=True, stop=False)
                        mm = nc.tensor.matmul(cells, rk[:, h, :], v[:, a, hv], start=False, stop=(a == 0))
                        if a == 1:
                            lo, c = (h % 2) * N, h // 2
                            mm = nc.tensor.matmul(cells, query[lo:lo + N, c, P:2 * P], s0[lo:lo + N, c * N:(c + 1) * N],
                                                  start=False, stop=True)
                    mm.then_inc(ymm, 1)
                if a == 0:
                    for h in range(H):
                        lo, c, hv = (h % 2) * N, h // 2, slice(h * N, (h + 1) * N)
                        cells = bank[0][lo:lo + N, c * N:(c + 1) * N]
                        hu = slice((h % 2) * HALF + c * N, (h % 2) * HALF + (c + 1) * N)
                        nc.tensor.matmul(cells, bh[:, hv], u[:, hu], start=True, stop=False)
                        mm = nc.tensor.matmul(cells, kh[:, hv], v[:, 0, hv], start=False, stop=True)
                    mm.then_inc(state_mm, 1)
            pe.wait_ge(o_ready, 1)
            turn_pe(toks(W_YC), 0)
            turned_in(pe, TURN_RWKV)
            wide(pe, "w_o", 4, lambda k, a: chan(W_OT)[:, k, a * P:(a + 1) * P], 4)

        def rwkv_act(act):
            lora = buf(W_LORA)
            after_slots(act, "lora_wa")
            nc.scalar.activation(lora[0:64, 0:T], bank[4][0:64, 0:T], ACT.Tanh).then_inc(lora_hidden, 1)
            nc.scalar.activation(lora[0:64, T:2 * T], bank[5][0:64, 0:T], ACT.Copy).then_inc(lora_hidden, 1)
            for s in range(4):
                after_slots(act, "w_k", s + 1)
                nc.scalar.activation(buf(W_K, s * HALF, (s + 1) * HALF), bank[s][:, :], ACT.Copy).then_inc(k_evac, 1)
            after_slots(act, "lora_wa2")
            for bias, dst, base, done in (("a_w0", W_SIG, 4, decay_sig), ("a_a0", W_A, 0, iclr_sig)):
                for c in range(DC):
                    op = nc.scalar.activation(chan(dst)[:, c, :], bank[base + c // 2][:, (c % 2) * T:(c % 2 + 1) * T],
                                              ACT.Sigmoid, bias=col(bias, c))
                    if c % 2 == 1:
                        op.then_inc(done, 1)
            after_slots(act, "lora_g")
            nc.scalar.activation(lora[:, 2 * T:3 * T], bank[4][:, 0:T], ACT.Sigmoid).then_inc(gate_hidden, 1)
            nc.scalar.activation(lora[0:32, 3 * T:4 * T], bank[4][0:32, T:2 * T], ACT.Sigmoid).then_inc(gate_hidden, 1)
            act.wait_ge(kk_ready, 1)
            nc.scalar.activation(buf(W_RINV), buf(W_KK), ACT.Square).then_inc(kk_squared, 1)
            for s in range(4):
                after_slots(act, "w_r", s + 1)
                nc.scalar.activation(buf(W_R, s * HALF, (s + 1) * HALF), bank[s][:, :], ACT.Copy).then_inc(r_evac, 1)
            act.wait_ge(cum_ready, 1)
            nc.scalar.activation(buf(W_EP), buf(W_CUM), ACT.Exp, scale=-KAPPA).then_inc(decay_exp, 1)
            nc.scalar.activation(buf(W_EM), buf(W_CUM), ACT.Exp, scale=KAPPA).then_inc(decay_exp, 1)
            nc.scalar.activation(buf(W_SIG), buf(W_SIG), ACT.Exp, scale=-KAPPA).then_inc(decay_exp, 1)
            nc.scalar.activation(s_scale, last_e, ACT.Exp, scale=-KAPPA).then_inc(decay_exp, 1)
            for j in range(4):
                act.wait_ge(kk_normed, j + 1)
                nc.scalar.activation(buf(W_RINV, j * HALF, (j + 1) * HALF), bank[4 + j][:, :], ACT.Sqrt).then_inc(kk_root, 1)
            for name, dst, base, done in (("lora_g2", W_G, 0, g_evac), ("w_v", W_V, 4, v_evac)):
                after_slots(act, name)
                for j in range(4):
                    nc.scalar.activation(buf(dst, j * HALF, (j + 1) * HALF), bank[base + j][:, :], ACT.Copy).then_inc(done, 1)
            act.wait_ge(y_saved, 16)
            for j in range(4):
                act.wait_ge(tok_mm, j + 1)
                nc.scalar.activation(buf(W_TOK, j * HALF, (j + 1) * HALF), bank[j][:, :], ACT.Copy).then_inc(tok_evac, 1)
            for a in range(NT):
                for s in range(1, 2 * NB, 2):
                    for q in range(2):
                        act.wait_ge(u_mm, a * 4 * NB + 2 * s + q + 1)
                        if a == 1 and s == 1:
                            act.wait_ge(state_mm, 1)
                        nc.scalar.activation(buf(W_U, q * HALF, (q + 1) * HALF), bank[2 + q][:, :], ACT.Copy).then_inc(u_sol, 1)
            act.wait_ge(yc_ready, 1)
            nc.scalar.activation(buf(W_YSQ), buf(W_YC), ACT.Square).then_inc(yc_sq, 1)
            turn_act(act, TURN_RWKV, 0, [(None, W_OT)])

        def rwkv_dve(dve):
            hT, dx = chan(W_HT), chan(W_DX)
            turned_in(dve, TURN_PRE0)
            nc.vector.tensor_scalar(dx[:, :, 0:1], hT[:, :, 0:1], -1.0, None, ALU.mult)
            link(dve, nc.vector.tensor_tensor(dx[:, :, 1:T], hT[:, :, 0:T - 1], hT[:, :, 1:T], ALU.subtract))
            for name, row in MIXES:
                for c in range(DC):
                    op = nc.vector.scalar_tensor_tensor(chan(W_XS[name])[:, c, :], dx[:, c, :], col("a_mu", row * DC + c),
                                                        hT[:, c, :], ALU.mult, ALU.add)
                op.then_inc(mix_done, 1)
            kT, kk, sig, cum, aT = chan(W_K), chan(W_KK), chan(W_SIG), chan(W_CUM), chan(W_A)
            dve.wait_ge(k_evac, 4)
            for c in range(DC):
                op = nc.vector.tensor_scalar(kk[:, c, :], kT[:, c, :], col("a_k_k", c), None, ALU.mult)
            op.then_inc(kk_ready, 1)
            dve.wait_ge(decay_sig, 4)
            for c in range(DC):
                for a in range(NT):
                    t = slice(a * P, (a + 1) * P)
                    op = nc.vector.tensor_tensor_scan(cum[:, c, t], const("ones"), sig[:, c, t], 0.0, ALU.mult, ALU.add)
            link(dve, op)
            tiles = buf(W_CUM).rearrange("p (n t) -> p n t", t=P)
            link(dve, nc.vector.tensor_copy(mid, tiles[:, :, P // 2 - 1]))
            link(dve, nc.vector.tensor_tensor(tiles, tiles, spread(mid.unsqueeze(2), [P, 16, P]), ALU.subtract))
            nc.vector.tensor_tensor(last_e, tiles[:, 0:16:2, P - 1], mid[:, 1:16:2], ALU.add)
            nc.vector.tensor_tensor(buf(W_SIG), buf(W_CUM), buf(W_SIG), ALU.subtract).then_inc(cum_ready, 1)
            dve.wait_ge(iclr_sig, 4)
            for c in range(DC):
                op = nc.vector.tensor_scalar(chan(W_T1)[:, c, :], aT[:, c, :], 1.0, col("a_k_a", c), ALU.subtract, ALU.mult)
            link(dve, op)
            k_new = step(nc.vector.scalar_tensor_tensor(buf(W_K), buf(W_T1), 1.0, buf(W_K), ALU.add, ALU.mult))
            dve.wait_ge(kk_root, 4)
            link(dve, nc.vector.tensor_scalar(buf(W_RINV), buf(W_RINV), 1e-12, None, ALU.max))
            link(dve, nc.vector.reciprocal(buf(W_RINV), buf(W_RINV)))
            link(dve, nc.vector.tensor_tensor(buf(W_KK), buf(W_KK), buf(W_RINV), ALU.mult))
            link(dve, nc.vector.tensor_tensor(buf(W_A), buf(W_A), buf(W_KK), ALU.mult))
            dve.wait_ge(decay_exp, 4)
            nc.vector.scalar_tensor_tensor(buf(W_REMOVE), buf(W_KK), -1.0, buf(W_SIG), ALU.mult, ALU.mult)
            nc.vector.tensor_tensor(buf(W_ADD), buf(W_A), buf(W_EM), ALU.mult).then_inc(removal_ready, 1)
            dve.wait_ge(dve_step, k_new)
            nc.vector.tensor_tensor(buf(W_KEY), buf(W_K), buf(W_EM), ALU.mult).then_inc(keys_ready, 1)
            dve.wait_ge(r_evac, 4)
            nc.vector.tensor_tensor(buf(W_QUERY), buf(W_R), buf(W_EP), ALU.mult).then_inc(queries_ready, 1)
            dve.wait_ge(keys_ready, 1)
            for c in range(DC):
                op = nc.vector.scalar_tensor_tensor(kT[:, c, :], chan(W_R)[:, c, :], col("a_r_k", c), kT[:, c, :],
                                                    ALU.mult, ALU.mult)
            op.then_inc(bonus_ready, 1)

            def masked(dst, l, src, mask):
                first = l % 2 + 8 * (l % 4 // 2)
                return nc.vector.tensor_tensor(heads(dst[l % 8 // 4])[:, first:first + 7:2, :],
                                               src[:, :].rearrange("p (h t) -> p h t", t=P),
                                               spread(const(mask).unsqueeze(1), [P, 4, P]), ALU.mult)

            for l in range(8):
                dve.wait_ge(n_mm, l + 1)
                masked(W_N, l, bank[l % 4], "before").then_inc(n_masked, 1)
            for l in range(24):
                dve.wait_ge(prod_mm, l + 1)
                masked((W_LK, W_RB, W_RK)[l // 8], l, bank[4 + l % 4],
                       ("before", "upto", "upto")[l // 8]).then_inc(prod_masked, 1)
            dve.wait_ge(bonus_summed, 1)
            nc.vector.tensor_copy(bon, bank[4][:, 0:NT * H]).then_inc(bonus_copied, 1)
            link(dve, nc.vector.memset(buf(W_SOLVE, BS * BS, 2 * BS * BS), 0.0))
            link(dve, nc.vector.memset(buf(W_SOLVE, BS * BS, 2 * BS * BS)[:, 0:BS * BS:BS + 1], 1.0))
            dve.wait_ge(nd_landed, 16)
            for j in range(BS - 1):
                m, w = j + 1, BS - 1 - j
                outer = solve_tmp[:, 0:m * w].rearrange("p (s t) -> p s t", t=w)
                link(dve, nc.vector.tensor_tensor(outer, spread(yd[:, 0:m, j:j + 1], [P, m, w]),
                                                  spread(nd[:, j:j + 1, j + 1:BS], [P, m, w]), ALU.mult))
                op = nc.vector.tensor_tensor(yd[:, 0:m, j + 1:BS], yd[:, 0:m, j + 1:BS], outer, ALU.add)
                if j < BS - 2:
                    link(dve, op)
            op.then_inc(solved, 1)
            for a in range(NT):
                for s in range(0, 2 * NB, 2):
                    for q in range(2):
                        dve.wait_ge(u_mm, a * 4 * NB + 2 * s + q + 1)
                        cells = slice(q * HALF, (q + 1) * HALF)
                        if s == 0:
                            if a == 0 and q == 0:
                                dve.wait_ge(tok_mm, 4)
                            op = nc.vector.tensor_copy(buf(W_RHS, 0, D)[:, cells], bank[q][:, :])
                        else:
                            op = nc.vector.tensor_tensor(buf(W_RHS, D, 2 * D)[:, cells], bank[q][:, :],
                                                         buf(W_RHS, 0, D)[:, cells], ALU.add)
                        op.then_inc(u_rhs, 1)
                if a == 0:
                    dve.wait_ge(state_mm, 1)
                    nc.vector.tensor_tensor(buf(W_S0, 0, HP * N).rearrange("p (c n) -> p c n", n=N),
                                            bank[0][:, :].rearrange("p (c n) -> p c n", n=N),
                                            spread(s_scale.unsqueeze(2), [P, HP, N]), ALU.mult).then_inc(state_ready, 1)
            yc = buf(W_YC)
            sums = []
            for j in range(4):
                dve.wait_ge(ymm, j + 1)
                sums.append(step(nc.vector.tensor_reduce(y_sum[:, 8 * j:8 * j + 8],
                                                         bank[4 + j][:, :].rearrange("p (h n) -> p h n", n=N), AX, ALU.add)))
            dve.wait_ge(dve_step, sums[-1])
            link(dve, nc.vector.tensor_scalar(y_mean, y_sum, -1.0 / N, None, ALU.mult))
            for j in range(4):
                op = nc.vector.tensor_tensor(toks(W_YC)[:, j // 2, :].rearrange("p (c g n) -> p g c n", g=2, n=N)[:, j % 2],
                                             bank[4 + j][:, :].rearrange("p (h n) -> p h n", n=N),
                                             spread(y_mean[:, 8 * j:8 * j + 8].unsqueeze(2), [P, 8, N]), ALU.add)
            op.then_inc(yc_ready, 1)
            dve.wait_ge(yc_sq, 1)
            link(dve, nc.vector.tensor_reduce(y_sq, buf(W_YSQ).rearrange("p (h n) -> p h n", n=N), AX, ALU.add))
            nc.vector.tensor_scalar(y_var, y_sq, 1.0 / N, LNX_EPS, ALU.mult, ALU.add).then_inc(y_var_ready, 1)
            dve.wait_ge(y_rstd_ready, 1)
            dve.wait_ge(yc_ready, 1)
            y32 = yc.rearrange("p (h n) -> p h n", n=N)
            link(dve, nc.vector.tensor_tensor(y32, y32, spread(y_rstd.unsqueeze(2), [P, NT * H, N]), ALU.mult))
            dve.wait_ge(lnx_landed, 32)
            for i, op in ((0, ALU.mult), (1, ALU.add)):
                link(dve, nc.vector.tensor_tensor(toks(W_YC), toks(W_YC),
                                                  spread(buf(W_LNX, i * D, (i + 1) * D).unsqueeze(1), [P, NT, D]), op))
            dve.wait_ge(bv_ready, 1)
            link(dve, nc.vector.tensor_tensor(yc, yc, buf(W_BV), ALU.add))
            nc.vector.tensor_tensor(yc, yc, buf(W_G), ALU.mult).then_inc(o_ready, 1)
            turn_dve(dve, TURN_RWKV, 0, [(None, W_OT)])

        def rwkv_pool(pool):
            after_slots(pool, "w_v")
            for m in W_Z:
                nc.gpsimd.memset(buf(m), 0.0).then_inc(z_zeroed, 1)
            pool.wait_ge(n_saved, 16 * NT * NB)
            for m in W_N:
                nc.gpsimd.tensor_tensor(heads(m), heads(m), spread(const("off").unsqueeze(1), [P, H, P]),
                                        ALU.mult).then_inc(n_cut, 1)
            pool.wait_ge(u_mm, 8 * NB)
            pool.dma_start(buf(W_LNX, 0, D), A["a_lnx_w"][0].partition_broadcast(P)).then_inc(lnx_landed, 16)
            pool.dma_start(buf(W_LNX, D, 2 * D), A["a_lnx_b"][0].partition_broadcast(P)).then_inc(lnx_landed, 16)
            pool.wait_ge(ymm, 4)
            nc.gpsimd.tensor_tensor(buf(W_BV).rearrange("p (h n) -> p h n", n=N), buf(W_V).rearrange("p (h n) -> p h n", n=N),
                                    spread(bon.unsqueeze(2), [P, NT * H, N]), ALU.mult).then_inc(bv_ready, 1)
            pool.wait_ge(y_var_ready, 1)
            nc.gpsimd.tensor_tensor(y_rstd, y_var, minus_half, ALU.pow).then_inc(y_rstd_ready, 1)

        def rwkv_blocks_sp(sp):
            for a in range(NT):
                for b in range(NB):
                    if b == 0:
                        sp.wait_ge(n_masked, 4 * (a + 1))
                    sp.dma_start(n_dram[a, :, b].rearrange("h s t -> s h t"),
                                 heads(W_N[a])[b * BS:(b + 1) * BS, :, b * BS:(b + 1) * BS]).then_inc(n_saved, 16)
            sp.wait_ge(n_saved, 16 * NT * NB)
            sp.wait_ge(bonus_ready, 1)
            sp.dma_start(buf(W_SOLVE, 0, BS * BS), n_dram.rearrange("a h b s t -> (a h b) (s t)")).then_inc(nd_landed, 16)
            sp.wait_ge(solved, 1)
            sp.dma_start(y_dram.rearrange("a h b s t -> (a h b) (s t)"), buf(W_SOLVE, BS * BS, 2 * BS * BS)).then_inc(y_saved, 16)
            sp.wait_ge(y_saved, 16)
            sp.wait_ge(z_zeroed, NT)
            for a in range(NT):
                for b in range(NB):
                    sp.dma_start(heads(W_Z[a])[b * BS:(b + 1) * BS, :, b * BS:(b + 1) * BS],
                                 y_dram[a, :, b].rearrange("h s t -> s h t")).then_inc(z_landed, 16)

        M_H, M_XKV, M_TOK, M_LATT, M_K, M_Q, M_V, M_ROT, M_S, M_PT, M_OT = 0, 1, 2, 3, 4, 6, 8, 9, 10, 11, 12
        ckv = buf(M_TOK, 0, NT * KV_LORA).rearrange("p (a n) -> p a n", a=NT)
        cq = buf(M_TOK, 512, 512 + NT * Q_LORA).rearrange("p (a n) -> p a n", a=NT)
        kr = buf(M_TOK, 1280, 1280 + NT * QK).rearrange("p (a n) -> p a n", a=NT)
        kraw = buf(M_TOK, 1472, 1472 + NT * ROPE).rearrange("p (a n) -> p a n", a=NT)
        krt = [buf(M_TOK, 1536 + 32 * i, 1568 + 32 * i).rearrange("p (a n) -> p a n", a=NT) for i in range(4)]
        ckvT = buf(M_LATT, 0, 512).rearrange("p (c t) -> p c t", t=T)
        cqT = buf(M_LATT, 512, 1280).rearrange("p (c t) -> p c t", t=T)
        kT = arena[:, M_K:M_K + 2, :].rearrange("p b (h t) -> p (b h) t", t=T)
        qT = arena[:, M_Q:M_Q + 2, :].rearrange("p b (h t) -> p (b h) t", t=T)
        s_buf = [buf(M_S, i * 384, (i + 1) * 384) for i in range(2)]
        pt_buf = [buf(M_PT, i * 384, (i + 1) * 384) for i in range(2)]
        lat_sum, lat_var, lat_rstd = small(4), small(4), small(4)
        sm_nmax, sm_sum, sm_inv = small(2 * H), small(2 * H), small(2 * H)
        (lat_ss, lat_var_ready, lat_rstd_ready, lat_ready, lat_turned, lat_in, krope_in, nope_evac, vh_evac, q_evac, perm_mm,
         q_roped, s_mm, sm_max, sm_exp, p_ready, pt_mm, pt_evac, pv_mm, ot_evac) = (
            sem(n) for n in ("lat_ss", "lat_var_ready", "lat_rstd_ready", "lat_ready", "lat_turned", "lat_in", "krope_in",
                             "nope_evac", "vh_evac", "q_evac", "perm_mm", "q_roped", "mla_s_mm", "mla_max", "mla_exp",
                             "mla_p_ready", "mla_pt_mm", "mla_pt_evac", "mla_pv_mm", "mla_ot_evac"))

        def mla_pe(pe):
            turned_in(pe, TURN_PRE2)
            for name, src, width, base in (("kv_down", M_XKV, KV_LORA + ROPE, 0), ("q_down", M_H, Q_LORA, 2)):
                for s in range(2):
                    w = weights(pe, FIRST[name] + s)
                    for kk in range(4):
                        k = 4 * s + kk
                        for a in range(NT):
                            mm = nc.tensor.matmul(bank[base + a][:, 0:width], chan(src)[:, k, a * P:(a + 1) * P],
                                                  w[:, kk * width:(kk + 1) * width], start=(k == 0), stop=(k == DC - 1))
                    mm.then_inc(slot_done, 1)
            pe.wait_ge(lat_ready, 1)
            for a in range(NT):
                for c in range(2):
                    nc.tensor.transpose(bank[4][:, c * T + a * P:c * T + (a + 1) * P], ckv[:, a, c * P:(c + 1) * P], ident)
                for c in range(3):
                    nc.tensor.transpose(bank[5 + c // 2][:, (c % 2) * T + a * P:(c % 2) * T + (a + 1) * P],
                                        cq[:, a, c * P:(c + 1) * P], ident)
                mm = nc.tensor.transpose(bank[7][0:QK, a * P:(a + 1) * P], kr[:, a, :], ident)
            mm.then_inc(lat_turned, 1)
            pe.wait_ge(lat_in, 5)
            for s in range(2):
                w = weights(pe, FIRST["kv_up"] + s).rearrange("p (k h n) -> p k h n", k=2, n=2 * N)
                if s == 1:
                    pe.wait_ge(krope_in, 1)
                for i in range(8):
                    if s == 1 and i % 2 == 0:
                        pe.wait_ge(nope_evac, i // 2 + 1)
                    for k in range(2):
                        mm = nc.tensor.matmul(bank[i // 2][0:NOPE, (i % 2) * T:(i % 2 + 1) * T], w[:, k, i, 0:NOPE], ckvT[:, k, :],
                                              start=(k == 0), stop=(k == 1))
                for a in range(NT):
                    for k in range(2):
                        mm = nc.tensor.matmul(bank[4 + 2 * s + a][:, :].rearrange("p (h n) -> p h n", n=N),
                                              ckvT[:, k, a * P:(a + 1) * P], w[:, k, :, NOPE:2 * N],
                                              start=(k == 0), stop=(k == 1))
                mm.then_inc(slot_done, 1)
            pe.wait_ge(nope_evac, 8)
            for s in range(4):
                w = weights(pe, FIRST["q_up"] + s)[:, 0:3 * 4 * QK].rearrange("p (k n) -> p k n", k=3)
                for i in range(4):
                    g = 2 * s + i // 2
                    if g >= 4 and i % 2 == 0:
                        pe.wait_ge(q_evac, g - 3)
                    for k in range(3):
                        mm = nc.tensor.matmul(bank[g % 4][0:QK, (i % 2) * T:(i % 2 + 1) * T], w[:, k, i * QK:(i + 1) * QK],
                                              cqT[:, k, :], start=(k == 0), stop=(k == 2))
                mm.then_inc(slot_done, 1)
            pe.wait_ge(vh_evac, 4)
            for g in range(8):
                pe.wait_ge(q_evac, g + 1)
                if g >= 4:
                    pe.wait_ge(q_roped, g - 3)
                nc.tensor.matmul(bank[4 + g % 4][0:QK, :], const("perm")[0:QK, :], qT[0:QK, 2 * g:2 * g + 2, :],
                                 start=True, stop=True).then_inc(perm_mm, 1)
            pe.wait_ge(q_roped, 8)
            v = toks(M_V)

            def scores(h):
                if h >= 2:
                    pe.wait_ge(sm_max, h - 1)
                for i, (a, b) in enumerate(((0, 0), (1, 1), (1, 0))):
                    mm = nc.tensor.matmul(bank[h % 2][:, i * P:(i + 1) * P], qT[0:QK, h, a * P:(a + 1) * P],
                                          kT[0:QK, h, b * P:(b + 1) * P], start=True, stop=True)
                mm.then_inc(s_mm, 1)

            def turn_p(h):
                pe.wait_ge(p_ready, h + 1)
                if h >= 2:
                    pe.wait_ge(pt_evac, h - 1)
                for i in range(3):
                    mm = nc.tensor.transpose(bank[2 + h % 2][:, i * P:(i + 1) * P], s_buf[h % 2][:, i * P:(i + 1) * P], ident)
                mm.then_inc(pt_mm, 1)

            def values(h):
                pe.wait_ge(pt_evac, h + 1)
                c, rows_, hv = h // 2, slice((h % 2) * N, (h % 2 + 1) * N), slice(h * N, (h + 1) * N)
                dst = bank[4 + c // 2][rows_, (c % 2) * T:(c % 2 + 1) * T]
                pt = pt_buf[h % 2]
                nc.tensor.matmul(dst[:, 0:P], v[:, 0, hv], pt[:, 0:P], start=True, stop=True)
                nc.tensor.matmul(dst[:, P:T], v[:, 1, hv], pt[:, P:2 * P], start=True, stop=False)
                nc.tensor.matmul(dst[:, P:T], v[:, 0, hv], pt[:, 2 * P:3 * P], start=False, stop=True).then_inc(pv_mm, 1)

            scores(0)
            for h in range(H):
                if h + 1 < H:
                    scores(h + 1)
                turn_p(h)
                if h >= 1:
                    values(h - 1)
            values(H - 1)
            pe.wait_ge(ot_evac, 4)
            wide(pe, "o_w", 4, lambda k, a: chan(M_OT)[:, k, a * P:(a + 1) * P], 4)

        def mla_act(act):
            after_slots(act, "kv_down")
            for i in range(4):
                if i == 2:
                    after_slots(act, "q_down")
                n = (KV_LORA, Q_LORA)[i // 2]
                nc.scalar.activation(buf(SQ, i * HALF, i * HALF + n), bank[i][:, 0:n], ACT.Square,
                                     accum_out=lat_sum[:, i:i + 1]).then_inc(lat_ss, 1)
            act.wait_ge(lat_turned, 1)
            nc.scalar.activation(kT[NOPE:QK, :, :], spread(bank[7][NOPE:QK, 0:T].unsqueeze(1), [ROPE, H, T]),
                                 ACT.Copy).then_inc(krope_in, 1)
            for s in range(2):
                after_slots(act, "kv_up", s + 1)
                for j in range(4):
                    h = 8 * s + 2 * j
                    nc.scalar.activation(kT[0:NOPE, h:h + 2, :], bank[j][0:NOPE, :].rearrange("p (h t) -> p h t", t=T),
                                         ACT.Copy).then_inc(nope_evac, 1)
            for g in range(8):
                after_slots(act, "q_up", g // 2 + 1)
                nc.scalar.activation(qT[0:QK, 2 * g:2 * g + 2, :], bank[g % 4][0:QK, :].rearrange("p (h t) -> p h t", t=T),
                                     ACT.Copy).then_inc(q_evac, 1)

            def exps(h):
                act.wait_ge(sm_max, h + 1)
                for a, (lo, hi) in enumerate(((0, P), (P, 3 * P))):
                    op = nc.scalar.activation(s_buf[h % 2][:, lo:hi], s_buf[h % 2][:, lo:hi], ACT.Exp,
                                              bias=sm_nmax[:, 2 * h + a:2 * h + a + 1],
                                              accum_out=sm_sum[:, 2 * h + a:2 * h + a + 1])
                op.then_inc(sm_exp, 1)

            def evac(h):
                act.wait_ge(pt_mm, h + 1)
                if h >= 2:
                    act.wait_ge(pv_mm, h - 1)
                nc.scalar.activation(pt_buf[h % 2], bank[2 + h % 2][:, 0:3 * P], ACT.Copy).then_inc(pt_evac, 1)

            def outputs(b):
                act.wait_ge(pv_mm, 4 * (b + 1))
                nc.scalar.activation(buf(M_OT, b * HALF, (b + 1) * HALF), bank[4 + b][:, :], ACT.Copy).then_inc(ot_evac, 1)

            for h in range(H):
                exps(h)
                if h >= 1:
                    evac(h - 1)
                if h >= 6 and h % 4 == 2:
                    outputs(h // 4 - 1)
            evac(H - 1)
            outputs(3)

        def mla_dve(dve):
            nc.vector.memset(kr[:, :, 0:NOPE], 0.0)
            dve.wait_ge(lat_ss, 4)
            link(dve, nc.vector.tensor_scalar(lat_var[:, 0:2], lat_sum[:, 0:2], 1.0 / KV_LORA, EPS, ALU.mult, ALU.add))
            nc.vector.tensor_scalar(lat_var[:, 2:4], lat_sum[:, 2:4], 1.0 / Q_LORA, EPS, ALU.mult, ALU.add).then_inc(lat_var_ready, 1)
            for a in range(NT):
                op = nc.vector.tensor_copy(kraw[:, a, :], bank[a][:, KV_LORA:KV_LORA + ROPE])
            link(dve, op)
            half = ROPE // 2
            x1, x2 = kraw[:, :, 0:half], kraw[:, :, half:ROPE]
            cos, sin = (const(n).rearrange("p (a n) -> p a n", a=NT) for n in ("kcos", "ksin"))
            for i, (x, f) in enumerate(((x1, cos), (x2, sin), (x1, sin), (x2, cos))):
                op = nc.vector.tensor_tensor(krt[i], x, f, ALU.mult)
            link(dve, op)
            nc.vector.tensor_tensor(kr[:, :, NOPE:NOPE + half], krt[0], krt[1], ALU.subtract)
            nc.vector.tensor_tensor(kr[:, :, NOPE + half:QK], krt[2], krt[3], ALU.add)
            dve.wait_ge(lat_rstd_ready, 1)
            for i in range(4):
                n, dst = ((KV_LORA, ckv), (Q_LORA, cq))[i // 2]
                op = nc.vector.tensor_scalar(dst[:, i % 2, :], bank[i][:, 0:n], lat_rstd[:, i:i + 1], None, ALU.mult)
            op.then_inc(lat_ready, 1)
            dve.wait_ge(lat_turned, 1)
            for c in range(5):
                src = bank[4 + c // 2][:, (c % 2) * T:(c % 2 + 1) * T]
                dst, gain = (ckvT[:, c, :], col("kv_a_norm_g", c)) if c < 2 else (cqT[:, c - 2, :], col("q_norm_g", c - 2))
                nc.vector.tensor_scalar(dst, src, gain, None, ALU.mult).then_inc(lat_in, 1)
            for s in range(2):
                after_slots(dve, "kv_up", s + 1)
                for a in range(NT):
                    nc.vector.tensor_copy(toks(M_V)[:, a, s * HALF:(s + 1) * HALF], bank[4 + 2 * s + a][:, :]).then_inc(vh_evac, 1)
            rot = slice(NOPE, QK)
            for g in range(8):
                q = qT[rot, 2 * g:2 * g + 2, :]
                tmp = arena[rot, M_ROT, (g % 2) * HALF:(g % 2 + 1) * HALF].rearrange("p (h t) -> p h t", t=T)
                sin, cos = (spread(cst[rot, CONST_AT[n]:CONST_AT[n] + T].unsqueeze(1), [ROPE, 2, T]) for n in ("sinT", "cosT"))
                dve.wait_ge(perm_mm, g + 1)
                nc.vector.tensor_tensor(tmp, bank[4 + g % 4][rot, :].rearrange("p (h t) -> p h t", t=T), sin, ALU.mult)
                link(dve, nc.vector.tensor_tensor(q, q, cos, ALU.mult))
                nc.vector.tensor_tensor(q, q, tmp, ALU.add).then_inc(q_roped, 1)

            def maxima(h):
                dve.wait_ge(s_mm, h + 1)
                if h >= 2:
                    dve.wait_ge(pt_mm, h - 1)
                s = s_buf[h % 2]
                link(dve, nc.vector.scalar_tensor_tensor(s, bank[h % 2][:, 0:3 * P], MLA_SCALE, const("maskb"), ALU.mult, ALU.add))
                nc.vector.tensor_reduce(sm_nmax[:, 2 * h:2 * h + 1], s[:, 0:P], AX, ALU.max, negate=True)
                nc.vector.tensor_reduce(sm_nmax[:, 2 * h + 1:2 * h + 2], s[:, P:3 * P], AX, ALU.max, negate=True).then_inc(sm_max, 1)

            def normalize(h):
                dve.wait_ge(sm_exp, h + 1)
                link(dve, nc.vector.reciprocal(sm_inv[:, 2 * h:2 * h + 2], sm_sum[:, 2 * h:2 * h + 2]))
                for a, (lo, hi) in enumerate(((0, P), (P, 3 * P))):
                    op = nc.vector.tensor_scalar(s_buf[h % 2][:, lo:hi], s_buf[h % 2][:, lo:hi],
                                                 sm_inv[:, 2 * h + a:2 * h + a + 1], None, ALU.mult)
                op.then_inc(p_ready, 1)

            for h in range(H):
                maxima(h)
                if h >= 1:
                    normalize(h - 1)
            normalize(H - 1)

        def mla_pool(pool):
            pool.wait_ge(lat_var_ready, 1)
            nc.gpsimd.tensor_tensor(lat_rstd, lat_var, minus_half[:, 0:4], ALU.pow).then_inc(lat_rstd_ready, 1)

        B_H, B_XC, B_XS, B_Z, B_GA, B_GS, B_QK, B_QR, B_QT, B_P, B_PT, B_OT = 0, 1, 3, 4, 5, 6, 7, 8, 9, 10, 11, 12
        B_CB, B_XF, B_XB, B_LHS, B_E, B_Y, B_SQ = 13, 14, 15, 16, 17, 1, 2
        HD = (GH + GKV) * N
        xcT = arena[:, B_XC:B_XC + 2, :].rearrange("p b s -> p (b s)")[:, 0:XC * T].rearrange("p (c t) -> p c t", t=T)
        xc_acc = [buf(B_XC + 1, 1024 + i * T, 1024 + (i + 1) * T) for i in range(4)]
        qk = buf(B_QK, 0, NT * HD).rearrange("p (a n) -> p a n", a=NT)
        vg = buf(B_QK, NT * HD, NT * HD + NT * P).rearrange("p (a n) -> p a n", a=NT)
        qr = buf(B_QR, 0, NT * HD).rearrange("p (a n) -> p a n", a=NT)
        rot_tmp = [buf(B_QR, NT * HD + i * HD // 2, NT * HD + (i + 1) * HD // 2) for i in range(2)]
        qgT = buf(B_QT, 0, GJ * T).rearrange("p (j t) -> p j t", t=T)
        kgT = buf(B_QT, GJ * T, (GJ + 1) * T)
        qk_gain = buf(B_QT, (GJ + 1) * T, (GJ + 1) * T + HD)
        gp_buf = [buf(B_P, i * HALF, (i + 1) * HALF) for i in range(2)]
        gpt_buf = [buf(B_PT, i * HALF, (i + 1) * HALF) for i in range(2)]
        cb = [buf(B_CB, g * 768, (g + 1) * 768).rearrange("p (n l) -> p n l", l=P) for g in range(2)]
        seg_lhs = [buf(B_LHS, i * 768, (i + 1) * 768).rearrange("p (n l) -> p n l", l=P) for i in range(2)]
        e_buf = [buf(B_E, i * 768, (i + 1) * 768) for i in range(2)]
        arena_small = buf(B_OT, GJ * T, SLOT)
        (dt_bias, a_log, dt_x, dt_n, dt_e, dt_l, dt, adt) = (
            arena_small[:, i * 64:(i + 1) * 64].rearrange("p (a h) -> p a h", a=NT) for i in range(8))
        d_skip = arena_small[:, 512:512 + H]
        qk_ss, qk_var, qk_rstd = (arena_small[:, 540 + 20 * i:560 + 20 * i] for i in range(3))
        g_max, g_nmax, g_sum, g_inv = (arena_small[:, 600 + 16 * i:616 + 16 * i] for i in range(4))
        yg_ss, yg_var, yg_rstd = (arena_small[:, 670 + 2 * i:672 + 2 * i] for i in range(3))
        (blk_params, kv_evac, dt_read, conv2_done, xc_done, qg_evac, z_evac, gate_evac, dt_neg, dt_exp, dt_ln, a_exp, adt_ready, qk_sq,
         qk_var_ready, qk_rstd_ready, qk_roped, qk_turned, qk_in, cb_mm, cb_in, xs_turned, xs_in, xd_f_ready, xd_b_ready) = (
            sem(n) for n in ("blk_params", "kv_evac", "dt_read", "conv2_done", "xc_done", "qg_evac", "z_evac", "gate_evac",
                             "dt_neg", "dt_exp", "dt_ln", "a_exp", "adt_ready", "qk_sq", "qk_var_ready", "qk_rstd_ready", "qk_roped",
                             "qk_turned", "qk_in", "cb_mm", "cb_in", "xs_turned", "xs_in", "xd_f_ready", "xd_b_ready"))
        (g_s_mm, g_max_ready, g_exp, g_p_ready, g_pt_mm, g_pt_evac, g_pv_mm, g_ot_evac, lhs_ready, seg_mm, e_ready,
         m_ready, ssd_mm, dx_ready, yz_ready, yg_sq, yg_var_ready, yg_rstd_ready, yn_a, yn_v, attn_gated, mix_ready) = (
            sem(n) for n in ("gqa_s_mm", "gqa_max", "gqa_exp", "gqa_p_ready", "gqa_pt_mm", "gqa_pt_evac", "gqa_pv_mm",
                             "gqa_ot_evac", "lhs_ready", "seg_mm", "e_ready", "m_ready", "ssd_mm", "dx_ready", "yz_ready",
                             "yg_sq", "yg_var_ready", "yg_rstd_ready", "yn_a", "yn_v", "attn_gated", "mix_ready"))
        B_MIX, B_T2, B_DX = 11, 10, 3

        def block_pe(pe):
            turned_in(pe, TURN_PRE4)
            hT = chan(B_H)
            for s in range(2):
                w = weights(pe, FIRST["kvdt"] + s)[:, 0:4 * 288].rearrange("p (k n) -> p k n", n=288)
                for kk in range(4):
                    k = 4 * s + kk
                    for a in range(NT):
                        mm = nc.tensor.matmul(bank[2 + a][:, 0:288], hT[:, k, a * P:(a + 1) * P], w[:, kk, :],
                                              start=(k == 0), stop=(k == DC - 1))
                mm.then_inc(slot_done, 1)
            for s in range(6):
                w = weights(pe, FIRST["xbc"] + s).rearrange("p (k n) -> p k n", n=T)
                if s >= 4:
                    pe.wait_ge(conv2_done, 2 * (s - 3))
                for n in range(2):
                    for k in range(DC):
                        mm = nc.tensor.matmul(bank[4 + s % 4][:, n * T:(n + 1) * T], w[:, k, n * P:(n + 1) * P], hT[:, k, :],
                                              start=(k == 0), stop=(k == DC - 1))
                mm.then_inc(slot_done, 1)
            for s in range(2):
                w = weights(pe, FIRST["q"] + s).rearrange("p (k n) -> p k n", n=HALF)
                for kk in range(4):
                    k = 4 * s + kk
                    for a in range(NT):
                        mm = nc.tensor.matmul(bank[a][:, :], hT[:, k, a * P:(a + 1) * P], w[:, kk, :],
                                              start=(k == 0), stop=(k == DC - 1))
                mm.then_inc(slot_done, 1)
            pe.wait_ge(conv2_done, XC)
            wide(pe, "z", 4, lambda k, a: hT[:, k, a * P:(a + 1) * P], 4)
            for g in range(2):
                if g == 0:
                    pe.wait_ge(qg_evac, NT)
                    pe.wait_ge(dt_read, 1)
                else:
                    pe.wait_ge(z_evac, 4)
                for s in range(4):
                    w = weights(pe, FIRST["gates"] + 4 * g + s)
                    for kk in range(2):
                        k = 2 * s + kk
                        for a in range(NT):
                            for half in range(2):
                                mm = nc.tensor.matmul(bank[4 * g + 2 * a + half][:, :], hT[:, k, a * P:(a + 1) * P],
                                                      w[:, kk * D + half * HALF:kk * D + (half + 1) * HALF],
                                                      start=(k == 0), stop=(k == DC - 1))
                    mm.then_inc(slot_done, 1)
            pe.wait_ge(xc_done, XC)
            pe.wait_ge(gate_evac, 8)
            for g in range(2):
                for b in range(NT):
                    mm = nc.tensor.matmul(bank[g][:, b * T:(b + 1) * T], xcT[:, 8 + g, b * P:(b + 1) * P], xcT[:, 10 + g, :],
                                          start=True, stop=True)
                mm.then_inc(cb_mm, 1)
            for j in range(4):
                for i in range(4):
                    a, c = j // 2, 4 * (j % 2) + i
                    mm = nc.tensor.transpose(bank[2 + j][:, i * P:(i + 1) * P], xcT[:, c, a * P:(a + 1) * P], ident)
                mm.then_inc(xs_turned, 1)
            pe.wait_ge(qk_roped, NT)
            for a in range(NT):
                for j in range(GJ):
                    nc.tensor.transpose(bank[6 + j // 2][:, (j % 2) * T + a * P:(j % 2) * T + (a + 1) * P], qr[:, a, j * P:(j + 1) * P], ident)
            pe.wait_ge(cb_in, 2)
            for a in range(NT):
                mm = nc.tensor.transpose(bank[0][:, a * P:(a + 1) * P], qr[:, a, GH * N:HD], ident)
            mm.then_inc(qk_turned, 1)

            def scores(i):
                j, g = i // GKV, i % GKV
                if i >= 2:
                    pe.wait_ge(g_exp, i - 1)
                for a in range(NT):
                    mm = nc.tensor.matmul(bank[i % 2][:, a * T:(a + 1) * T], qgT[g * N:(g + 1) * N, j, a * P:(a + 1) * P],
                                          kgT[g * N:(g + 1) * N, :], start=True, stop=True)
                mm.then_inc(g_s_mm, 1)

            def turn_p(i):
                pe.wait_ge(g_p_ready, i + 1)
                if i >= 2:
                    pe.wait_ge(g_pt_evac, i - 1)
                for b in range(NT):
                    for a in range(NT):
                        mm = nc.tensor.transpose(bank[2 + i % 2][:, b * T + a * P:b * T + (a + 1) * P],
                                                 gp_buf[i % 2][:, a * T + b * P:a * T + (b + 1) * P], ident)
                mm.then_inc(g_pt_mm, 1)

            def values(i):
                j, g = i // GKV, i % GKV
                pe.wait_ge(g_pt_evac, i + 1)
                for b in range(NT):
                    mm = nc.tensor.matmul(bank[4 + j // 2][g * N:(g + 1) * N, (j % 2) * T:(j % 2 + 1) * T],
                                          vg[:, b, g * N:(g + 1) * N], gpt_buf[i % 2][:, b * T:(b + 1) * T],
                                          start=(b == 0), stop=(b == NT - 1))
                mm.then_inc(g_pv_mm, 1)

            pe.wait_ge(qk_in, 3)
            pe.wait_ge(xs_in, 4)
            scores(0)
            for i in range(GH):
                if i + 1 < GH:
                    scores(i + 1)
                turn_p(i)
                if i >= 1:
                    values(i - 1)
            values(GH - 1)
            pe.wait_ge(g_ot_evac, 2)

            pe.wait_ge(xd_f_ready, 1)
            pe.wait_ge(xd_b_ready, 1)
            xf, xb = toks(B_XF), toks(B_XB)

            def segments(h):
                pe.wait_ge(lhs_ready, h + 1)
                if h >= 2:
                    pe.wait_ge(e_ready, h - 1)
                l, near, far = seg_lhs[h % 2], bank[2 * (h % 2)], bank[2 * (h % 2) + 1]
                for i, (n, right) in enumerate(((0, "upto"), (1, "upto"), (3, "from"), (4, "from"))):
                    nc.tensor.matmul(near[:, i * P:(i + 1) * P], l[:, n, :], const(right), start=True, stop=True)
                for i, (n, m, right) in enumerate(((0, 2, "upto"), (4, 5, "from"))):
                    nc.tensor.matmul(far[:, i * P:(i + 1) * P], l[:, n, :], const("ones"), start=True, stop=False)
                    mm = nc.tensor.matmul(far[:, i * P:(i + 1) * P], l[:, m, :], const(right), start=False, stop=True)
                mm.then_inc(seg_mm, 1)

            def mix_tokens(h):
                pe.wait_ge(m_ready, h + 1)
                m, hv = e_buf[h % 2], slice(h * N, (h + 1) * N)
                for a, parts in enumerate((((0, xf, 0), (2, xb, 0), (5, xb, 1)), ((4, xf, 0), (1, xf, 1), (3, xb, 1)))):
                    for i, (n, xd, b) in enumerate(parts):
                        mm = nc.tensor.matmul(bank[4 + 2 * a + h // 8][:, (h % 8) * N:(h % 8 + 1) * N], m[:, n * P:(n + 1) * P],
                                              xd[:, b, hv], start=(i == 0), stop=(i == 2))
                mm.then_inc(ssd_mm, 1)

            for h in range(H):
                segments(h)
                if h >= 1:
                    mix_tokens(h - 1)
            mix_tokens(H - 1)
            pe.wait_ge(e_ready, H)
            for s in range(2):
                w = weights(pe, FIRST["attn_proj"] + s)
                for kk in range(2):
                    j = 2 * s + kk
                    for a in range(NT):
                        for half in range(2):
                            mm = nc.tensor.matmul(bank[2 * a + half][:, :], buf(B_OT, j * T + a * P, j * T + (a + 1) * P),
                                                  w[:, kk * D + half * HALF:kk * D + (half + 1) * HALF],
                                                  start=(j == 0), stop=(j == GJ - 1))
                mm.then_inc(slot_done, 1)
            pe.wait_ge(attn_gated, 4)
            pe.wait_ge(yn_a, 1)
            pe.wait_ge(yn_v, 1)
            turn_pe(toks(B_Y), 0)
            turned_in(pe, TURN_SSD)
            wide(pe, "ssd_proj", 4, lambda k, a: chan(B_SQ)[:, k, a * P:(a + 1) * P], 4)
            pe.wait_ge(mix_ready, 1)
            turn_pe(toks(B_MIX), 0)
            turned_in(pe, TURN_MIX)
            wide(pe, "w_out", 4, lambda k, a: chan(B_T2)[:, k, a * P:(a + 1) * P], 4)

        def block_act(act):
            after_slots(act, "kvdt")
            for a in range(NT):
                nc.scalar.activation(qk[:, a, GH * N:HD], bank[2 + a][:, 0:P], ACT.Copy)
                nc.scalar.activation(vg[:, a, :], bank[2 + a][:, P:2 * P], ACT.Copy).then_inc(kv_evac, 1)
            for c in range(XC):
                act.wait_ge(conv2_done, c + 1)
                nc.scalar.activation(xcT[:, c, :], xc_acc[c % 4], ACT.Silu).then_inc(xc_done, 1)
            after_slots(act, "q")
            for a in range(NT):
                nc.scalar.activation(qk[:, a, 0:GH * N].rearrange("p (j g d) -> p g j d", g=GKV, d=N),
                                     bank[a][:, :].rearrange("p (g j d) -> p g j d", g=GKV, d=N), ACT.Copy).then_inc(qg_evac, 1)
            act.wait_ge(qg_evac, NT)
            act.wait_ge(kv_evac, NT)
            nc.scalar.activation(buf(B_P, 0, NT * HD), buf(B_QK, 0, NT * HD), ACT.Square).then_inc(qk_sq, 1)
            after_slots(act, "z")
            for j in range(4):
                nc.scalar.activation(buf(B_Z, j * HALF, (j + 1) * HALF), bank[4 + j][:, :], ACT.Silu).then_inc(z_evac, 1)
            for g, dst in enumerate((B_GA, B_GS)):
                after_slots(act, "gates", 4 * (g + 1))
                for j in range(4):
                    nc.scalar.activation(buf(dst, j * HALF, (j + 1) * HALF), bank[4 * g + j][:, :], ACT.Sigmoid).then_inc(gate_evac, 1)
            act.wait_ge(blk_params, 16 * 7)
            nc.scalar.activation(a_log[:, 0, :], a_log[:, 0, :], ACT.Exp).then_inc(a_exp, 1)
            act.wait_ge(dt_neg, 1)
            nc.scalar.activation(dt_e, dt_n, ACT.Exp).then_inc(dt_exp, 1)
            act.wait_ge(dt_exp, 1)
            nc.scalar.activation(dt_l, dt_e, ACT.Ln, bias=1.0).then_inc(dt_ln, 1)
            for j in range(4):
                act.wait_ge(xs_turned, j + 1)
                nc.scalar.activation(buf(B_XS, j * HALF, (j + 1) * HALF), bank[2 + j][:, :], ACT.Copy).then_inc(xs_in, 1)

            def exps(i):
                act.wait_ge(g_max_ready, i + 1)
                if i >= 2:
                    act.wait_ge(g_pt_mm, i - 1)
                for a in range(NT):
                    op = nc.scalar.activation(gp_buf[i % 2][:, a * T:(a + 1) * T], bank[i % 2][:, a * T:(a + 1) * T], ACT.Exp,
                                              bias=g_nmax[:, 2 * i + a:2 * i + a + 1], scale=GQA_SCALE,
                                              accum_out=g_sum[:, 2 * i + a:2 * i + a + 1])
                op.then_inc(g_exp, 1)

            def evac(i):
                act.wait_ge(g_pt_mm, i + 1)
                if i >= 2:
                    act.wait_ge(g_pv_mm, i - 1)
                nc.scalar.activation(gpt_buf[i % 2], bank[2 + i % 2][:, :], ACT.Copy).then_inc(g_pt_evac, 1)

            for i in range(GH):
                exps(i)
                if i >= 1:
                    evac(i - 1)
            evac(GH - 1)
            for b in range(2):
                act.wait_ge(g_pv_mm, 4 * (b + 1))
                nc.scalar.activation(buf(B_OT, b * HALF, (b + 1) * HALF), bank[4 + b][:, :], ACT.Copy).then_inc(g_ot_evac, 1)
            for h in range(H):
                act.wait_ge(seg_mm, h + 1)
                if h >= 2:
                    act.wait_ge(ssd_mm, h - 1)
                nc.scalar.activation(e_buf[h % 2][:, 0:HALF], bank[2 * (h % 2)][:, :], ACT.Exp)
                nc.scalar.activation(e_buf[h % 2][:, HALF:768], bank[2 * (h % 2) + 1][:, 0:T], ACT.Exp).then_inc(e_ready, 1)
            for a in range(NT):
                act.wait_ge(yz_ready, a + 1)
                nc.scalar.activation(buf(B_SQ, a * D, (a + 1) * D), toks(B_Y)[:, a, :], ACT.Square,
                                     accum_out=yg_ss[:, a:a + 1]).then_inc(yg_sq, 1)
            act.wait_ge(yg_rstd_ready, 1)
            nc.scalar.activation(toks(B_Y)[:, 0, :], toks(B_Y)[:, 0, :], ACT.Copy, scale=yg_rstd[:, 0:1]).then_inc(yn_a, 1)
            turn_act(act, TURN_SSD, 0, [(("ssd_norm_2", 0), B_SQ)])
            turn_act(act, TURN_MIX, 0, [(None, B_T2)])

        def block_dve(dve):
            dve.wait_ge(blk_params, 16 * 7)
            dve.wait_ge(kv_evac, NT)
            for a in range(NT):
                op = nc.vector.tensor_tensor(dt_x[:, a, :], bank[2 + a][:, 2 * P:2 * P + 32], dt_bias[:, 0, :], ALU.add)
            op.then_inc(dt_read, 1)
            dve.wait_ge(dt_read, 1)
            nc.vector.scalar_tensor_tensor(dt_n, dt_x, -1.0, dt_x, ALU.mult, ALU.min).then_inc(dt_neg, 1)
            for c in range(XC):
                u = bank[4 + (c // 2) % 4][:, (c % 2) * T:(c % 2 + 1) * T]
                acc = xc_acc[c % 4]
                after_slots(dve, "xbc", c // 2 + 1)
                if c >= 4:
                    dve.wait_ge(xc_done, c - 3)
                link(dve, nc.vector.tensor_scalar(acc, u, col("conv_w_2", 2 * XC + c), col("conv_b_2", c), ALU.mult, ALU.add))
                for j in (0, 1, 3, 4):
                    shift = j - 2
                    dst = slice(max(0, -shift), T - max(0, shift))
                    src = slice(max(0, shift), T - max(0, -shift))
                    op = nc.vector.scalar_tensor_tensor(acc[:, dst], u[:, src], col("conv_w_2", j * XC + c), acc[:, dst],
                                                        ALU.mult, ALU.add)
                    if j < 4:
                        link(dve, op)
                op.then_inc(conv2_done, 1)
            dve.wait_ge(qk_sq, 1)
            nh = GH + GKV
            link(dve, nc.vector.tensor_reduce(qk_ss, buf(B_P, 0, NT * HD).rearrange("p (h n) -> p h n", n=N), AX, ALU.add))
            nc.vector.tensor_scalar(qk_var, qk_ss, 1.0 / N, EPS, ALU.mult, ALU.add).then_inc(qk_var_ready, 1)
            dve.wait_ge(qk_rstd_ready, 1)
            qk_flat = buf(B_QK, 0, NT * HD).rearrange("p (h n) -> p h n", n=N)
            link(dve, nc.vector.tensor_tensor(qk_flat, qk_flat, spread(qk_rstd.unsqueeze(2), [P, NT * nh, N]), ALU.mult))
            link(dve, nc.vector.tensor_tensor(qk, qk, spread(qk_gain.unsqueeze(1), [P, NT, HD]), ALU.mult))
            for a in range(NT):
                src = qk[:, a, :].rearrange("p (h r n) -> p h r n", r=2, n=32)
                dst = qr[:, a, :].rearrange("p (h r n) -> p h r n", r=2, n=32)
                t0, t1 = (x.rearrange("p (h r n) -> p h r n", r=2, n=16) for x in rot_tmp)
                cos, sin = (spread(const(n, a * 32, (a + 1) * 32).rearrange("p (r n) -> p r n", r=2).unsqueeze(1),
                                   [P, nh, 2, 16]) for n in ("acos", "asin"))
                x1, x2 = src[:, :, :, 0:16], src[:, :, :, 16:32]
                for lo, f1, f2, op in ((0, cos, sin, ALU.subtract), (16, sin, cos, ALU.add)):
                    nc.vector.tensor_tensor(t0, x1, f1, ALU.mult)
                    link(dve, nc.vector.tensor_tensor(t1, x2, f2, ALU.mult))
                    last = nc.vector.tensor_tensor(dst[:, :, :, lo:lo + 16], t0, t1, op)
                    if lo == 0:
                        link(dve, last)
                last.then_inc(qk_roped, 1)
                dve.wait_ge(qk_roped, a + 1)
            dve.wait_ge(dt_ln, 1)
            dve.wait_ge(a_exp, 1)
            link(dve, nc.vector.scalar_tensor_tensor(dt, dt_x, 0.0, dt_l, ALU.max, ALU.add))
            for a in range(NT):
                op = nc.vector.scalar_tensor_tensor(adt[:, a, :], a_log[:, 0, :], -1.0, dt[:, a, :], ALU.mult, ALU.mult)
            op.then_inc(adt_ready, 1)
            for g in range(2):
                dve.wait_ge(cb_mm, g + 1)
                blocks = bank[g][:, :].rearrange("p (n l) -> p n l", l=P)
                for i, mask in ((0, "upto"), (2, "from")):
                    nc.vector.tensor_tensor(cb[g][:, i:i + 2, :], blocks[:, 0:4:3, :],
                                            spread(const(mask).unsqueeze(1), [P, 2, P]), ALU.mult)
                nc.vector.tensor_copy(cb[g][:, 4:6, :], blocks[:, 1:3, :]).then_inc(cb_in, 1)
            dve.wait_ge(qk_turned, 1)
            nc.vector.tensor_copy(buf(B_QT, 0, HALF), bank[6][:, :]).then_inc(qk_in, 1)
            nc.vector.tensor_copy(buf(B_QT, HALF, 2 * HALF), bank[7][:, :]).then_inc(qk_in, 1)
            nc.vector.tensor_copy(kgT, bank[0][:, 0:T]).then_inc(qk_in, 1)
            dve.wait_ge(xs_in, 4)
            nc.vector.tensor_tensor(toks(B_XB).rearrange("p a (h n) -> p a h n", n=N), toks(B_XS).rearrange("p a (h n) -> p a h n", n=N),
                                    spread(dt[:, :, H:2 * H].unsqueeze(3), [P, NT, H, N]), ALU.mult).then_inc(xd_b_ready, 1)

            def maxima(i):
                dve.wait_ge(g_s_mm, i + 1)
                link(dve, nc.vector.tensor_reduce(g_max[:, 2 * i:2 * i + 2], bank[i % 2][:, :].rearrange("p (a t) -> p a t", t=T),
                                                  AX, ALU.max))
                nc.vector.tensor_scalar(g_nmax[:, 2 * i:2 * i + 2], g_max[:, 2 * i:2 * i + 2], -GQA_SCALE, None,
                                        ALU.mult).then_inc(g_max_ready, 1)

            def normalize(i):
                dve.wait_ge(g_exp, i + 1)
                link(dve, nc.vector.reciprocal(g_inv[:, 2 * i:2 * i + 2], g_sum[:, 2 * i:2 * i + 2]))
                for a in range(NT):
                    p = gp_buf[i % 2][:, a * T:(a + 1) * T]
                    op = nc.vector.tensor_scalar(p, p, g_inv[:, 2 * i + a:2 * i + a + 1], None, ALU.mult)
                op.then_inc(g_p_ready, 1)

            for i in range(GH):
                maxima(i)
                if i >= 1:
                    normalize(i - 1)
            normalize(GH - 1)

            def left_sides(h):
                if h >= 2:
                    dve.wait_ge(seg_mm, h - 1)
                l = seg_lhs[h % 2]
                f, b = adt[:, :, h:h + 1], adt[:, :, H + h:H + h + 1]
                for n, (mask, c) in enumerate((("after", f[:, 0]), ("after", f[:, 1]), ("ones", f[:, 1]),
                                               ("before", b[:, 0]), ("before", b[:, 1]), ("ones", b[:, 0]))):
                    op = nc.vector.tensor_scalar(l[:, n, :], const(mask), c, None, ALU.mult)
                op.then_inc(lhs_ready, 1)

            def matrices(h):
                dve.wait_ge(e_ready, h + 1)
                nc.vector.tensor_tensor(e_buf[h % 2], e_buf[h % 2], buf(B_CB, (h // 8) * 768, (h // 8 + 1) * 768),
                                        ALU.mult).then_inc(m_ready, 1)

            dve.wait_ge(adt_ready, 1)
            left_sides(0)
            for h in range(H):
                if h + 1 < H:
                    left_sides(h + 1)
                matrices(h)
            dve.wait_ge(ssd_mm, H)
            dve.wait_ge(dx_ready, 1)
            y = toks(B_Y)
            for a in range(NT):
                for q in range(2):
                    cells = slice(q * HALF, (q + 1) * HALF)
                    op = nc.vector.tensor_tensor(y[:, a, cells], bank[4 + 2 * a + q][:, :], toks(B_DX)[:, a, cells], ALU.add)
                link(dve, op)
                nc.vector.tensor_tensor(y[:, a, :], y[:, a, :], toks(B_Z)[:, a, :], ALU.mult).then_inc(yz_ready, 1)
            dve.wait_ge(yg_sq, NT)
            nc.vector.tensor_scalar(yg_var, yg_ss, 1.0 / D, EPS, ALU.mult, ALU.add).then_inc(yg_var_ready, 1)
            after_slots(dve, "attn_proj")
            for j in range(4):
                nc.vector.tensor_tensor(buf(B_MIX, j * HALF, (j + 1) * HALF), bank[j][:, :], buf(B_GA, j * HALF, (j + 1) * HALF),
                                        ALU.mult).then_inc(attn_gated, 1)
            dve.wait_ge(yg_rstd_ready, 1)
            nc.vector.tensor_scalar(y[:, 1, :], y[:, 1, :], yg_rstd[:, 1:2], None, ALU.mult).then_inc(yn_v, 1)
            turn_dve(dve, TURN_SSD, 0, [(("ssd_norm_2", 0), B_SQ)])
            after_slots(dve, "ssd_proj")
            for j in range(4):
                op = nc.vector.tensor_tensor(buf(B_T2, j * HALF, (j + 1) * HALF), bank[4 + j][:, :], buf(B_GS, j * HALF, (j + 1) * HALF),
                                             ALU.mult)
            link(dve, op)
            dve.wait_ge(attn_gated, 4)
            nc.vector.tensor_tensor(buf(B_MIX), buf(B_MIX), buf(B_T2), ALU.add).then_inc(mix_ready, 1)
            turn_dve(dve, TURN_MIX, 0, [(None, B_T2)])

        def block_params_pool(pool):
            pool.wait_ge(x_updated, NT * 4)
            gain = qk_gain.rearrange("p (h n) -> p h n", n=N)
            pool.dma_start(gain[:, 0:GH, :], spread(A["q_norm_2"][0].partition_broadcast(P).unsqueeze(1), [P, GH, N])).then_inc(blk_params, 16)
            pool.dma_start(gain[:, GH:, :], spread(A["k_norm_2"][0].partition_broadcast(P).unsqueeze(1), [P, GKV, N])).then_inc(blk_params, 16)
            for dst, names in ((dt_bias, ("dt_bias_f_2", "dt_bias_b_2")), (a_log, ("a_log_f_2", "a_log_b_2"))):
                for i, name in enumerate(names):
                    pool.dma_start(dst[:, 0, i * H:(i + 1) * H], A[name][0].partition_broadcast(P)).then_inc(blk_params, 16)
            pool.dma_start(d_skip, A["d_skip_2"][0].partition_broadcast(P)).then_inc(blk_params, 16)

        def block_pool(pool):
            pool.wait_ge(qk_var_ready, 1)
            nc.gpsimd.tensor_tensor(qk_rstd, qk_var, minus_half[:, 0:NT * (GH + GKV)], ALU.pow).then_inc(qk_rstd_ready, 1)
            pool.wait_ge(adt_ready, 1)
            pool.wait_ge(xs_in, 4)
            xs = toks(B_XS).rearrange("p a (h n) -> p a h n", n=N)
            nc.gpsimd.tensor_tensor(toks(B_XF).rearrange("p a (h n) -> p a h n", n=N), xs,
                                    spread(dt[:, :, 0:H].unsqueeze(3), [P, NT, H, N]), ALU.mult).then_inc(xd_f_ready, 1)
            pool.wait_ge(blk_params, 16 * 7)
            pool.wait_ge(xd_b_ready, 1)
            nc.gpsimd.tensor_tensor(xs, xs, spread(d_skip.unsqueeze(1).unsqueeze(3), [P, NT, H, N]), ALU.mult).then_inc(dx_ready, 1)
            pool.wait_ge(yg_var_ready, 1)
            nc.gpsimd.tensor_tensor(yg_rstd, yg_var, minus_half[:, 0:NT], ALU.pow).then_inc(yg_rstd_ready, 1)

        def weights_sp(sp):
            def into(n, width=SLOT):
                if n >= RING:
                    sp.wait_ge(slot_done, n - RING + 1)
                return ring[:, n % RING, 0:width]

            def send(n, dst, src):
                sp.dma_start(dst, src).then_inc(landed[n % RING], 16)

            def rows_of(name, w, chunks):
                count = {k: c for k, c, _ in PLAN}[name]
                for s in range(count):
                    n = FIRST[name] + s
                    dst = into(n, chunks * w.shape[1]).rearrange("p (k n) -> p k n", k=chunks)
                    send(n, dst, w[s * chunks * P:(s + 1) * chunks * P, :].rearrange("(k p) n -> p k n", p=P))

            def columns_of(name, w, width):
                chunks = w.shape[0] // P
                for s in range({k: c for k, c, _ in PLAN}[name]):
                    n = FIRST[name] + s
                    dst = into(n, chunks * width).rearrange("p (k n) -> p k n", k=chunks)
                    send(n, dst, w[:, s * width:(s + 1) * width].rearrange("(k p) n -> p k n", p=P))

            def ffn(f, w_in, w_out):
                src = w_in.rearrange("(k p) (g n) -> p k g n", p=P, g=2)
                first = FIRST[f"ffn_in{f}"]

                def tile(it, j):
                    r = (first + j) % RING
                    sp.wait_ge(slot_done, it * RING + (first + j - RING + 1))
                    at = slice((it * RING + j) * P, (it * RING + j + 1) * P) if isinstance(it, int) else bass.ds(it * (RING * P) + j * P, P)
                    dst = ring[:, r, :].rearrange("p (k g n) -> p k g n", k=DC, g=2)
                    for g in range(2):
                        sp.dma_start(dst[:, :, g, :], src[:, :, g, at]).then_inc(landed[r], 16)

                rounds(sp, tile)
                rows_of(f"ffn_out{f}", w_out, 2)

            n = FIRST["lora_wa"]
            dst = into(n, 2 * DC * 64).rearrange("p (g k n) -> p g k n", g=2, k=DC)
            for g, w in enumerate(("a_w1", "a_a1")):
                send(n, dst[:, g], A[w][0].rearrange("(k p) n -> p k n", p=P))
            columns_of("w_k", A["a_w_rkv"][0, 1], T)
            n = FIRST["lora_wa2"]
            dst = into(n)
            for g, w in enumerate(("a_w2", "a_a2")):
                send(n, dst[0:64, g * D:(g + 1) * D], A[w][0])
            columns_of("lora_g", A["a_g1"][0], GATE_LORA)
            columns_of("w_r", A["a_w_rkv"][0, 0], T)
            n = FIRST["lora_g2"]
            dst = into(n)
            send(n, dst[:, 0:D], A["a_g2"][0, 0:P])
            send(n, dst[0:GATE_LORA - P, D:2 * D], A["a_g2"][0, P:GATE_LORA])
            rows_of("w_v", A["a_w_rkv"][0, 2], 2)
            rows_of("w_o", A["a_w_o"][0], 2)
            rwkv_blocks_sp(sp)
            ffn(0, A["ffn_w_in"][0], A["ffn_w_out"][0])
            rows_of("kv_down", A["kv_w_down"], 4)
            rows_of("q_down", A["q_w_down"][0], 4)
            columns_of("kv_up", A["kv_w_up"], D)
            columns_of("q_up", A["q_w_up"][0], 4 * QK)
            rows_of("o_w", A["o_w"][0], 2)
            ffn(1, A["ffn_w_in"][1], A["ffn_w_out"][1])
            w_in = A["w_in_2"][0]
            at_z = GH * N + 2 * GKV * N
            at_x = at_z + D
            at_dt = at_x + XC * P
            at_g = at_dt + 2 * H
            for s in range(2):
                n = FIRST["kvdt"] + s
                dst = into(n, 4 * 288).rearrange("p (k n) -> p k n", k=4)
                part = w_in[s * HALF:(s + 1) * HALF, :].rearrange("(k p) n -> p k n", p=P)
                send(n, dst[:, :, 0:2 * P], part[:, :, GH * N:at_z])
                send(n, dst[:, :, 2 * P:288], part[:, :, at_dt:at_g])
            columns_of("xbc", w_in[:, at_x:at_dt], T)
            rows_of("q", w_in[:, 0:GH * N], 4)
            rows_of("z", w_in[:, at_z:at_x], 2)
            for g in range(2):
                for s in range(4):
                    n = FIRST["gates"] + 4 * g + s
                    send(n, into(n).rearrange("p (k n) -> p k n", k=2),
                         w_in[s * T:(s + 1) * T, at_g + g * D:at_g + (g + 1) * D].rearrange("(k p) n -> p k n", p=P))
            proj = A["w_attn_proj_2"][0].rearrange("(g j d) n -> g d j n", g=GKV, j=GJ)
            for s in range(2):
                n = FIRST["attn_proj"] + s
                dst = into(n).rearrange("p (k n) -> p k n", k=2)
                for g in range(GKV):
                    send(n, dst[g * N:(g + 1) * N], proj[g, :, 2 * s:2 * s + 2, :])
            rows_of("ssd_proj", A["w_ssd_proj_2"][0], 2)
            rows_of("w_out", A["w_out_2"][0], 2)
            ffn(2, A["w_gate_up_2"][0], A["w_down_2"][0])

        block = ctx.enter_context(nc.Block())

        @block.sync
        def _(sp):
            weights_sp(sp)
            sp.wait_ge(x_updated, NT * 6)
            for a in range(NT):
                sp.dma_start(out[0, a * P:(a + 1) * P, :], x_sb[:, a, :]).then_inc(out_stored, 16)
            sp.wait_ge(out_stored, 16 * NT)

        @block.gpsimd
        def _(pool):
            start_pool(pool)
            pre_norm_pool(pool, 0)
            pool.wait_ge(const_landed, 16)
            rwkv_pool(pool)
            post_norm_pool(pool, 0)
            pre_norm_pool(pool, 1)
            load_gain(pool, 2, A["norm_g"][1, 1])
            post_norm_pool(pool, 1)
            pre_norm_pool(pool, 2)
            load_gain(pool, 3, A["norm_g"][1, 3])
            mla_pool(pool)
            post_norm_pool(pool, 2)
            pre_norm_pool(pool, 3)
            load_gain(pool, 4, A["norm1_post_2"][0])
            post_norm_pool(pool, 3)
            pre_norm_pool(pool, 4)
            block_params_pool(pool)
            load_gain(pool, 5, A["norm2_post_2"][0])
            block_pool(pool)
            post_norm_pool(pool, 4)
            pre_norm_pool(pool, 5)
            post_norm_pool(pool, 5)

        @block.tensor
        def _(pe):
            start_pe(pe)
            pre_norm_pe(pe, 0)
            rwkv_pe(pe)
            pre_norm_pe(pe, 1)
            ffn_pe(pe, 0, TURN_PRE1)
            pre_norm_pe(pe, 2)
            mla_pe(pe)
            pre_norm_pe(pe, 3)
            ffn_pe(pe, 1, TURN_PRE3)
            pre_norm_pe(pe, 4)
            block_pe(pe)
            pre_norm_pe(pe, 5)
            ffn_pe(pe, 2, TURN_PRE5)

        @block.scalar
        def _(act):
            start_act(act)
            act.wait_ge(cols_ready, 1)
            pre_norm_act(act, 0, [(("norm_g", 0 * DC), W_HT)])
            rwkv_act(act)
            post_norm_act(act, 0, lambda e: after_slots(e, "w_o"))
            pre_norm_act(act, 1, [(("norm_g", 2 * DC), FFN_H)])
            ffn_act(act, 0)
            post_norm_act(act, 1, ffn_ready(0))
            pre_norm_act(act, 2, [(("norm_g", 4 * DC), M_H), (("kv_norm_g", 0), M_XKV)])
            mla_act(act)
            post_norm_act(act, 2, lambda e: after_slots(e, "o_w"))
            pre_norm_act(act, 3, [(("norm_g", 6 * DC), FFN_H)])
            ffn_act(act, 1)
            post_norm_act(act, 3, ffn_ready(1))
            pre_norm_act(act, 4, [(("norm1_pre_2", 0), B_H)])
            block_act(act)
            post_norm_act(act, 4, lambda e: after_slots(e, "w_out"))
            pre_norm_act(act, 5, [(("norm2_pre_2", 0), FFN_H)])
            ffn_act(act, 2)
            post_norm_act(act, 5, ffn_ready(2))

        @block.vector
        def _(dve):
            start_dve(dve)
            dve.wait_ge(cols_ready, 1)
            pre_norm_dve(dve, 0, [(("norm_g", 0 * DC), W_HT)])
            rwkv_dve(dve)
            post_norm_dve(dve, 0)
            pre_norm_dve(dve, 1, [(("norm_g", 2 * DC), FFN_H)])
            ffn_dve(dve, 0)
            post_norm_dve(dve, 1)
            pre_norm_dve(dve, 2, [(("norm_g", 4 * DC), M_H), (("kv_norm_g", 0), M_XKV)])
            mla_dve(dve)
            post_norm_dve(dve, 2)
            pre_norm_dve(dve, 3, [(("norm_g", 6 * DC), FFN_H)])
            ffn_dve(dve, 1)
            post_norm_dve(dve, 3)
            pre_norm_dve(dve, 4, [(("norm1_pre_2", 0), B_H)])
            block_dve(dve)
            post_norm_dve(dve, 4)
            pre_norm_dve(dve, 5, [(("norm2_pre_2", 0), FFN_H)])
            ffn_dve(dve, 2)
            post_norm_dve(dve, 5)


INPUTS = ["x", "norm_g", "ffn_w_in", "ffn_conv_w", "ffn_conv_b", "ffn_w_out", "a_mu", "a_w_rkv", "a_w0", "a_w1", "a_w2",
          "a_a0", "a_a1", "a_a2", "a_g1", "a_g2", "a_k_k", "a_k_a", "a_r_k", "a_lnx_w", "a_lnx_b", "a_w_o", "kv_norm_g",
          "kv_w_down", "kv_a_norm_g", "kv_w_up", "q_w_down", "q_norm_g", "q_w_up", "o_w", "w_in_2", "q_norm_2", "k_norm_2",
          "conv_w_2", "conv_b_2", "dt_bias_f_2", "dt_bias_b_2", "a_log_f_2", "a_log_b_2", "d_skip_2", "ssd_norm_2",
          "w_attn_proj_2", "w_ssd_proj_2", "w_out_2", "norm1_pre_2", "norm1_post_2", "norm2_pre_2", "norm2_post_2",
          "w_gate_up_2", "w_down_2"]


def kernel(**inputs):
    import concourse.bacc as bacc
    from concourse.bass_utils import run_bass_kernel_spmd

    nc = bacc.Bacc("TRN2", target_bir_lowering=False, num_devices=1)
    arrays, args = {}, {}
    for name in INPUTS:
        a = np.ascontiguousarray(inputs[name])
        arrays[f"in_{name}"] = a
        args[name] = nc.dram_tensor(f"in_{name}", a.shape, mybir.dt.from_np(a.dtype), kind="ExternalInput").ap()
    arrays["constants"] = np.ascontiguousarray(np.concatenate(list(CONSTANTS.values()), axis=1))
    const_dram = nc.dram_tensor("constants", (P, CONST_W), F32, kind="ExternalInput").ap()
    out = nc.dram_tensor("out", (1, T, D), F32, kind="ExternalOutput").ap()
    build(nc, args, const_dram, out)
    r = run_bass_kernel_spmd(nc, [arrays], core_ids=[0])
    return r.results[0]["out"]
```

```python
from contextlib import ExitStack

import numpy as np

import concourse.bass as bass
from concourse import mybir

F32 = mybir.dt.float32
F32R = mybir.dt.float32r
ALU = mybir.AluOpType
ACT = mybir.ActivationFunctionType
AX = mybir.AxisListType.X

P = 128
T = 256
NT = T // P
D = 1024
DC = D // P
HALF = 512
F = 2816
FC = F // P
H = 16
N = 64
HP = H // 2
NOPE, ROPE = 64, 32
QK = NOPE + ROPE
Q_LORA, KV_LORA = 384, 256
GATE_LORA = 160
GH, GKV, GJ = 8, 2, 4
XC = 12
EPS = 1e-6
LNX_EPS = 64e-5
KAPPA = float(np.exp(-0.5))
BS = 32
NB = P // BS
MLA_SCALE = float(QK) ** -0.5
GQA_SCALE = float(N) ** -0.5
NEG = -1e30

RING = 4
SLOT = 2048
ARENA = [(0, 4), (4, 5), (9, 4), (13, 5)]

PLAN = [("lora_wa", 1, 2), ("w_k", 4, 1), ("lora_wa2", 1, 2), ("w_r", 4, 1), ("lora_g", 1, 1), ("lora_g2", 1, 2),
        ("w_v", 4, 1), ("w_o", 4, 1), ("ffn_in0", FC, 2), ("ffn_out0", FC // 2, 2),
        ("kv_down", 2, 1), ("q_down", 2, 1), ("kv_up", 2, 1), ("q_up", 4, 1), ("o_w", 4, 1),
        ("ffn_in1", FC, 2), ("ffn_out1", FC // 2, 2),
        ("kvdt", 2, 2), ("xbc", 6, 1), ("q", 2, 1), ("z", 4, 1), ("gates", 8, 1),
        ("attn_proj", 2, 2), ("ssd_proj", 4, 1), ("w_out", 4, 1), ("ffn_in2", FC, 2), ("ffn_out2", FC // 2, 2)]
WIDTH = {"kv_down": 4 * 288, "q_down": 4 * Q_LORA, "q_up": 12 * QK, "kvdt": 4 * 288}
FIRST = {}
LANDED = []
SLOT_WIDTH = []
_count = [0] * RING
for _name, _n, _dmas in PLAN:
    FIRST[_name] = len(LANDED)
    for _ in range(_n):
        _r = len(LANDED) % RING
        _count[_r] += 16 * _dmas
        LANDED.append(_count[_r])
        SLOT_WIDTH.append(WIDTH.get(_name, SLOT))
LAST = {_name: FIRST[_name] + _n - 1 for _name, _n, _ in PLAN}
SPLIT0 = FIRST["ffn_in0"]
AHEAD = RING - 1

ROW_TILES = [[("norm_g", 64), ("a_mu", 48), ("a_w0", 8), ("a_a0", 8)],
             [("a_k_k", 8), ("a_k_a", 8), ("a_r_k", 8), ("kv_norm_g", 8), ("kv_a_norm_g", 2), ("q_norm_g", 3),
              ("norm1_pre_2", 8), ("norm2_pre_2", 8), ("ssd_norm_2", 8), ("conv_w_2", 60)],
             [("conv_b_2", 12), ("ffn_conv_w0", 66), ("ffn_conv_b", 44)],
             [("ffn_conv_w1", 66)]]
COL = {}
for _q, _tile in enumerate(ROW_TILES):
    _at = 0
    for _name, _n in _tile:
        COL[_name] = _q * P + _at
        _at += _n
PARAM_DMAS = sum(len(t) for t in ROW_TILES)


def constants():
    s, t = np.arange(P)[:, None], np.arange(P)[None, :]
    tok = np.arange(T, dtype=np.float32)
    inv = (1.0 / (10000.0 ** (np.arange(0, ROPE, 2, dtype=np.float32) / ROPE))).astype(np.float32)
    ang = tok[:, None] * inv[None, :]
    c, sn = np.cos(ang), np.sin(ang)
    perm = np.zeros((P, QK))
    cosT, sinT = np.zeros((P, T)), np.zeros((P, T))
    half = ROPE // 2
    for i in range(half):
        perm[NOPE + half + i, NOPE + i] = 1
        perm[NOPE + i, NOPE + half + i] = 1
        cosT[NOPE + i] = cosT[NOPE + half + i] = c[:, i]
        sinT[NOPE + i], sinT[NOPE + half + i] = -sn[:, i], sn[:, i]
    ktok = lambda a: a.reshape(NT, P, half).transpose(1, 0, 2).reshape(P, -1)
    maskb = np.where((t // 64) <= (s // 64), 0.0, NEG)
    inv2 = (10000.0 ** (-np.arange(0, 32, 2, dtype=np.float32) / 32)).astype(np.float32)
    a2 = np.stack([(tok // 64)[:, None] * inv2, (tok % 64)[:, None] * inv2], 1)
    axial = lambda a: a.reshape(NT, P, 32).transpose(1, 0, 2).reshape(P, -1)
    return {
        "ident": s == t, "before": s < t, "upto": s <= t, "after": s > t, "from": s >= t,
        "off": (s < t) & (s // BS != t // BS), "ones": np.ones((P, P)),
        "head_of": s // N == np.arange(2)[None, :], "perm": perm, "cosT": cosT, "sinT": sinT,
        "kcos": ktok(c), "ksin": ktok(sn), "maskb": np.concatenate([maskb, 0 * maskb, maskb], 1),
        "acos": axial(np.cos(a2)), "asin": axial(np.sin(a2)),
    }


CONSTANTS = {k: np.asarray(v, np.float32) for k, v in constants().items()}
CONST_AT, _at = {}, 0
for _k, _v in CONSTANTS.items():
    CONST_AT[_k] = _at
    _at += _v.shape[1]
CONST_W = _at


def build(nc, A, const_dram, out):
    with ExitStack() as ctx:
        def sb(name, shape, dtype=F32, stack=ctx):
            return stack.enter_context(nc.sbuf_tensor(name, shape, dtype))

        def sem(name):
            return ctx.enter_context(nc.semaphore(name))

        with ExitStack() as first:
            ring = sb("ring", [P, RING, SLOT], F32, first)
            arena = [sb(f"arena{i}", [P, n, SLOT], F32, first) for i, n in ARENA]
        ring12 = sb("ring12", [P, RING, SLOT], F32R)
        arena12 = [sb(f"arena12_{i}", [P, n, SLOT], F32R) for i, n in ARENA]
        x_sb = sb("x_sb", [P, NT, D])
        cst = sb("cst", [P, CONST_W])
        cols = sb("cols", [P, 4 * P])
        gpost, gpre = sb("gpost", [P, D]), sb("gpre", [P, D])
        unread = sb("unread", [P, 2, HALF], mybir.dt.bfloat16)
        stat = sb("stat", [P, 704])
        bank = [ctx.enter_context(nc.psum_tensor(f"bank{i}", [P, HALF], F32)) for i in range(8)]

        stat_used = [0]

        def small(n):
            stat_used[0] += n
            assert stat_used[0] <= 704
            return stat[:, stat_used[0] - n:stat_used[0]]

        def const(name, lo=0, hi=None):
            w = CONSTANTS[name].shape[1]
            return cst[:, CONST_AT[name] + lo:CONST_AT[name] + (w if hi is None else hi)]

        def col(name, i):
            return cols[:, COL[name] + i:COL[name] + i + 1]

        def bufs(i, n, mem=arena):
            tensor = [m for m, (first, count) in zip(mem, ARENA) if first <= i < first + count][0]
            at = [i - first for first, count in ARENA if first <= i < first + count][0]
            return tensor[:, at:at + n, :].rearrange("p b s -> p (b s)")

        def buf(i, lo=0, hi=SLOT, mem=arena):
            return bufs(i, 1, mem)[:, lo:hi]

        def chan(i, mem=arena):
            return buf(i, mem=mem).rearrange("p (c t) -> p c t", t=T)

        def toks(i):
            return buf(i).rearrange("p (a d) -> p a d", a=NT)

        def heads(i):
            return buf(i).rearrange("p (h t) -> p h t", t=P)

        def spread(ap, shape):
            return ap.broadcast_to(shape)

        ident = const("ident")
        po_ss, po_var, po_rstd, pr_ss, pr_var, pr_rstd = (small(n) for n in (4, 2, 2, 4, 2, 2))
        minus_half = small(32)

        landed = [sem(f"landed{r}") for r in range(RING)]
        slot_done = sem("slot_done")
        hi_ready, split_ready = sem("hi_ready"), sem("split_ready")
        x_landed = [sem("x_landed0"), sem("x_landed1")]
        const_landed, rows_zeroed, rows_landed = (sem(n) for n in ("const_landed", "rows_zeroed", "rows_landed"))
        cols_turned, cols_ready, consts_set = sem("cols_turned"), sem("cols_ready"), sem("consts_set")
        gpost_landed, gpre_landed, kv_gain_landed = (sem(n) for n in ("gpost_landed", "gpre_landed", "kv_gain_landed"))
        x_updated, out_stored = sem("x_updated"), sem("out_stored")
        dve_step = sem("dve_step")
        rows_done, post_mul, post_ss, post_var, post_rstd, pre_ss, pre_var, pre_rstd, xn_ready = (
            sem(n) for n in ("rows_done", "post_mul", "post_ss", "post_var", "post_rstd", "pre_ss", "pre_var", "pre_rstd",
                             "xn_ready"))
        squared, var_ready, rstd_ready = (sem(n) for n in ("squared", "var_ready", "rstd_ready"))
        turned, turn_a, turn_v = sem("turned"), sem("turn_a"), sem("turn_v")
        conv_step, act_done, ffn_prod, ffn_hi, ffn_done = (
            sem(n) for n in ("conv_step", "ffn_act_done", "ffn_prod", "ffn_hi", "ffn_done"))

        TURN_PRE0, TURN_PRE1, TURN_XKV, TURN_PRE2, TURN_PRE3, TURN_PRE4, TURN_SSD, TURN_MIX, TURN_PRE5 = range(9)

        def half_turns(turn, a):
            if turn in (TURN_XKV, TURN_PRE2):
                return 2 * TURN_XKV + 2 * a + (turn == TURN_PRE2)
            return 2 * turn + a

        HI = 13
        XN = TMP = 17
        XN_KV, GAIN_KV = 9, 12
        MEAN = D ** -0.5

        def after_slots(eng, name, n=None):
            eng.wait_ge(slot_done, LAST[name] + 1 if n is None else FIRST[name] + n)

        def weights(pe, n):
            pe.wait_ge(landed[n % RING], LANDED[n])
            return ring[:, n % RING, :]

        def split_weights(pe, n):
            pe.wait_ge(split_ready, n - SPLIT0 + 1)
            return buf(HI + n % RING, mem=arena12), ring12[:, n % RING, :]

        def product(dst, stationary, moving, start, stop):
            nc.tensor.matmul(dst, stationary[0], moving[0], start=start, stop=False)
            nc.tensor.matmul(dst, stationary[0], moving[1], start=False, stop=False)
            return nc.tensor.matmul(dst, stationary[1], moving[0], start=False, stop=stop)

        def both(views, *at):
            return tuple(v[at] for v in views)

        def chan2(hi, lo):
            return chan(hi, arena12), chan(lo, arena12)

        def wide2(pe, first, nslots, act2, base, turn=None, before=None, rows=False, told=None):
            def part(s, w, a):
                for kk in range(2):
                    k = 2 * s + kk
                    if turn is not None and k % 4 == 0:
                        turned_out(pe, turn, a, k // 4)
                    x = both(act2, slice(None), k, slice(a * P, (a + 1) * P))
                    for half in range(2):
                        at = slice(kk * D + half * HALF, kk * D + (half + 1) * HALF)
                        mm = product(bank[base + 2 * a + half][:, :], x, both(w, slice(None), at), k == 0, k == 2 * nslots - 1)
                return mm

            groups = [(s,) for s in range(nslots)]
            if turn is not None:
                groups = [(s, s + 1) for s in range(0, nslots, 2)]
            elif rows:
                groups[-2:] = [(nslots - 2, nslots - 1)]
            for group in groups:
                for a in range(NT):
                    if before is not None and group[0] == 0:
                        before(a)
                    for s in group:
                        mm = part(s, split_weights(pe, first + s), a)
                        if a == NT - 1:
                            mm.then_inc(slot_done, 1)
                    if a == 0 and group[-1] == nslots - 1 and (rows or told is not None):
                        mm.then_inc(rows_done if rows else told, 1)

        def turn_pe(src, base, a):
            for q in range(2):
                for c in range(4 * q, 4 * q + 4):
                    mm = nc.tensor.transpose(bank[base + 2 * a + q][:, c % 4 * P:(c % 4 + 1) * P], src[:, c * P:(c + 1) * P], ident)
                mm.then_inc(turned, 1)

        def xn_turn(pe, n, a, xn=XN, base=4):
            pe.wait_ge(xn_ready, n + 1)
            turn_pe(toks(xn)[:, a, :], base, a)

        def turned_out(eng, turn, a=NT - 1, q=1):
            eng.wait_ge(turn_v, half_turns(turn, a) * 2 + q + 1)
            if turn == TURN_PRE0:
                eng.wait_ge(turn_a, half_turns(turn, a) * 2 + q + 1)

        emitted = {}

        def ahead(eng, last, split):
            for n in range(emitted.get(eng, SPLIT0), last + 1):
                split(eng, n)
            emitted[eng] = max(emitted.get(eng, SPLIT0), last + 1)

        def split_act(act, n, rounds_on=0):
            r, w = n % RING, SLOT_WIDTH[n]
            act.wait_ge(landed[r], LANDED[n] + rounds_on * 32)
            nc.scalar.activation(buf(HI + r, 0, w, arena12), ring[:, r, 0:w], ACT.Copy).then_inc(hi_ready, 1)

        def split_lo(eng, on, n, rounds_on=0):
            r, w = n % RING, SLOT_WIDTH[n]
            eng.wait_ge(hi_ready, n - SPLIT0 + 1 + rounds_on * RING)
            on.tensor_tensor(ring12[:, r, 0:w], ring[:, r, 0:w], buf(HI + r, 0, w, arena12).bitcast(F32),
                             ALU.subtract).then_inc(split_ready, 1)

        def split_dve(dve, n, rounds_on=0):
            split_lo(dve, nc.vector, n, rounds_on)

        def turn_act(act, turn, a, base, hi):
            whole = turn == TURN_PRE0
            for q in range(1 if whole else 2):
                act.wait_ge(turned, half_turns(turn, a) * 2 + q + 1)
                nc.scalar.activation(chan(hi, arena if whole else arena12)[:, 4 * q:4 * q + 4, a * P:(a + 1) * P],
                                     bank[base + 2 * a + q][:, :].rearrange("p (c t) -> p c t", t=P),
                                     ACT.Copy).then_inc(turn_a, 2 if whole else 1)

        def turn_dve(dve, turn, a, base, hi, lo=None):
            for q in range(2) if lo is not None else (1,):
                src = bank[base + 2 * a + q][:, :].rearrange("p (c t) -> p c t", t=P)
                at = (slice(None), slice(4 * q, 4 * q + 4), slice(a * P, (a + 1) * P))
                if lo is None:
                    dve.wait_ge(turned, half_turns(turn, a) * 2 + q + 1)
                    nc.vector.tensor_copy(chan(hi)[at], src).then_inc(turn_v, 2)
                else:
                    dve.wait_ge(turn_a, half_turns(turn, a) * 2 + q + 1)
                    nc.vector.tensor_tensor(chan(lo, arena12)[at], src, chan(hi, arena12)[at].bitcast(F32),
                                            ALU.subtract).then_inc(turn_v, 1)

        steps = [0]

        def step(ins):
            steps[0] += 1
            ins.then_inc(dve_step, 1)
            return steps[0]

        def link(dve, ins):
            dve.wait_ge(dve_step, step(ins))

        POST = ["w_o", "ffn_out0", "o_w", "ffn_out1", "w_out", "ffn_out2"]

        def rows_ready(eng, i, a):
            if a == 0:
                eng.wait_ge(rows_done, i + 1)
            else:
                after_slots(eng, POST[i])

        def post_squares(act, i, a):
            rows_ready(act, i, a)
            if i == len(POST) - 1 and a == 1:
                act.wait_ge(post_ss, 4 * i + 2)
            else:
                act.wait_ge(pre_ss, 4 * i + 2 * a + 4)
            nc.scalar.activation(unread[:, 0, :], bank[4 + 2 * a][:, :], ACT.Square, scale=MEAN,
                                 accum_out=po_ss[:, 2 * a:2 * a + 1]).then_inc(post_ss, 1)
            act.wait_ge(post_mul, 4 * i + 2 * a + 1)
            nc.scalar.activation(unread[:, 1, :], bank[5 + 2 * a][:, :], ACT.Square, scale=MEAN,
                                 accum_out=po_ss[:, 2 * a + 1:2 * a + 2]).then_inc(post_ss, 1)

        def post_scale(dve, i, a):
            tmp = toks(TMP)[:, a, :]
            dve.wait_ge(gpost_landed, 16 * (i + 1))
            rows_ready(dve, i, a)
            nc.vector.tensor_tensor(tmp[:, HALF:D], bank[5 + 2 * a][:, :], gpost[:, HALF:D], ALU.mult).then_inc(post_mul, 1)
            dve.wait_ge(post_ss, 4 * i + 2 * a + 1)
            nc.vector.tensor_tensor(tmp[:, 0:HALF], bank[4 + 2 * a][:, :], gpost[:, 0:HALF], ALU.mult).then_inc(post_mul, 1)
            dve.wait_ge(post_ss, 4 * i + 2 * a + 2)
            nc.vector.scalar_tensor_tensor(po_var[:, a:a + 1], po_ss[:, 2 * a:2 * a + 1], EPS, po_ss[:, 2 * a + 1:2 * a + 2],
                                           ALU.add, ALU.add).then_inc(post_var, 1)

        def post_root(pool, i, a):
            pool.wait_ge(post_var, NT * i + a + 1)
            nc.gpsimd.tensor_tensor(po_rstd[:, a:a + 1], po_var[:, a:a + 1], minus_half[:, 0:1], ALU.pow).then_inc(post_rstd, 1)

        def x_update(dve, i, a):
            dve.wait_ge(post_mul, 4 * i + 2 * a + 2)
            dve.wait_ge(post_rstd, NT * i + a + 1)
            for half in range(2):
                at = slice(half * HALF, (half + 1) * HALF)
                nc.vector.scalar_tensor_tensor(x_sb[:, a, at], toks(TMP)[:, a, at], po_rstd[:, a:a + 1], x_sb[:, a, at],
                                               ALU.mult, ALU.add).then_inc(x_updated, 1)

        def x_squares(act, i, a):
            for half in range(2):
                if i == 0:
                    act.wait_ge(x_landed[a], 16)
                else:
                    act.wait_ge(x_updated, 4 * (i - 1) + 2 * a + half + 1)
                if i or a:
                    act.wait_ge(pre_ss, 4 * i + 2 * a + half - 1)
                nc.scalar.activation(unread[:, half, :], x_sb[:, a, half * HALF:(half + 1) * HALF], ACT.Square, scale=MEAN,
                                     accum_out=pr_ss[:, 2 * a + half:2 * a + half + 1]).then_inc(pre_ss, 1)

        def pre_mean(dve, i, a):
            dve.wait_ge(pre_ss, 4 * i + 2 * a + 2)
            nc.vector.scalar_tensor_tensor(pr_var[:, a:a + 1], pr_ss[:, 2 * a:2 * a + 1], EPS, pr_ss[:, 2 * a + 1:2 * a + 2],
                                           ALU.add, ALU.add).then_inc(pre_var, 1)

        def pre_root(pool, i, a):
            pool.wait_ge(pre_var, NT * i + a + 1)
            nc.gpsimd.tensor_tensor(pr_rstd[:, a:a + 1], pr_var[:, a:a + 1], minus_half[:, 0:1], ALU.pow).then_inc(pre_rstd, 1)

        def x_scaled(dve, i, a, gain=None, dst=XN):
            dve.wait_ge(pre_rstd, NT * i + a + 1)
            if gain is None:
                gain = gpre[:, :]
                dve.wait_ge(gpre_landed, 16 * (i + 1))
            else:
                dve.wait_ge(kv_gain_landed, 16)
            nc.vector.scalar_tensor_tensor(toks(dst)[:, a, :], x_sb[:, a, :], pr_rstd[:, a:a + 1], gain,
                                           ALU.mult, ALU.mult).then_inc(xn_ready, 1)

        XN_OF = [0, 2, 4, 8, 10, 12, 14]

        def between_act(act, i, turns, last):
            ahead(act, last + 1, split_act)
            post_squares(act, i, 0)
            ahead(act, last + 2, split_act)
            x_squares(act, i + 1, 0)
            post_squares(act, i, 1)
            if len(turns) > 1:
                ahead(act, last + 4, split_act)
            for turn, base, hi, lo, gain, xn in turns:
                turn_act(act, turn, 0, base, hi)
            x_squares(act, i + 1, 1)
            for turn, base, hi, lo, gain, xn in turns:
                turn_act(act, turn, 1, base, hi)

        def between_dve(dve, i, turns, last):
            ahead(dve, last + 1, split_dve)
            post_scale(dve, i, 0)
            x_update(dve, i, 0)
            pre_mean(dve, i + 1, 0)
            post_scale(dve, i, 1)
            for turn, base, hi, lo, gain, xn in turns:
                x_scaled(dve, i + 1, 0, gain, xn)
            x_update(dve, i, 1)
            for turn, base, hi, lo, gain, xn in turns:
                turn_dve(dve, turn, 0, base, hi, lo)
            pre_mean(dve, i + 1, 1)
            if len(turns) > 1:
                ahead(dve, last + 4, split_dve)
            for turn, base, hi, lo, gain, xn in turns:
                x_scaled(dve, i + 1, 1, gain, xn)
            for turn, base, hi, lo, gain, xn in turns:
                turn_dve(dve, turn, 1, base, hi, lo)

        def between_pool(pool, i):
            for a in range(NT):
                post_root(pool, i, a)
                pre_root(pool, i + 1, a)

        def load_gains(pool, i, post, pre):
            pool.wait_ge(xn_ready, XN_OF[i + 1])
            if i > 0:
                pool.wait_ge(post_mul, 4 * i)
            if pre is not None:
                pool.dma_start(gpre[:, :], pre.partition_broadcast(P)).then_inc(gpre_landed, 16)
            pool.dma_start(gpost[:, :], post.partition_broadcast(P)).then_inc(gpost_landed, 16)

        FFN_H, FFN_H_LO, FFN_F, FFN_F_LO, FFN_CONV, FFN_P = 0, 5, 1, 6, 4, 9
        fT_hi, fT_lo = (bufs(i, 3, arena12) for i in (FFN_F, FFN_F_LO))
        conv_acc = [buf(FFN_CONV, j * T, (j + 1) * T) for j in range(RING)]
        gate_act = [buf(FFN_CONV, (RING + j) * T, (RING + j + 1) * T) for j in range(RING)]
        gated = [buf(FFN_P, j * T, (j + 1) * T) for j in range(RING)]
        LOOPS = FC // RING

        def rounds(eng, tile):
            for j in range(RING):
                tile(0, j)
            with eng.Fori(1, LOOPS) as it:
                for j in range(RING):
                    tile(it, j)
            for j in range(FC - LOOPS * RING):
                tile(LOOPS, j)

        def tile_cells(whole, it, j):
            if isinstance(it, int):
                return whole[:, (it * RING + j) * T:(it * RING + j + 1) * T]
            return whole[:, bass.ds(it * (RING * T) + j * T, T)]

        def ffn_pe(pe, f, i, turn):
            first = FIRST[f"ffn_in{f}"]
            h2 = chan2(FFN_H, FFN_H_LO)

            for a in range(NT):
                xn_turn(pe, XN_OF[i] + a, a)

            def tile(it, j):
                r = (first + j) % RING
                pe.wait_ge(split_ready, first + j - SPLIT0 + 1 + it * RING)
                if not (isinstance(it, int) and it == 0):
                    pe.wait_ge(ffn_prod, f * FC + it * RING + (j - RING + 1))
                w = [v.rearrange("p (k g n) -> p k g n", k=DC, g=2) for v in (buf(HI + r, mem=arena12), ring12[:, r, :])]
                for g in range(2):
                    for k in range(DC):
                        if isinstance(it, int) and it == j == g == 0 and k % 4 == 0:
                            turned_out(pe, turn, 0, k // 4)
                            turned_out(pe, turn, 1, k // 4)
                        mm = product(bank[j][:, g * T:(g + 1) * T], both(w, slice(None), k, g), both(h2, slice(None), k),
                                     k == 0, k == DC - 1)
                mm.then_inc(slot_done, 1)

            rounds(pe, tile)

            def rows(k, a):
                w = split_weights(pe, FIRST[f"ffn_out{f}"] + k // 2)
                pe.wait_ge(ffn_done, f * FC + k + 1)
                at = slice(k * T + a * P, k * T + (a + 1) * P)
                for half in range(2):
                    cells = slice((k % 2) * D + half * HALF, (k % 2) * D + (half + 1) * HALF)
                    mm = product(bank[4 + 2 * a + half][:, :], (fT_hi[:, at], fT_lo[:, at]), both(w, slice(None), cells),
                                 k == 0, k == FC - 1)
                return mm

            for k in range(FC - 4):
                for a in range(NT):
                    mm = rows(k, a)
                if k % 2 == 1:
                    mm.then_inc(slot_done, 1)
            for a in range(NT):
                for k in range(FC - 4, FC):
                    mm = rows(k, a)
                    if a == NT - 1 and k % 2 == 1:
                        mm.then_inc(slot_done, 1)
                if a == 0:
                    mm.then_inc(rows_done, 1)

        def ffn_act(act, f):
            first = FIRST[f"ffn_in{f}"]

            def tile(it, j):
                split_act(act, first + AHEAD + j, it)
                if f < 2:
                    act.wait_ge(conv_step, 3 * f * FC + it * (3 * RING) + 3 * (j + 1))
                    nc.scalar.activation(gate_act[j], conv_acc[j], ACT.Gelu_apprx_tanh).then_inc(act_done, 1)
                else:
                    act.wait_ge(slot_done, first + it * RING + (j + 1))
                    nc.scalar.activation(gate_act[j], bank[j][:, 0:T], ACT.Silu).then_inc(act_done, 1)

            ahead(act, first + AHEAD - 1, split_act)
            rounds(act, tile)
            emitted[act] = first + FC + AHEAD

        def ffn_dve(dve, f):
            first = FIRST[f"ffn_in{f}"]

            def at(it, j, name):
                if isinstance(it, int):
                    return col(name[0], name[1] + it * RING + j)
                return cols[:, bass.ds(it * RING + (COL[name[0]] + name[1] + j), 1)]

            def tile(it, j):
                gate, up = bank[j][:, 0:T], bank[j][:, T:2 * T]
                if f < 2:
                    tap = [(f"ffn_conv_w{f}", i * FC) for i in range(3)]
                    dve.wait_ge(slot_done, first + it * RING + (j + 1))
                    nc.vector.tensor_scalar(conv_acc[j], gate, at(it, j, tap[2]), at(it, j, ("ffn_conv_b", f * FC)),
                                            ALU.mult, ALU.add).then_inc(conv_step, 1)
                    for i in (1, 0):
                        back = 2 - i
                        dve.wait_ge(conv_step, 3 * f * FC + it * (3 * RING) + 3 * j + back)
                        nc.vector.scalar_tensor_tensor(conv_acc[j][:, back:T], gate[:, 0:T - back], at(it, j, tap[i]),
                                                       conv_acc[j][:, back:T], ALU.mult, ALU.add).then_inc(conv_step, 1)
                split_dve(dve, first + AHEAD + j, it)
                dve.wait_ge(act_done, f * FC + it * RING + (j + 1))
                if not (isinstance(it, int) and it == 0):
                    dve.wait_ge(ffn_done, f * FC + it * RING + (j - RING + 1))
                nc.vector.tensor_tensor(gated[j], gate_act[j], up, ALU.mult).then_inc(ffn_prod, 1)

            ahead(dve, first + AHEAD - 1, split_dve)
            rounds(dve, tile)
            emitted[dve] = first + FC + AHEAD

        def ffn_pool(pool, f):
            def tile(it, j):
                pool.wait_ge(ffn_prod, f * FC + it * RING + (j + 1))
                nc.gpsimd.tensor_copy(tile_cells(fT_hi, it, j), gated[j]).then_inc(ffn_hi, 1)
                pool.wait_ge(ffn_hi, f * FC + it * RING + (j + 1))
                nc.gpsimd.tensor_tensor(tile_cells(fT_lo, it, j), gated[j], tile_cells(fT_hi, it, j).bitcast(F32),
                                        ALU.subtract).then_inc(ffn_done, 1)

            rounds(pool, tile)

        ROWS = 15
        rows = buf(ROWS, 0, 4 * P).rearrange("p (q n) -> p q n", n=P)

        def row_view(name):
            if name[-1] in "01" and name.startswith("ffn_conv_w"):
                return A["ffn_conv_w"][int(name[-1])].rearrange("j (c p) -> (j c) p", p=P)
            a = A[name]
            if name == "a_r_k":
                return a.rearrange("o (c g) n -> (o c) (g n)", g=2)
            if len(a.shape) == 1:
                return a.rearrange("(c p) -> c p", p=P)
            if len(a.shape) == 2:
                return a.rearrange("o (c p) -> (o c) p", p=P)
            return a.rearrange("o j (c p) -> (o j c) p", p=P)

        def start_act(act):
            for a in range(NT):
                act.dma_start(x_sb[:, a, :], A["x"][0, a * P:(a + 1) * P, :]).then_inc(x_landed[a], 16)
            act.dma_start(cst[:, :], const_dram).then_inc(const_landed, 16)

        def start_sp(sp):
            sp.wait_ge(rows_zeroed, 1)
            for q, tile in enumerate(ROW_TILES):
                for name, n in tile:
                    lo = COL[name] - q * P
                    sp.dma_start(rows[lo:lo + n, q, :], row_view(name)).then_inc(rows_landed, 16)

        def start_pool(pool):
            nc.gpsimd.memset(minus_half, -0.5).then_inc(consts_set, 1)
            pool.dma_start(gpre[:, :], A["norm_g"][0, 0].partition_broadcast(P)).then_inc(gpre_landed, 16)
            pool.wait_ge(consts_set, 1)

        def start_pe(pe):
            pe.wait_ge(const_landed, 16)
            for a in range(NT):
                xn_turn(pe, a, a)
            pe.wait_ge(rows_landed, 16 * PARAM_DMAS)
            for q in range(4):
                mm = nc.tensor.transpose(bank[0][:, q * P:(q + 1) * P], rows[:, q, :], ident)
            mm.then_inc(cols_turned, 1)

        def start_dve(dve):
            nc.vector.memset(buf(ROWS, 0, 4 * P), 0.0).then_inc(rows_zeroed, 1)
            for a in range(NT):
                pre_mean(dve, 0, a)
                x_scaled(dve, 0, a)
            for a in range(NT):
                turn_dve(dve, TURN_PRE0, a, 4, W_HT)
            dve.wait_ge(cols_turned, 1)
            nc.vector.tensor_copy(cols[:, :], bank[0][:, :]).then_inc(cols_ready, 1)
            dve.wait_ge(const_landed, 16)
            dve.wait_ge(cols_ready, 1)

        W_HT, W_DX = 0, 1
        W_XS = {"w": 3, "a": 13, "r": 14, "k": 2, "g": 15, "v": 16}
        MIXES = [("w", 3), ("a", 4), ("k", 1), ("r", 0), ("g", 5), ("v", 2)]
        MIXED = {name: i + 1 for i, (name, _) in enumerate(MIXES)}
        W_K, W_SIG, W_CUM, W_A, W_EP, W_EM, W_KK, W_LORA, W_G, W_R = 4, 5, 6, 7, 8, 9, 10, 11, 12, 17
        W_RINV, W_T1, W_V = 0, 1, 11
        W_REMOVE, W_ADD, W_KEY, W_QUERY = W_SIG, W_A, W_EM, W_EP
        W_N, W_Z, W_LK, W_RK, W_RB = (13, 14), (2, 3), (0, 1), (15, 16), (6, 10)
        W_SOLVE, W_TOK = 1, 17
        W_RHS0, W_RHS1, W_SUM1, W_U1, W_U0 = 5, 4, 7, 0, 1
        W_LNX, W_YC, W_YSQ, W_C, W_OT = 9, 13, 14, 2, 3
        HALVES = [slice(hf * D, (hf + 1) * D) for hf in range(2)]
        nd = buf(W_SOLVE, 0, BS * BS).rearrange("p (s t) -> p s t", t=BS)
        yd = buf(W_SOLVE, BS * BS, 2 * BS * BS).rearrange("p (s t) -> p s t", t=BS)
        n_dram = nc.dram_tensor("n_blocks", (NT, H, NB, BS, BS), F32, kind="Internal").ap()
        y_dram = nc.dram_tensor("y_blocks", (NT, H, NB, BS, BS), F32, kind="Internal").ap()
        rhs0, sum0, u0 = buf(W_RHS0, 0, D), buf(W_RHS0, D, 2 * D), buf(W_U0, 0, D)
        s1 = buf(W_U0, D, D + HP * N)
        u1, q_turned = buf(W_SUM1, 0, D), buf(W_RHS0, 0, D).rearrange("p (c t) -> p c t", t=P)
        sides = lambda i: buf(i).rearrange("p (x h n) -> p x h n", x=2, n=N)
        mid, last_e, s_scale = small(16), small(8), small(8)
        solve_tmp = small(256)
        kk_inv = small(NT * H)
        bon, y_sum, y_mean, y_sq, y_var, y_rstd = (small(32) for _ in range(6))

        (mix_done, lora_hidden, gate_hidden, k_evac, decay_sig, iclr_sig, r_evac, g_evac, v_evac) = (
            sem(n) for n in ("mix_done", "lora_hidden", "gate_hidden", "k_evac", "decay_sig", "iclr_sig", "r_evac",
                             "g_evac", "v_evac"))
        (kk_ready, kk_summed, kk_wide, kk_turned, cum_ready, decay_exp, removal_ready, keys_ready, queries_ready, bonus_ready,
         bonus_summed, bonus_copied, n_mm, n_masked, prod_mm, prod_evac, lk_masked, rk_masked) = (
            sem(n) for n in ("kk_ready", "kk_summed", "kk_wide", "kk_turned", "cum_ready", "decay_exp", "removal_ready", "keys_ready",
                             "queries_ready", "bonus_ready", "bonus_summed", "bonus_copied", "n_mm", "n_masked",
                             "prod_mm", "prod_evac", "lk_masked", "rk_masked"))
        (n_saved, nd_landed, solved, y_saved, z_zeroed, z_landed, n_cut, tok_mm, tok_evac, u_mm, u_rhs, u_sol,
         state_mm, state_ready, q_mm, q_in, u1_mm, u1_ready, ymm, lnx_landed, yc_ready, c_step, c_ready, o_ready, o_mm,
         o_in) = (
            sem(n) for n in ("n_saved", "nd_landed", "solved", "y_saved", "z_zeroed", "z_landed", "n_cut", "tok_mm",
                             "tok_evac", "u_mm", "u_rhs", "u_sol", "state_mm", "state_ready", "q_mm", "q_in", "u1_mm",
                             "u1_ready", "y_mm", "lnx_landed", "yc_ready", "c_step", "c_ready", "o_ready", "o_mm",
                             "o_in"))
        ROUNDS = 2 * NB
        before_round = lambda s: 0 if s == 0 else 4 + 6 * (s - 1)
        sums_before = lambda s: 4 + 6 * (s // 2 - 1) if s else 0
        sols_before = lambda s: 6 * (s // 2)
        PAIR_BANKS = NT * HP
        bank_heads = lambda l: [l % 2 + 2 * (2 * (l % 8 // 2) + i) for i in range(2)]
        Y_BANK = ((5, 0), (6, 7))

        def wide_part(w, s, nslots, stationary, base, a):
            for kk in range(2):
                k = 2 * s + kk
                for half in range(2):
                    mm = nc.tensor.matmul(bank[base + 2 * a + half][:, :], stationary(k, a),
                                          w[:, kk * D + half * HALF:kk * D + (half + 1) * HALF],
                                          start=(k == 0), stop=(k == 2 * nslots - 1))
            return mm

        def rwkv_pe(pe):
            xs = {name: chan(i) for name, i in W_XS.items()}
            lora = buf(W_LORA)

            def columns(name, x, base, s):
                w = weights(pe, FIRST[name] + s).rearrange("p (k n) -> p k n", n=T)
                for n in range(2):
                    for k in range(DC):
                        mm = nc.tensor.matmul(bank[base + s][:, n * T:(n + 1) * T], w[:, k, n * P:(n + 1) * P], x[:, k, :],
                                              start=(k == 0), stop=(k == DC - 1))
                mm.then_inc(slot_done, 1)

            w = weights(pe, FIRST["lora_wa"])[:, 0:2 * DC * 64].rearrange("p (g k n) -> p g k n", g=2, k=DC)
            for g, name in enumerate(("w", "a")):
                pe.wait_ge(mix_done, MIXED[name])
                for k in range(DC):
                    mm = nc.tensor.matmul(bank[g][0:64, 0:T], w[:, g, k, :], xs[name][:, k, :],
                                          start=(k == 0), stop=(k == DC - 1))
            mm.then_inc(slot_done, 1)
            pe.wait_ge(mix_done, MIXED["k"])
            for s in range(4):
                columns("w_k", xs["k"], 4, s)
            w = weights(pe, FIRST["lora_wa2"])
            pe.wait_ge(lora_hidden, 2)
            for g in range(2):
                for c in range(DC):
                    if g == 1 and c % 2 == 0:
                        pe.wait_ge(k_evac, c // 2 + 1)
                    mm = nc.tensor.matmul(bank[4 * g + c // 2][:, (c % 2) * T:(c % 2 + 1) * T],
                                          w[0:64, g * D + c * P:g * D + (c + 1) * P], lora[0:64, g * T:(g + 1) * T],
                                          start=True, stop=True)
            mm.then_inc(slot_done, 1)
            pe.wait_ge(mix_done, MIXED["r"])
            for s in range(4):
                pe.wait_ge(decay_sig, s + 1)
                columns("w_r", xs["r"], 0, s)
                if s == 0:
                    pe.wait_ge(iclr_sig, 1)
                    for c in range(DC):
                        pe.wait_ge(squared, c // 4 + 1)
                        for a in range(NT):
                            mm = nc.tensor.matmul(bank[4][:, a * H + 2 * c:a * H + 2 * c + 2],
                                                  chan(W_RINV)[:, c, a * P:(a + 1) * P], const("head_of"), start=True, stop=True)
                    mm.then_inc(kk_summed, 1)
                if s == 2:
                    pe.wait_ge(iclr_sig, 4)
                    pe.wait_ge(kk_wide, 1)
                    for c in range(DC):
                        for a in range(NT):
                            mm = nc.tensor.transpose(bank[4 + c // 2][:, c % 2 * T + a * P:c % 2 * T + (a + 1) * P],
                                                     toks(W_RINV)[:, a, c * P:(c + 1) * P], ident)
                        if c % 4 == 3:
                            mm.then_inc(kk_turned, 1)
            w = weights(pe, FIRST["lora_g"])[:, 0:DC * GATE_LORA].rearrange("p (k n) -> p k n", n=GATE_LORA)
            pe.wait_ge(mix_done, MIXED["g"])
            pe.wait_ge(r_evac, 1)
            for lo, hi in ((0, P), (P, GATE_LORA)):
                at = 0 if lo == 0 else T
                for k in range(DC):
                    mm = nc.tensor.matmul(bank[0][0:hi - lo, at:at + T], w[:, k, lo:hi], xs["g"][:, k, :],
                                          start=(k == 0), stop=(k == DC - 1))
            mm.then_inc(slot_done, 1)
            w = weights(pe, FIRST["lora_g2"])
            pe.wait_ge(r_evac, 4)
            pe.wait_ge(gate_hidden, 2)
            for a in range(NT):
                for half in range(2):
                    dst = bank[2 * a + half][:, :]
                    nc.tensor.matmul(dst, lora[:, 2 * T + a * P:2 * T + (a + 1) * P],
                                     w[:, half * HALF:(half + 1) * HALF], start=True, stop=False)
                    mm = nc.tensor.matmul(dst, lora[0:32, 3 * T + a * P:3 * T + (a + 1) * P],
                                          w[0:32, D + half * HALF:D + (half + 1) * HALF], start=False, stop=True)
            mm.then_inc(slot_done, 1)

            remove, add, key, query = (chan(i) for i in (W_REMOVE, W_ADD, W_KEY, W_QUERY))
            both_sides = bufs(W_REMOVE, 4).rearrange("p (b c t) -> p b c t", b=4, t=T)[:, 0:4:W_QUERY - W_REMOVE]

            def pairs(l, left, a):
                for i, h in enumerate(bank_heads(l)):
                    lo = (h % 2) * N
                    at = (slice(lo, lo + N), h // 2, slice(a * P, (a + 1) * P))
                    mm = nc.tensor.matmul(bank[4 + l % 4][:, i * T:(i + 1) * T].rearrange("p (x t) -> p x t", t=P), left[at],
                                          both_sides[lo:lo + N, :, h // 2, a * P:(a + 1) * P], start=True, stop=True)
                return mm

            pe.wait_ge(removal_ready, 2)
            pe.wait_ge(queries_ready, 1)
            for l in range(PAIR_BANKS):
                if l >= 4:
                    pe.wait_ge(n_masked, 2 * (l - 3))
                pairs(l, add, l // 8).then_inc(n_mm, 1)

            pe.wait_ge(mix_done, MIXED["v"])
            pe.wait_ge(g_evac, 4)
            for s in range(4):
                w = weights(pe, FIRST["w_v"] + s)
                for a in range(NT):
                    mm = wide_part(w, s, 4, lambda k, a: xs["v"][:, k, a * P:(a + 1) * P], 0, a)
                mm.then_inc(slot_done, 1)
                if s == 0:
                    pe.wait_ge(n_masked, 2 * PAIR_BANKS)
                    pe.wait_ge(keys_ready, 1)
                    for j in range(4):
                        for i in range(4):
                            c = 4 * (j % 2) + i
                            mm = nc.tensor.transpose(bank[4 + j][:, i * P:(i + 1) * P], (add, key)[j // 2][:, c, 0:P], ident)
                        mm.then_inc(tok_mm, 1)
                if s == 1:
                    for j in range(2):
                        pe.wait_ge(tok_evac, j + 1)
                        for i in range(4):
                            mm = nc.tensor.transpose(bank[4 + j][:, i * P:(i + 1) * P], remove[:, 4 * j + i, P:T], ident)
                        mm.then_inc(tok_mm, 1)
                    pe.wait_ge(bonus_ready, 1)
                    pe.wait_ge(tok_evac, 3)
                    for a in range(NT):
                        for c in range(DC):
                            mm = nc.tensor.matmul(bank[6][:, a * H + 2 * c:a * H + 2 * c + 2],
                                                  chan(W_K)[:, c, a * P:(a + 1) * P], const("head_of"), start=True, stop=True)
                    mm.then_inc(bonus_summed, 1)
            pe.wait_ge(bonus_copied, 1)
            pe.wait_ge(tok_evac, 6)
            for l in range(PAIR_BANKS):
                if l >= 4:
                    pe.wait_ge(prod_evac, l - 3)
                pairs(l, key, l // 8).then_inc(prod_mm, 1)

            v = toks(W_V)
            z, n_off, lk, rb, rk = ([heads(m) for m in two] for two in (W_Z, W_N, W_LK, W_RB, W_RK))
            for s in range(ROUNDS):
                if s == 1:
                    pe.wait_ge(z_landed, 16 * NT * NB)
                if s == 2:
                    pe.wait_ge(n_cut, NT)
                for g in range(4 if s == 0 else 6):
                    a = 0 if g < 2 else 1
                    if s == 0:
                        pe.wait_ge(v_evac, 4)
                        pe.wait_ge(lk_masked, g + 1)
                    elif s % 2 == 1:
                        pe.wait_ge(u_rhs, 4 if s == 1 and g >= 2 else sums_before(s - 1) + g + 1)
                    else:
                        pe.wait_ge(u_sol, sols_before(s - 1) + g + 1)
                    wide_sides = a == 1 and s > 0
                    for i in range(4 if wide_sides else 8):
                        h = 4 * (g - 2) + i if wide_sides else 8 * (g % 2) + i
                        hv = slice(h * N, (h + 1) * N)
                        if s == 0:
                            left, right = lk, v[:, a, hv]
                        elif s % 2 == 0:
                            left, right = n_off, sides(W_U1)[:, :, h, :] if a else u0[:, hv]
                        else:
                            left, right = z, (sides(W_RHS1 if s == 1 else W_SUM1)[:, :, h, :] if a else
                                              (rhs0 if s == 1 else sum0)[:, hv])
                        w = 2 * N if wide_sides else N
                        mm = nc.tensor.matmul(bank[g][:, i * w:(i + 1) * w], left[a][:, h, :], right, start=True, stop=True)
                    mm.then_inc(u_mm, 1)
            bh, kh = buf(W_TOK, 0, D), buf(W_TOK, D, 2 * D)
            pe.wait_ge(u_sol, sols_before(ROUNDS - 1) + 2)
            for h in range(H):
                lo, c, hv = (h % 2) * N, h // 2, slice(h * N, (h + 1) * N)
                cells = bank[0][lo:lo + N, c * N:(c + 1) * N]
                nc.tensor.matmul(cells, bh[:, hv], u0[:, hv], start=True, stop=False)
                mm = nc.tensor.matmul(cells, kh[:, hv], v[:, 0, hv], start=False, stop=True)
            mm.then_inc(state_mm, 1)
            pe.wait_ge(u_sol, sols_before(ROUNDS - 1) + 6)
            for c in range(DC):
                mm = nc.tensor.transpose(bank[1 + c // 4][:, c % 4 * P:(c % 4 + 1) * P],
                                         buf(W_U1, D + c * P, D + (c + 1) * P), ident)
            mm.then_inc(q_mm, 1)
            def y_bank(a, q):
                for c in range(HP):
                    h = 2 * c + q
                    cells, hv = bank[Y_BANK[a][q]][:, c * N:(c + 1) * N], slice(h * N, (h + 1) * N)
                    nc.tensor.matmul(cells, rb[a][:, h, :], (u0, u1)[a][:, hv], start=True, stop=False)
                    mm = nc.tensor.matmul(cells, rk[a][:, h, :], v[:, a, hv], start=False, stop=(a == 0))
                    if a == 1:
                        mm = nc.tensor.matmul(cells, query[q * N:(q + 1) * N, c, P:2 * P],
                                              s1[q * N:(q + 1) * N, c * N:(c + 1) * N], start=False, stop=True)
                mm.then_inc(ymm, 1)

            pe.wait_ge(rk_masked, NT)
            y_bank(0, 0)
            pe.wait_ge(q_in, 2)
            pe.wait_ge(state_ready, 1)
            for q in range(2):
                for c in range(HP):
                    mm = nc.tensor.matmul(bank[3 + q][:, c * N:(c + 1) * N], q_turned[q * N:(q + 1) * N, c, :],
                                          s1[q * N:(q + 1) * N, c * N:(c + 1) * N], start=True, stop=True)
            mm.then_inc(u1_mm, 1)
            y_bank(0, 1)
            pe.wait_ge(u1_ready, 2)
            y_bank(1, 0)
            y_bank(1, 1)
            for a in range(NT):
                pe.wait_ge(o_ready, a + 1)
                for c in range(DC):
                    mm = nc.tensor.transpose(bank[2 * a + c // 4][:, c % 4 * P:(c % 4 + 1) * P],
                                             toks(W_YC)[:, a, c * P:(c + 1) * P], ident)
                mm.then_inc(o_mm, 1)
                pe.wait_ge(o_in, 2 * (a + 1))
                for s in range(4):
                    w = weights(pe, FIRST["w_o"] + s)
                    mm = wide_part(w, s, 4, lambda k, a: chan(W_OT)[:, k, a * P:(a + 1) * P], 4, a)
                    if a == NT - 1:
                        mm.then_inc(slot_done, 1)
                if a == 0:
                    mm.then_inc(rows_done, 1)

        def rwkv_act(act):
            lora = buf(W_LORA)
            after_slots(act, "lora_wa")
            nc.scalar.activation(lora[0:64, 0:T], bank[0][0:64, 0:T], ACT.Tanh).then_inc(lora_hidden, 1)
            nc.scalar.activation(lora[0:64, T:2 * T], bank[1][0:64, 0:T], ACT.Copy).then_inc(lora_hidden, 1)
            for s in range(4):
                after_slots(act, "w_k", s + 1)
                nc.scalar.activation(buf(W_K, s * HALF, (s + 1) * HALF), bank[4 + s][:, :], ACT.Copy).then_inc(k_evac, 1)
            for hf in range(2):
                act.wait_ge(kk_ready, hf + 1)
                nc.scalar.activation(buf(W_RINV)[:, HALVES[hf]], buf(W_KK)[:, HALVES[hf]], ACT.Square).then_inc(squared, 1)
            after_slots(act, "lora_wa2")
            for bias, dst, base, done in (("a_w0", W_SIG, 0, decay_sig), ("a_a0", W_A, 4, iclr_sig)):
                for c in range(DC):
                    op = nc.scalar.activation(chan(dst)[:, c, :], bank[base + c // 2][:, (c % 2) * T:(c % 2 + 1) * T],
                                              ACT.Sigmoid, bias=col(bias, c))
                    if c % 2 == 1:
                        op.then_inc(done, 1)
            act.wait_ge(cum_ready, 1)
            nc.scalar.activation(buf(W_EP), buf(W_CUM), ACT.Exp, scale=-KAPPA).then_inc(decay_exp, 1)
            nc.scalar.activation(buf(W_EM), buf(W_CUM), ACT.Exp, scale=KAPPA).then_inc(decay_exp, 1)
            nc.scalar.activation(buf(W_SIG), buf(W_SIG), ACT.Exp, scale=-KAPPA).then_inc(decay_exp, 1)
            nc.scalar.activation(s_scale, last_e, ACT.Exp, scale=-KAPPA).then_inc(decay_exp, 1)
            for s in range(4):
                if s == 2:
                    act.wait_ge(rstd_ready, 1)
                    nc.scalar.activation(buf(W_RINV).rearrange("p (h n) -> p h n", n=N),
                                         spread(kk_inv.unsqueeze(2), [P, NT * H, N]), ACT.Copy).then_inc(kk_wide, 1)
                after_slots(act, "w_r", s + 1)
                nc.scalar.activation(buf(W_R, s * HALF, (s + 1) * HALF), bank[s][:, :], ACT.Copy).then_inc(r_evac, 1)
            after_slots(act, "lora_g")
            nc.scalar.activation(lora[:, 2 * T:3 * T], bank[0][:, 0:T], ACT.Sigmoid).then_inc(gate_hidden, 1)
            nc.scalar.activation(lora[0:32, 3 * T:4 * T], bank[0][0:32, T:2 * T], ACT.Sigmoid).then_inc(gate_hidden, 1)
            after_slots(act, "lora_g2")
            for j in range(4):
                nc.scalar.activation(buf(W_G, j * HALF, (j + 1) * HALF), bank[j][:, :], ACT.Copy).then_inc(g_evac, 1)
            act.wait_ge(bonus_ready, 1)
            for j in range(6):
                if j == 4:
                    act.wait_ge(bonus_summed, 1)
                    nc.scalar.activation(bon, bank[6][:, 0:NT * H], ACT.Copy).then_inc(bonus_copied, 1)
                act.wait_ge(tok_mm, j + 1)
                dst = buf(W_TOK, j * HALF, (j + 1) * HALF) if j < 4 else buf(W_RHS1, D + (j - 4) * HALF, D + (j - 3) * HALF)
                nc.scalar.activation(dst, bank[4 + j % 4][:, :], ACT.Copy).then_inc(tok_evac, 1)
            after_slots(act, "w_v")
            for j in range(4):
                nc.scalar.activation(buf(W_V, j * HALF, (j + 1) * HALF), bank[j][:, :], ACT.Copy).then_inc(v_evac, 1)
            for l in range(PAIR_BANKS):
                a, first = l // 8, bank_heads(l)[0]
                act.wait_ge(prod_mm, l + 1)
                if l == 8:
                    act.wait_ge(y_saved, 16)
                src = bank[4 + l % 4][:, :].rearrange("p (h x t) -> p h x t", x=2, t=P)
                nc.scalar.activation(heads(W_LK[a])[:, first:first + 3:2, :], src[:, :, 0, :], ACT.Copy)
                nc.scalar.activation(heads(W_RK[a])[:, first:first + 3:2, :], src[:, :, 1, :], ACT.Copy).then_inc(prod_evac, 1)
            for s in range(1, ROUNDS, 2):
                for g in range(6):
                    act.wait_ge(u_mm, before_round(s) + g + 1)
                    if g < 2:
                        dst, src = u0[:, g * HALF:(g + 1) * HALF], bank[g][:, :]
                    else:
                        dst = sides(W_U1)[:, :, 4 * (g - 2):4 * (g - 1), :]
                        src = bank[g][:, :].rearrange("p (h x n) -> p x h n", x=2, n=N)
                    nc.scalar.activation(dst, src, ACT.Copy).then_inc(u_sol, 1)
            act.wait_ge(q_mm, 1)
            for j in range(2):
                nc.scalar.activation(q_turned[:, 4 * j:4 * j + 4, :], bank[1 + j][:, :].rearrange("p (c t) -> p c t", t=P),
                                     ACT.Copy).then_inc(q_in, 1)
            for a in range(NT):
                act.wait_ge(yc_ready, a + 1)
                nc.scalar.activation(toks(W_YSQ)[:, a, :], toks(W_YC)[:, a, :], ACT.Square).then_inc(squared, 1)
                act.wait_ge(o_mm, a + 1)
                for q in range(2):
                    nc.scalar.activation(chan(W_OT)[:, 4 * q:4 * q + 4, a * P:(a + 1) * P],
                                         bank[2 * a + q][:, :].rearrange("p (c t) -> p c t", t=P), ACT.Copy).then_inc(o_in, 1)

        def rwkv_dve(dve):
            hT, dx = chan(W_HT), chan(W_DX)
            turned_out(dve, TURN_PRE0)
            nc.vector.tensor_scalar(dx[:, :, 0:1], hT[:, :, 0:1], -1.0, None, ALU.mult)
            link(dve, nc.vector.tensor_tensor(dx[:, :, 1:T], hT[:, :, 0:T - 1], hT[:, :, 1:T], ALU.subtract))
            for name, row in MIXES:
                for c in range(DC):
                    op = nc.vector.scalar_tensor_tensor(chan(W_XS[name])[:, c, :], dx[:, c, :], col("a_mu", row * DC + c),
                                                        hT[:, c, :], ALU.mult, ALU.add)
                op.then_inc(mix_done, 1)
            kT, kk, sig, cum, aT = chan(W_K), chan(W_KK), chan(W_SIG), chan(W_CUM), chan(W_A)
            for hf in range(2):
                dve.wait_ge(k_evac, 2 * hf + 2)
                for c in range(4 * hf, 4 * hf + 4):
                    op = nc.vector.tensor_scalar(kk[:, c, :], kT[:, c, :], col("a_k_k", c), None, ALU.mult)
                op.then_inc(kk_ready, 1)
            dve.wait_ge(decay_sig, 4)
            for c in range(DC):
                for a in range(NT):
                    t = slice(a * P, (a + 1) * P)
                    op = nc.vector.tensor_tensor_scan(cum[:, c, t], const("ones"), sig[:, c, t], 0.0, ALU.mult, ALU.add)
            link(dve, op)
            tiles = buf(W_CUM).rearrange("p (n t) -> p n t", t=P)
            link(dve, nc.vector.tensor_copy(mid, tiles[:, :, P // 2 - 1]))
            link(dve, nc.vector.tensor_tensor(tiles, tiles, spread(mid.unsqueeze(2), [P, 16, P]), ALU.subtract))
            nc.vector.tensor_tensor(last_e, tiles[:, 0:16:2, P - 1], mid[:, 1:16:2], ALU.add)
            nc.vector.tensor_tensor(buf(W_SIG), buf(W_CUM), buf(W_SIG), ALU.subtract).then_inc(cum_ready, 1)
            dve.wait_ge(kk_summed, 1)
            nc.vector.tensor_scalar(kk_inv, bank[4][:, 0:NT * H], 1e-24, None, ALU.max).then_inc(var_ready, 1)
            dve.wait_ge(mix_done, len(MIXES))
            dve.wait_ge(iclr_sig, 4)
            for c in range(DC):
                op = nc.vector.tensor_scalar(chan(W_T1)[:, c, :], aT[:, c, :], 1.0, col("a_k_a", c), ALU.subtract, ALU.mult)
            link(dve, op)
            dve.wait_ge(kk_ready, 2)
            k_new = step(nc.vector.scalar_tensor_tensor(buf(W_K), buf(W_T1), 1.0, buf(W_K), ALU.add, ALU.mult))
            dve.wait_ge(decay_exp, 4)
            for hf in range(2):
                at = HALVES[hf]
                dve.wait_ge(kk_turned, hf + 1)
                for j in (2 * hf, 2 * hf + 1):
                    cells = buf(W_KK, j * HALF, (j + 1) * HALF)
                    op = nc.vector.tensor_tensor(cells, cells, bank[4 + j][:, :], ALU.mult)
                link(dve, op)
                link(dve, nc.vector.tensor_tensor(buf(W_A)[:, at], buf(W_A)[:, at], buf(W_KK)[:, at], ALU.mult))
                link(dve, nc.vector.tensor_tensor(buf(W_ADD)[:, at], buf(W_A)[:, at], buf(W_EM)[:, at], ALU.mult))
                nc.vector.scalar_tensor_tensor(buf(W_REMOVE)[:, at], buf(W_KK)[:, at], -1.0, buf(W_SIG)[:, at],
                                               ALU.mult, ALU.mult).then_inc(removal_ready, 1)

            dve.wait_ge(r_evac, 4)
            nc.vector.tensor_tensor(buf(W_QUERY), buf(W_R), buf(W_EP), ALU.mult).then_inc(queries_ready, 1)

            for l in range(PAIR_BANKS):
                a, first = l // 8, bank_heads(l)[0]
                src = bank[4 + l % 4][:, :].rearrange("p (h x t) -> p h x t", x=2, t=P)
                dve.wait_ge(n_mm, l + 1)
                for x, (dst, mask) in enumerate(((W_N, "before"), (W_RB, "upto"))):
                    nc.vector.tensor_tensor(heads(dst[a])[:, first:first + 3:2, :], src[:, :, x, :],
                                            spread(const(mask).unsqueeze(1), [P, 2, P]), ALU.mult).then_inc(n_masked, 1)
            dve.wait_ge(dve_step, k_new)
            nc.vector.tensor_tensor(buf(W_KEY), buf(W_K), buf(W_EM), ALU.mult).then_inc(keys_ready, 1)
            dve.wait_ge(keys_ready, 1)
            for c in range(DC):
                op = nc.vector.scalar_tensor_tensor(kT[:, c, :], chan(W_R)[:, c, :], col("a_r_k", c), kT[:, c, :],
                                                    ALU.mult, ALU.mult)
            op.then_inc(bonus_ready, 1)
            dve.wait_ge(removal_ready, 2)
            link(dve, nc.vector.memset(buf(W_SOLVE, BS * BS, 2 * BS * BS), 0.0))
            link(dve, nc.vector.memset(buf(W_SOLVE, BS * BS, 2 * BS * BS)[:, 0:BS * BS:BS + 1], 1.0))
            dve.wait_ge(nd_landed, 16)
            for j in range(BS - 1):
                m, w = j + 1, BS - 1 - j
                outer = solve_tmp[:, 0:m * w].rearrange("p (s t) -> p s t", t=w)
                link(dve, nc.vector.tensor_tensor(outer, spread(yd[:, 0:m, j:j + 1], [P, m, w]),
                                                  spread(nd[:, j:j + 1, j + 1:BS], [P, m, w]), ALU.mult))
                op = nc.vector.tensor_tensor(yd[:, 0:m, j + 1:BS], yd[:, 0:m, j + 1:BS], outer, ALU.add)
                if j < BS - 2:
                    link(dve, op)
            op.then_inc(solved, 1)
            for g in range(4):
                at = slice(g % 2 * 8, g % 2 * 8 + 8)
                dve.wait_ge(prod_evac, 4 * (g + 1))
                nc.vector.tensor_tensor(heads(W_LK[g // 2])[:, at], heads(W_LK[g // 2])[:, at],
                                        spread(const("before").unsqueeze(1), [P, 8, P]), ALU.mult).then_inc(lk_masked, 1)
            for s in range(0, ROUNDS, 2):
                for g in range(4 if s == 0 else 6):
                    dve.wait_ge(u_mm, before_round(s) + g + 1)
                    cells = slice(g % 2 * HALF, (g % 2 + 1) * HALF)
                    if s == 0:
                        if g == 0:
                            dve.wait_ge(tok_mm, 6)
                        if g == 2:
                            dve.wait_ge(bonus_summed, 1)
                        op = nc.vector.tensor_copy((rhs0 if g < 2 else buf(W_RHS1, 0, D))[:, cells], bank[g][:, :])
                    elif g < 2:
                        op = nc.vector.tensor_tensor(sum0[:, cells], bank[g][:, :], rhs0[:, cells], ALU.add)
                    else:
                        at = (slice(None), slice(None), slice(4 * (g - 2), 4 * (g - 1)))
                        op = nc.vector.tensor_tensor(sides(W_SUM1)[at], bank[g][:, :].rearrange("p (h x n) -> p x h n", x=2, n=N),
                                                     sides(W_RHS1)[at], ALU.add)
                    op.then_inc(u_rhs, 1)
            dve.wait_ge(state_mm, 1)
            nc.vector.tensor_tensor(s1.rearrange("p (c n) -> p c n", n=N), bank[0][:, :].rearrange("p (c n) -> p c n", n=N),
                                    spread(s_scale.unsqueeze(2), [P, HP, N]), ALU.mult).then_inc(state_ready, 1)
            dve.wait_ge(u1_mm, 1)
            for q in range(2):
                by_parity = lambda ap: ap.rearrange("p (c g n) -> p g c n", g=2, n=N)[:, q]
                nc.vector.tensor_tensor(by_parity(u1), bank[3 + q][:, :].rearrange("p (c n) -> p c n", n=N),
                                        by_parity(buf(W_U1, 0, D)), ALU.add).then_inc(u1_ready, 1)
            dve.wait_ge(u_mm, before_round(ROUNDS))
            for a in range(NT):
                yc = toks(W_YC)[:, a, :]
                stat = slice(a * H, (a + 1) * H)
                for q in range(2):
                    dve.wait_ge(ymm, 2 * a + q + 1)
                    op = nc.vector.tensor_reduce(y_sum[:, a * H + q:(a + 1) * H:2], bank[Y_BANK[a][q]][:, :].rearrange(
                        "p (c n) -> p c n", n=N), AX, ALU.add)
                link(dve, op)
                link(dve, nc.vector.tensor_scalar(y_mean[:, stat], y_sum[:, stat], -1.0 / N, None, ALU.mult))
                for q in range(2):
                    op = nc.vector.tensor_tensor(yc.rearrange("p (c g n) -> p g c n", g=2, n=N)[:, q],
                                                 bank[Y_BANK[a][q]][:, :].rearrange("p (c n) -> p c n", n=N),
                                                 spread(y_mean[:, a * H + q:(a + 1) * H:2].unsqueeze(2), [P, HP, N]), ALU.add)
                op.then_inc(yc_ready, 1)
                dve.wait_ge(squared, 2 + a + 1)
                link(dve, nc.vector.tensor_reduce(y_sq[:, stat], toks(W_YSQ)[:, a, :].rearrange("p (h n) -> p h n", n=N),
                                                  AX, ALU.add))
                nc.vector.tensor_scalar(y_var[:, stat], y_sq[:, stat], 1.0 / N, LNX_EPS, ALU.mult, ALU.add).then_inc(var_ready, 1)
                dve.wait_ge(yc_ready, a + 1)
                dve.wait_ge(rstd_ready, 1 + a + 1)
                y32 = yc.rearrange("p (h n) -> p h n", n=N)
                link(dve, nc.vector.tensor_tensor(y32, y32, spread(y_rstd[:, stat].unsqueeze(2), [P, H, N]), ALU.mult))
                dve.wait_ge(c_ready, a + 1)
                link(dve, nc.vector.tensor_tensor(yc, yc, toks(W_G)[:, a, :], ALU.mult))
                nc.vector.tensor_tensor(yc, yc, toks(W_C)[:, a, :], ALU.add).then_inc(o_ready, 1)

        def rwkv_pool(pool):
            pool.wait_ge(var_ready, 1)
            nc.gpsimd.tensor_tensor(kk_inv, kk_inv, minus_half, ALU.pow).then_inc(rstd_ready, 1)
            after_slots(pool, "w_k")
            for m in W_Z:
                nc.gpsimd.memset(buf(m), 0.0).then_inc(z_zeroed, 1)
            pool.wait_ge(n_saved, 16 * NT * NB)
            for m in W_N:
                nc.gpsimd.tensor_tensor(heads(m), heads(m), spread(const("off").unsqueeze(1), [P, H, P]),
                                        ALU.mult).then_inc(n_cut, 1)
            for a in range(NT):
                pool.wait_ge(prod_evac, 8 * (a + 1))
                nc.gpsimd.tensor_tensor(heads(W_RK[a]), heads(W_RK[a]), spread(const("upto").unsqueeze(1), [P, H, P]),
                                        ALU.mult).then_inc(rk_masked, 1)
            pool.wait_ge(prod_mm, PAIR_BANKS)
            pool.dma_start(buf(W_LNX, 0, D), A["a_lnx_w"][0].partition_broadcast(P)).then_inc(lnx_landed, 16)
            pool.dma_start(buf(W_LNX, D, 2 * D), A["a_lnx_b"][0].partition_broadcast(P)).then_inc(lnx_landed, 16)
            pool.wait_ge(lnx_landed, 32)
            pool.wait_ge(bonus_copied, 1)
            pool.wait_ge(u_mm, before_round(ROUNDS))
            steps_done = 0
            for a in range(NT):
                c, g = toks(W_C)[:, a, :], toks(W_G)[:, a, :]
                nc.gpsimd.tensor_tensor(c.rearrange("p (h n) -> p h n", n=N), toks(W_V)[:, a, :].rearrange("p (h n) -> p h n", n=N),
                                        spread(bon[:, a * H:(a + 1) * H].unsqueeze(2), [P, H, N]), ALU.mult).then_inc(c_step, 1)
                for in1, op in ((buf(W_LNX, D, 2 * D), ALU.add), (g, ALU.mult)):
                    steps_done += 1
                    pool.wait_ge(c_step, steps_done)
                    nc.gpsimd.tensor_tensor(c, c, in1, op).then_inc(c_step, 1)
                steps_done += 1
                pool.wait_ge(c_step, steps_done)
                nc.gpsimd.tensor_tensor(g, g, buf(W_LNX, 0, D), ALU.mult).then_inc(c_ready, 1)
                if a == 0:
                    pool.wait_ge(var_ready, 1 + 1)
                    nc.gpsimd.tensor_tensor(y_rstd[:, 0:H], y_var[:, 0:H], minus_half[:, 0:H], ALU.pow).then_inc(rstd_ready, 1)
            pool.wait_ge(var_ready, 1 + 2)
            nc.gpsimd.tensor_tensor(y_rstd[:, H:2 * H], y_var[:, H:2 * H], minus_half[:, 0:H], ALU.pow).then_inc(rstd_ready, 1)

        def rwkv_blocks_sp(sp):
            for a in range(NT):
                for b in range(NB):
                    if b == 0:
                        sp.wait_ge(n_masked, PAIR_BANKS * (a + 1))
                    sp.dma_start(n_dram[a, :, b].rearrange("h s t -> s h t"),
                                 heads(W_N[a])[b * BS:(b + 1) * BS, :, b * BS:(b + 1) * BS]).then_inc(n_saved, 16)
            sp.wait_ge(n_saved, 16 * NT * NB)
            sp.wait_ge(kk_turned, 2)
            sp.dma_start(buf(W_SOLVE, 0, BS * BS), n_dram.rearrange("a h b s t -> (a h b) (s t)")).then_inc(nd_landed, 16)
            sp.wait_ge(solved, 1)
            sp.dma_start(y_dram.rearrange("a h b s t -> (a h b) (s t)"), buf(W_SOLVE, BS * BS, 2 * BS * BS)).then_inc(y_saved, 16)
            sp.wait_ge(y_saved, 16)
            sp.wait_ge(z_zeroed, NT)
            for a in range(NT):
                for b in range(NB):
                    sp.dma_start(heads(W_Z[a])[b * BS:(b + 1) * BS, :, b * BS:(b + 1) * BS],
                                 y_dram[a, :, b].rearrange("h s t -> s h t")).then_inc(z_landed, 16)

        M_H, M_XKV, M_TOK, M_LATT, M_K, M_Q, M_V, M_ROT, M_S, M_PT, M_OT = 0, 1, 2, 3, 4, 6, 8, 9, 10, 11, 12
        M_H_LO, M_XKV_LO, M_LATT_LO, M_OT_LO = 10, 11, 0, 1
        ckv = buf(M_TOK, 0, NT * KV_LORA).rearrange("p (a n) -> p a n", a=NT)
        cq = buf(M_TOK, 512, 512 + NT * Q_LORA).rearrange("p (a n) -> p a n", a=NT)
        kr = buf(M_TOK, 1280, 1280 + NT * QK).rearrange("p (a n) -> p a n", a=NT)
        kraw = buf(M_TOK, 1472, 1472 + NT * ROPE).rearrange("p (a n) -> p a n", a=NT)
        krt = [buf(M_TOK, 1536 + 32 * i, 1568 + 32 * i).rearrange("p (a n) -> p a n", a=NT) for i in range(4)]
        down = ((bank[4], bank[6]), (bank[5], bank[7]))
        lat = chan2(M_LATT, M_LATT_LO)
        kT = bufs(M_K, 2).rearrange("p (h t) -> p h t", t=T)
        qT = bufs(M_Q, 2).rearrange("p (h t) -> p h t", t=T)
        s_buf = [buf(M_S, i * 384, (i + 1) * 384) for i in range(3)]
        pt_buf = [buf(M_PT, i * 384, (i + 1) * 384) for i in range(2)]
        lat_sum, lat_var, lat_rstd = small(4), small(4), small(4)
        sm_nmax, sm_sum, sm_inv = small(2 * H), small(2 * H), small(2 * H)
        (lat_ready, lat_turned, lat_hi, lat_in, krope_in, nope_evac, vh_evac, q_evac, perm_mm, q_cos, q_roped, s_mm, sm_max,
         sm_exp, p_ready, pt_mm, pt_evac, pv_mm, ot_hi, ot_in) = (
            sem(n) for n in ("lat_ready", "lat_turned", "lat_hi", "lat_in", "krope_in", "nope_evac", "vh_evac",
                             "q_evac", "perm_mm", "q_cos", "q_roped", "mla_s_mm", "mla_max", "mla_exp", "mla_p_ready",
                             "mla_pt_mm", "mla_pt_evac", "mla_pv_mm", "mla_ot_hi", "mla_ot_in"))

        rot = slice(NOPE, QK)

        def rope_table(name):
            return spread(cst[rot, CONST_AT[name]:CONST_AT[name] + T].unsqueeze(1), [ROPE, 2, T])

        def mla_pe(pe):
            downs = (("kv_down", chan2(M_XKV, M_XKV_LO), TURN_XKV, KV_LORA + ROPE),
                     ("q_down", chan2(M_H, M_H_LO), TURN_PRE2, Q_LORA))
            for a in range(NT):
                xn_turn(pe, XN_OF[2] + 2 * a, a, XN_KV, 4)
                xn_turn(pe, XN_OF[2] + 2 * a + 1, a, XN, 0)
                for n, (name, src, turn, width) in enumerate(downs):
                    for s in range(2):
                        w = split_weights(pe, FIRST[name] + s)
                        turned_out(pe, turn, a, s)
                        for kk in range(4):
                            k = 4 * s + kk
                            mm = product(down[n][a][:, 0:width], both(src, slice(None), k, slice(a * P, (a + 1) * P)),
                                         both(w, slice(None), slice(kk * width, (kk + 1) * width)), k == 0, k == DC - 1)
                        if a == NT - 1:
                            mm.then_inc(slot_done, 1)
            pe.wait_ge(lat_ready, 1)
            for a in range(NT):
                for c in range(2):
                    nc.tensor.transpose(bank[0][:, c * T + a * P:c * T + (a + 1) * P], ckv[:, a, c * P:(c + 1) * P], ident)
                for c in range(3):
                    nc.tensor.transpose(bank[1 + c // 2][:, (c % 2) * T + a * P:(c % 2) * T + (a + 1) * P],
                                        cq[:, a, c * P:(c + 1) * P], ident)
                mm = nc.tensor.transpose(bank[3][0:QK, a * P:(a + 1) * P], kr[:, a, :], ident)
            mm.then_inc(lat_turned, 1)
            pe.wait_ge(lat_in, 5)
            for s in range(2):
                w = [v.rearrange("p (k h n) -> p k h n", k=2, n=2 * N) for v in split_weights(pe, FIRST["kv_up"] + s)]
                for i in range(8):
                    if s == 0 and i == 6:
                        pe.wait_ge(krope_in, 1)
                    if s == 1 and i % 2 == 0:
                        pe.wait_ge(nope_evac, i // 2 + 1)
                    for k in range(2):
                        mm = product(bank[i // 2][0:NOPE, (i % 2) * T:(i % 2 + 1) * T],
                                     both(w, slice(None), k, i, slice(0, NOPE)), both(lat, slice(None), k), k == 0, k == 1)
                for a in range(NT):
                    for k in range(2):
                        mm = product(bank[4 + 2 * s + a][:, :].rearrange("p (h n) -> p h n", n=N),
                                     both(lat, slice(None), k, slice(a * P, (a + 1) * P)),
                                     both(w, slice(None), k, slice(None), slice(NOPE, 2 * N)), k == 0, k == 1)
                mm.then_inc(slot_done, 1)
            def swapped(g):
                pe.wait_ge(q_evac, g + 1)
                if g >= 4:
                    pe.wait_ge(q_roped, g - 3)
                nc.tensor.matmul(bank[4 + g % 4][0:QK, :], const("perm")[0:QK, :], qT[0:QK, 2 * g:2 * g + 2, :],
                                 start=True, stop=True).then_inc(perm_mm, 1)

            pe.wait_ge(nope_evac, 8)
            pe.wait_ge(vh_evac, 4)
            for s in range(4):
                w = [v[:, 0:3 * 4 * QK].rearrange("p (k n) -> p k n", k=3) for v in split_weights(pe, FIRST["q_up"] + s)]
                for i in range(4):
                    g = 2 * s + i // 2
                    if g >= 4 and i % 2 == 0:
                        pe.wait_ge(q_evac, g - 3)
                    for k in range(3):
                        mm = product(bank[g % 4][0:QK, (i % 2) * T:(i % 2 + 1) * T],
                                     both(w, slice(None), k, slice(i * QK, (i + 1) * QK)), both(lat, slice(None), 2 + k),
                                     k == 0, k == 2)
                mm.then_inc(slot_done, 1)
                if s > 0:
                    swapped(2 * s - 2)
                    swapped(2 * s - 1)
            swapped(6)
            swapped(7)
            pe.wait_ge(q_evac, 8)
            v = toks(M_V)

            def scores(h):
                if h >= 2:
                    pe.wait_ge(sm_max, h - 1)
                pe.wait_ge(q_roped, h // 2 + 1)
                for a, cells in enumerate((slice(0, P), slice(P, 3 * P))):
                    mm = nc.tensor.matmul(bank[h % 2][:, cells], qT[0:QK, h, a * P:(a + 1) * P],
                                          kT[0:QK, h, 0:(a + 1) * P], start=True, stop=True)
                mm.then_inc(s_mm, 1)

            def turn_p(h):
                pe.wait_ge(p_ready, h + 1)
                if h >= 2:
                    pe.wait_ge(pt_evac, h - 1)
                for i in range(3):
                    mm = nc.tensor.transpose(bank[2 + h % 2][:, i * P:(i + 1) * P], s_buf[h % 3][:, i * P:(i + 1) * P], ident)
                mm.then_inc(pt_mm, 1)

            def values(h):
                pe.wait_ge(pt_evac, h + 1)
                c, rows_, hv = h // 2, slice((h % 2) * N, (h % 2 + 1) * N), slice(h * N, (h + 1) * N)
                dst = bank[4 + c // 2][rows_, (c % 2) * T:(c % 2 + 1) * T]
                pt = pt_buf[h % 2]
                nc.tensor.matmul(dst, v[:, 0, hv], pt[:, 0:T], start=True, stop=False)
                nc.tensor.matmul(dst[:, P:T], v[:, 1, hv], pt[:, T:3 * P], start=False, stop=True).then_inc(pv_mm, 1)

            scores(0)
            scores(1)
            for h in range(H):
                if h == 1:
                    pe.wait_ge(q_roped, 8)
                if h >= 2:
                    values(h - 2)
                if h + 2 < H:
                    scores(h + 2)
                turn_p(h)
            values(H - 2)
            values(H - 1)
            pe.wait_ge(ot_in, 4)
            wide2(pe, FIRST["o_w"], 4, chan2(M_OT, M_OT_LO), 4, rows=True)

        def mla_act(act):
            after_slots(act, "kv_down")
            for i in range(4):
                if i == 2:
                    after_slots(act, "q_down")
                n = (KV_LORA, Q_LORA)[i // 2]
                nc.scalar.activation(buf(XN, i * HALF, i * HALF + n), down[i // 2][i % 2][:, 0:n], ACT.Square,
                                     accum_out=lat_sum[:, i:i + 1]).then_inc(squared, 1)
            ahead(act, FIRST["kv_up"], split_act)
            act.wait_ge(lat_turned, 1)
            for c in range(5):
                nc.scalar.activation(lat[0][:, c, :], bank[c // 2][:, (c % 2) * T:(c % 2 + 1) * T], ACT.Copy,
                                     scale=col("kv_a_norm_g", c) if c < 2 else col("q_norm_g", c - 2)).then_inc(lat_hi, 1)
            nc.scalar.activation(kT[NOPE:QK, :, :], spread(bank[3][NOPE:QK, 0:T].unsqueeze(1), [ROPE, H, T]),
                                 ACT.Copy).then_inc(krope_in, 1)
            ahead(act, FIRST["q_up"] + 1, split_act)
            for s in range(2):
                after_slots(act, "kv_up", s + 1)
                for j in range(4):
                    h = 8 * s + 2 * j
                    nc.scalar.activation(kT[0:NOPE, h:h + 2, :], bank[j][0:NOPE, :].rearrange("p (h t) -> p h t", t=T),
                                         ACT.Copy).then_inc(nope_evac, 1)
                ahead(act, FIRST["q_up"] + 2 + s, split_act)
            for g in range(8):
                after_slots(act, "q_up", g // 2 + 1)
                nc.scalar.activation(qT[0:QK, 2 * g:2 * g + 2, :], bank[g % 4][0:QK, :].rearrange("p (h t) -> p h t", t=T),
                                     ACT.Copy).then_inc(q_evac, 1)

            def exps(h):
                act.wait_ge(sm_max, h + 1)
                for a, (lo, hi) in enumerate(((0, P), (P, 3 * P))):
                    op = nc.scalar.activation(s_buf[h % 3][:, lo:hi], s_buf[h % 3][:, lo:hi], ACT.Exp,
                                              bias=sm_nmax[:, 2 * h + a:2 * h + a + 1],
                                              accum_out=sm_sum[:, 2 * h + a:2 * h + a + 1])
                op.then_inc(sm_exp, 1)

            def evac(h):
                act.wait_ge(pt_mm, h + 1)
                if h >= 2:
                    act.wait_ge(pv_mm, h - 1)
                nc.scalar.activation(pt_buf[h % 2], bank[2 + h % 2][:, 0:3 * P], ACT.Copy).then_inc(pt_evac, 1)

            def outputs(b):
                act.wait_ge(pv_mm, 4 * (b + 1))
                nc.scalar.activation(buf(M_OT, b * HALF, (b + 1) * HALF, arena12), bank[4 + b][:, :], ACT.Copy).then_inc(ot_hi, 1)

            for h in range(H):
                exps(h)
                if h >= 1:
                    evac(h - 1)
                if h >= 6 and h % 4 == 2:
                    outputs(h // 4 - 1)
                if h < 8 and h % 2 == 1:
                    ahead(act, FIRST["o_w"] + h // 2, split_act)
            evac(H - 1)
            outputs(3)
            ahead(act, LAST["o_w"], split_act)

        def mla_dve(dve):
            nc.vector.memset(kr[:, :, 0:NOPE], 0.0)
            dve.wait_ge(squared, 4 + 4)
            link(dve, nc.vector.tensor_scalar(lat_var[:, 0:2], lat_sum[:, 0:2], 1.0 / KV_LORA, EPS, ALU.mult, ALU.add))
            nc.vector.tensor_scalar(lat_var[:, 2:4], lat_sum[:, 2:4], 1.0 / Q_LORA, EPS, ALU.mult, ALU.add).then_inc(var_ready, 1)
            for a in range(NT):
                op = nc.vector.tensor_copy(kraw[:, a, :], down[0][a][:, KV_LORA:KV_LORA + ROPE])
            link(dve, op)
            half = ROPE // 2
            x1, x2 = kraw[:, :, 0:half], kraw[:, :, half:ROPE]
            cos, sin = (const(n).rearrange("p (a n) -> p a n", a=NT) for n in ("kcos", "ksin"))
            for i, (x, f) in enumerate(((x1, cos), (x2, sin), (x1, sin), (x2, cos))):
                op = nc.vector.tensor_tensor(krt[i], x, f, ALU.mult)
            link(dve, op)
            nc.vector.tensor_tensor(kr[:, :, NOPE:NOPE + half], krt[0], krt[1], ALU.subtract)
            nc.vector.tensor_tensor(kr[:, :, NOPE + half:QK], krt[2], krt[3], ALU.add)
            dve.wait_ge(rstd_ready, 3 + 1)
            for i in range(4):
                n, dst = ((KV_LORA, ckv), (Q_LORA, cq))[i // 2]
                op = nc.vector.tensor_scalar(dst[:, i % 2, :], down[i // 2][i % 2][:, 0:n], lat_rstd[:, i:i + 1], None, ALU.mult)
            op.then_inc(lat_ready, 1)
            ahead(dve, FIRST["kv_up"], split_dve)
            for c in range(5):
                dve.wait_ge(lat_hi, min(c // 2 * 2 + 2, 5))
                nc.vector.scalar_tensor_tensor(lat[1][:, c, :], bank[c // 2][:, (c % 2) * T:(c % 2 + 1) * T],
                                               col("kv_a_norm_g", c) if c < 2 else col("q_norm_g", c - 2), lat[0][:, c, :].bitcast(F32),
                                               ALU.mult, ALU.subtract).then_inc(lat_in, 1)
            ahead(dve, FIRST["q_up"] + 1, split_dve)
            for s in range(2):
                after_slots(dve, "kv_up", s + 1)
                for a in range(NT):
                    nc.vector.tensor_copy(toks(M_V)[:, a, s * HALF:(s + 1) * HALF], bank[4 + 2 * s + a][:, :]).then_inc(vh_evac, 1)
                ahead(dve, FIRST["q_up"] + 2 + s, split_dve)
            for g in range(8):
                q = qT[rot, 2 * g:2 * g + 2, :]
                tmp = buf(M_ROT, (g % 2) * HALF, (g % 2 + 1) * HALF)[rot, :].rearrange("p (h t) -> p h t", t=T)
                dve.wait_ge(perm_mm, g + 1)
                link(dve, nc.vector.tensor_tensor(tmp, bank[4 + g % 4][rot, :].rearrange("p (h t) -> p h t", t=T),
                                                  rope_table("sinT"), ALU.mult))
                dve.wait_ge(q_cos, g + 1)
                nc.vector.tensor_tensor(q, q, tmp, ALU.add).then_inc(q_roped, 1)

            def maxima(h):
                dve.wait_ge(s_mm, h + 1)
                if h >= 3:
                    dve.wait_ge(pt_mm, h - 2)
                s = s_buf[h % 3]
                link(dve, nc.vector.scalar_tensor_tensor(s, bank[h % 2][:, 0:3 * P], MLA_SCALE, const("maskb"), ALU.mult, ALU.add))
                nc.vector.tensor_reduce(sm_nmax[:, 2 * h:2 * h + 1], s[:, 0:P], AX, ALU.max, negate=True)
                nc.vector.tensor_reduce(sm_nmax[:, 2 * h + 1:2 * h + 2], s[:, P:3 * P], AX, ALU.max, negate=True).then_inc(sm_max, 1)

            def normalize(h):
                dve.wait_ge(sm_exp, h + 1)
                link(dve, nc.vector.reciprocal(sm_inv[:, 2 * h:2 * h + 2], sm_sum[:, 2 * h:2 * h + 2]))
                for a, (lo, hi) in enumerate(((0, P), (P, 3 * P))):
                    op = nc.vector.tensor_scalar(s_buf[h % 3][:, lo:hi], s_buf[h % 3][:, lo:hi],
                                                 sm_inv[:, 2 * h + a:2 * h + a + 1], None, ALU.mult)
                op.then_inc(p_ready, 1)

            def outputs(b):
                dve.wait_ge(ot_hi, b + 1)
                at = slice(b * HALF, (b + 1) * HALF)
                nc.vector.tensor_tensor(buf(M_OT_LO, mem=arena12)[:, at], bank[4 + b][:, :], buf(M_OT, mem=arena12)[:, at].bitcast(F32), ALU.subtract).then_inc(ot_in, 1)

            for h in range(H):
                maxima(h)
                if h >= 1:
                    normalize(h - 1)
                if h >= 7 and h % 4 == 3:
                    outputs(h // 4 - 1)
            normalize(H - 1)
            outputs(3)
            emitted[dve] = LAST["o_w"] + 1
            dve.wait_ge(split_ready, LAST["o_w"] - SPLIT0 + 1)

        def mla_pool(pool):
            pool.wait_ge(var_ready, 3 + 1)
            nc.gpsimd.tensor_tensor(lat_rstd, lat_var, minus_half[:, 0:4], ALU.pow).then_inc(rstd_ready, 1)
            for g in range(8):
                q = qT[rot, 2 * g:2 * g + 2, :]
                pool.wait_ge(perm_mm, g + 1)
                nc.gpsimd.tensor_tensor(q, q, rope_table("cosT"), ALU.mult).then_inc(q_cos, 1)
            pool.wait_ge(split_ready, LAST["q_up"] - SPLIT0 + 1)
            for n in range(FIRST["o_w"], LAST["o_w"] + 1):
                split_lo(pool, nc.gpsimd, n)

        B_H, B_XC, B_XS, B_Z, B_GA, B_GS, B_QK, B_QR, B_QT, B_P, B_OT = 0, 1, 3, 4, 5, 6, 7, 8, 9, 10, 12
        B_H_LO, B_OT_LO, B_SQ_LO, B_T2_LO = 11, 9, 0, 9
        B_CB, B_XF, B_XB, B_LHS, B_E, B_Y, B_SQ = 11, 0, 2, 8, 17, 1, 2
        HD = (GH + GKV) * N
        xcT = bufs(B_XC, 2)[:, 0:XC * T].rearrange("p (c t) -> p c t", t=T)
        xc_acc = [buf(B_XC + 1, 1024 + i * T, 1024 + (i + 1) * T) for i in range(4)]
        qk = buf(B_QK, 0, NT * HD).rearrange("p (a n) -> p a n", a=NT)
        vg = buf(B_QK, NT * HD, NT * HD + NT * P).rearrange("p (a n) -> p a n", a=NT)
        qr = buf(B_QR, 0, NT * HD).rearrange("p (a n) -> p a n", a=NT)
        rot_tmp = [buf(B_QR, NT * HD + i * HD // 2, NT * HD + (i + 1) * HD // 2) for i in range(2)]
        qgT = buf(B_QT, 0, GJ * T).rearrange("p (j t) -> p j t", t=T)
        kgT = buf(B_QT, GJ * T, (GJ + 1) * T)
        qk_gain = buf(B_QT, (GJ + 1) * T, (GJ + 1) * T + HD)
        gp_buf = [buf(B_P, 0, HALF), buf(B_P, HALF, 2 * HALF), buf(B_E, 0, HALF)]
        gpt_buf = [buf(B_P, (2 + i) * HALF, (3 + i) * HALF) for i in range(2)]
        cb = [buf(B_CB, g * 768, (g + 1) * 768).rearrange("p (n l) -> p n l", l=P) for g in range(2)]
        seg_lhs = [buf(B_LHS, i * HALF, (i + 1) * HALF).rearrange("p (n l) -> p n l", l=P) for i in range(2)]
        e_buf = [buf(B_E, i * HALF, (i + 1) * HALF) for i in range(3)]
        carry_decay = buf(B_E, 3 * HALF, 3 * HALF + 4 * H)
        arena_small = buf(B_OT, GJ * T, SLOT)
        (dt_bias, a_log, dt_x, dt_n, dt_e, dt_l, dt, adt) = (
            arena_small[:, i * 64:(i + 1) * 64].rearrange("p (a h) -> p a h", a=NT) for i in range(8))
        d_skip = arena_small[:, 512:512 + H]
        qk_ss, qk_var, qk_rstd = (arena_small[:, 540 + 20 * i:560 + 20 * i] for i in range(3))
        g_max, g_nmax, g_sum, g_inv = (arena_small[:, 600 + 16 * i:616 + 16 * i] for i in range(4))
        yg_gain = buf(B_LHS, 0, D)
        yg_ss, yg_var, yg_rstd = (arena_small[:, 670 + 2 * i:672 + 2 * i] for i in range(3))
        (blk_params, kv_evac, dt_read, conv2_done, xc_done, qg_evac, z_evac, gate_evac, dt_neg, dt_exp, dt_ln, a_exp,
         adt_ready, qk_roped, qk_turned, qk_in, cb_mm, cb_in, xs_turned, xs_in, xd_f_ready, xd_b_ready) = (
            sem(n) for n in ("blk_params", "kv_evac", "dt_read", "conv2_done", "xc_done", "qg_evac", "z_evac",
                             "gate_evac", "dt_neg", "dt_exp", "dt_ln", "a_exp", "adt_ready", "qk_roped", "qk_turned",
                             "qk_in", "cb_mm", "cb_in", "xs_turned", "xs_in", "xd_f_ready", "xd_b_ready"))
        (carry_mm, carry_ready, carried, off_mm, off_scaled, lhs_ready, seg_mm, e_ready, m_ready, ssd_mm, dx_ready, yz_ready, yn_ready, yg_gain_landed, ssd_rows,
         attn_gated, mix_ready) = (
            sem(n) for n in ("carry_mm", "carry_ready", "carried", "off_mm", "off_scaled", "lhs_ready", "seg_mm", "e_ready", "m_ready", "ssd_mm", "dx_ready", "yz_ready", "yn_ready",
                             "yg_gain_landed", "ssd_rows", "attn_gated", "mix_ready"))
        B_MIX, B_T2, B_DX, B_GATED = 11, 10, 3, 3
        S_BANK = (0, 1, 6, 7)

        def block_pe(pe):
            h2 = chan2(B_H, B_H_LO)

            def tile(k, a):
                return both(h2, slice(None), k, slice(a * P, (a + 1) * P))

            for a in range(NT):
                xn_turn(pe, XN_OF[4] + a, a)
            turned_out(pe, TURN_PRE4)
            for s in range(2):
                w = [v[:, 0:4 * 288].rearrange("p (k n) -> p k n", n=288) for v in split_weights(pe, FIRST["kvdt"] + s)]
                for kk in range(4):
                    k = 4 * s + kk
                    for a in range(NT):
                        mm = product(bank[2 + a][:, 0:288], tile(k, a), both(w, slice(None), kk), k == 0, k == DC - 1)
                mm.then_inc(slot_done, 1)
            for s in range(6):
                w = [v.rearrange("p (k n) -> p k n", n=T) for v in split_weights(pe, FIRST["xbc"] + s)]
                if s >= 4:
                    pe.wait_ge(conv2_done, 2 * (s - 3))
                for n in range(2):
                    for k in range(DC):
                        mm = product(bank[4 + s % 4][:, n * T:(n + 1) * T], both(w, slice(None), k, slice(n * P, (n + 1) * P)),
                                     both(h2, slice(None), k), k == 0, k == DC - 1)
                mm.then_inc(slot_done, 1)
            for s in range(2):
                w = [v.rearrange("p (k n) -> p k n", n=HALF) for v in split_weights(pe, FIRST["q"] + s)]
                for kk in range(4):
                    k = 4 * s + kk
                    for a in range(NT):
                        mm = product(bank[a][:, :], tile(k, a), both(w, slice(None), kk), k == 0, k == DC - 1)
                mm.then_inc(slot_done, 1)
            pe.wait_ge(conv2_done, XC)
            wide2(pe, FIRST["z"], 4, h2, 4)
            for g in range(2):
                if g == 0:
                    pe.wait_ge(qg_evac, NT)
                    pe.wait_ge(dt_read, 1)
                else:
                    pe.wait_ge(z_evac, 4)
                wide2(pe, FIRST["gates"] + 4 * g, 4, h2, 4 * g)
            pe.wait_ge(xc_done, XC)
            pe.wait_ge(gate_evac, 8)
            for g in range(2):
                for b in range(NT):
                    mm = nc.tensor.matmul(bank[g][:, b * T:(b + 1) * T], xcT[:, 8 + g, b * P:(b + 1) * P], xcT[:, 10 + g, :],
                                          start=True, stop=True)
                mm.then_inc(cb_mm, 1)
            for j in range(4):
                for i in range(4):
                    a, c = j // 2, 4 * (j % 2) + i
                    mm = nc.tensor.transpose(bank[2 + j][:, i * P:(i + 1) * P], xcT[:, c, a * P:(a + 1) * P], ident)
                mm.then_inc(xs_turned, 1)
            pe.wait_ge(qk_roped, NT)
            for a in range(NT):
                for j in range(GJ):
                    nc.tensor.transpose(bank[6 + j // 2][:, (j % 2) * T + a * P:(j % 2) * T + (a + 1) * P], qr[:, a, j * P:(j + 1) * P], ident)
            pe.wait_ge(cb_in, 2)
            for a in range(NT):
                mm = nc.tensor.transpose(bank[0][:, a * P:(a + 1) * P], qr[:, a, GH * N:HD], ident)
            mm.then_inc(qk_turned, 1)

            def scores(i):
                j, g = i // GKV, i % GKV
                if i >= 4:
                    pe.wait_ge(sm_exp, H + i - 3)
                for a in range(NT):
                    mm = nc.tensor.matmul(bank[S_BANK[i % 4]][:, a * T:(a + 1) * T], qgT[g * N:(g + 1) * N, j, a * P:(a + 1) * P],
                                          kgT[g * N:(g + 1) * N, :], start=True, stop=True)
                mm.then_inc(s_mm, 1)

            def turn_p(i):
                pe.wait_ge(p_ready, H + i + 1)
                if i >= 2:
                    pe.wait_ge(pt_evac, H + i - 1)
                for b in range(NT):
                    for a in range(NT):
                        mm = nc.tensor.transpose(bank[2 + i % 2][:, b * T + a * P:b * T + (a + 1) * P],
                                                 gp_buf[i % 3][:, a * T + b * P:a * T + (b + 1) * P], ident)
                mm.then_inc(pt_mm, 1)

            def values(i):
                j, g = i // GKV, i % GKV
                pe.wait_ge(pt_evac, H + i + 1)
                for b in range(NT):
                    mm = nc.tensor.matmul(bank[4 + j // 2][g * N:(g + 1) * N, (j % 2) * T:(j % 2 + 1) * T],
                                          vg[:, b, g * N:(g + 1) * N], gpt_buf[i % 2][:, b * T:(b + 1) * T],
                                          start=(b == 0), stop=(b == NT - 1))
                mm.then_inc(pv_mm, 1)

            pe.wait_ge(qk_in, 3)
            pe.wait_ge(xs_in, 4)
            for i in range(3):
                scores(i)
            for i in range(GH):
                if i >= 2:
                    values(i - 2)
                if i + 3 < GH:
                    scores(i + 3)
                turn_p(i)
            values(GH - 2)
            values(GH - 1)
            pe.wait_ge(ot_in, 4 + 2)

            pe.wait_ge(adt_ready, 1)
            pe.wait_ge(pt_evac, H + GH)
            for i, (mask, cells) in enumerate((("after", adt[:, 0, 0:H]), ("upto", adt[:, 1, 0:H]),
                                               ("before", adt[:, 1, H:2 * H]), ("from", adt[:, 0, H:2 * H]))):
                mm = nc.tensor.matmul(bank[2][:, i * H:(i + 1) * H], const(mask), cells, start=True, stop=True)
            mm.then_inc(carry_mm, 1)
            pe.wait_ge(xd_f_ready, 1)
            pe.wait_ge(xd_b_ready, 1)
            xf, xb = toks(B_XF), toks(B_XB)

            def segments(h):
                pe.wait_ge(lhs_ready, h + 1)
                if h >= 2:
                    pe.wait_ge(e_ready, h - 1)
                for n, right in enumerate(("upto", "upto", "from", "from")):
                    mm = nc.tensor.matmul(bank[h % 2][:, n * P:(n + 1) * P], seg_lhs[h % 2][:, n, :], const(right), start=True, stop=True)
                mm.then_inc(seg_mm, 1)

            def mix_tokens(h):
                pe.wait_ge(m_ready, h + 1)
                hv = slice(h * N, (h + 1) * N)
                for a in range(NT):
                    for i, xd in enumerate((xf, xb)):
                        mm = nc.tensor.matmul(bank[4 + 2 * a + h // 8][:, (h % 8) * N:(h % 8 + 1) * N],
                                              e_buf[h % 3][:, (2 * i + a) * P:(2 * i + a + 1) * P], xd[:, a, hv],
                                              start=(i == 0), stop=(i == 1))
                mm.then_inc(ssd_mm, 1)

            def carry(d):
                pe.wait_ge(carried, d + 1)
                if d == 0:
                    pe.wait_ge(carry_ready, 1)
                else:
                    pe.wait_ge(off_scaled, 2)
                for g in range(2):
                    nc.tensor.matmul(bank[2 + g][:, :], cb[g][:, 4 + d, :], buf(B_P, d * D + g * HALF, d * D + (g + 1) * HALF),
                                     start=True, stop=True).then_inc(off_mm, 1)

            for h in range(H):
                segments(h)
                if h >= 2:
                    mix_tokens(h - 2)
                if h == 5:
                    carry(0)
                if h == 9:
                    carry(1)
            mix_tokens(H - 2)
            mix_tokens(H - 1)
            pe.wait_ge(e_ready, H)
            pe.wait_ge(off_scaled, 4)
            wide2(pe, FIRST["attn_proj"], 2, chan2(B_OT, B_OT_LO), 0)
            pe.wait_ge(attn_gated, 4)

            def y_turn(a):
                pe.wait_ge(yn_ready, a + 1)
                turn_pe(toks(B_Y)[:, a, :], 0, a)

            def mix_turn(a):
                pe.wait_ge(mix_ready, a + 1)
                turn_pe(toks(B_MIX)[:, a, :], 0, a)

            wide2(pe, FIRST["ssd_proj"], 4, chan2(B_SQ, B_SQ_LO), 4, TURN_SSD, y_turn, told=ssd_rows)
            wide2(pe, FIRST["w_out"], 4, chan2(B_T2, B_T2_LO), 4, TURN_MIX, mix_turn, rows=True)

        def block_act(act):
            ahead(act, FIRST["xbc"] + 1, split_act)
            after_slots(act, "kvdt")
            for a in range(NT):
                nc.scalar.activation(qk[:, a, GH * N:HD], bank[2 + a][:, 0:P], ACT.Copy)
                nc.scalar.activation(vg[:, a, :], bank[2 + a][:, P:2 * P], ACT.Copy).then_inc(kv_evac, 1)
            ahead(act, FIRST["xbc"] + AHEAD, split_act)
            for c in range(XC):
                act.wait_ge(conv2_done, c + 1)
                nc.scalar.activation(xcT[:, c, :], xc_acc[c % 4], ACT.Silu).then_inc(xc_done, 1)
                if c % 2 == 1:
                    ahead(act, FIRST["xbc"] + c // 2 + 1 + AHEAD, split_act)
            ahead(act, LAST["q"] + 2, split_act)
            after_slots(act, "q")
            for a in range(NT):
                nc.scalar.activation(qk[:, a, 0:GH * N].rearrange("p (j g d) -> p g j d", g=GKV, d=N),
                                     bank[a][:, :].rearrange("p (g j d) -> p g j d", g=GKV, d=N), ACT.Copy).then_inc(qg_evac, 1)
            act.wait_ge(qg_evac, NT)
            act.wait_ge(kv_evac, NT)
            nc.scalar.activation(buf(B_P, 0, NT * HD), buf(B_QK, 0, NT * HD), ACT.Square).then_inc(squared, 1)
            ahead(act, LAST["z"] + AHEAD, split_act)
            after_slots(act, "z")
            for j in range(4):
                nc.scalar.activation(buf(B_Z, j * HALF, (j + 1) * HALF), bank[4 + j][:, :], ACT.Silu).then_inc(z_evac, 1)
            for g, dst in enumerate((B_GA, B_GS)):
                ahead(act, FIRST["gates"] + 4 * g + 3 + AHEAD, split_act)
                after_slots(act, "gates", 4 * (g + 1))
                for j in range(4):
                    nc.scalar.activation(buf(dst, j * HALF, (j + 1) * HALF), bank[4 * g + j][:, :], ACT.Sigmoid).then_inc(gate_evac, 1)
            act.wait_ge(blk_params, 16 * 7)
            nc.scalar.activation(a_log[:, 0, :], a_log[:, 0, :], ACT.Exp).then_inc(a_exp, 1)
            act.wait_ge(dt_neg, 1)
            nc.scalar.activation(dt_e, dt_n, ACT.Exp).then_inc(dt_exp, 1)
            act.wait_ge(dt_exp, 1)
            nc.scalar.activation(dt_l, dt_e, ACT.Ln, bias=1.0).then_inc(dt_ln, 1)
            for j in range(4):
                act.wait_ge(xs_turned, j + 1)
                nc.scalar.activation(buf(B_XS, j * HALF, (j + 1) * HALF), bank[2 + j][:, :], ACT.Copy).then_inc(xs_in, 1)

            def exps(i):
                act.wait_ge(sm_max, H + i + 1)
                if i >= 3:
                    act.wait_ge(pt_mm, H + i - 2)
                for a in range(NT):
                    op = nc.scalar.activation(gp_buf[i % 3][:, a * T:(a + 1) * T], bank[S_BANK[i % 4]][:, a * T:(a + 1) * T], ACT.Exp,
                                              bias=g_nmax[:, 2 * i + a:2 * i + a + 1], scale=GQA_SCALE,
                                              accum_out=g_sum[:, 2 * i + a:2 * i + a + 1])
                op.then_inc(sm_exp, 1)

            def evac(i):
                act.wait_ge(pt_mm, H + i + 1)
                if i >= 2:
                    act.wait_ge(pv_mm, H + i - 1)
                nc.scalar.activation(gpt_buf[i % 2], bank[2 + i % 2][:, :], ACT.Copy).then_inc(pt_evac, 1)

            for i in range(GH):
                exps(i)
                if i >= 1:
                    evac(i - 1)
            evac(GH - 1)
            for b in range(2):
                act.wait_ge(pv_mm, H + 4 * (b + 1))
                nc.scalar.activation(buf(B_OT, b * HALF, (b + 1) * HALF, arena12), bank[4 + b][:, :], ACT.Copy).then_inc(ot_hi, 1)
            act.wait_ge(carry_mm, 1)
            nc.scalar.activation(carry_decay, bank[2][:, 0:4 * H], ACT.Exp).then_inc(carry_ready, 1)
            for h in range(H):
                if h == 12:
                    ahead(act, FIRST["ssd_proj"] + 1, split_act)
                act.wait_ge(seg_mm, h + 1)
                if h >= 3:
                    act.wait_ge(ssd_mm, h - 2)
                nc.scalar.activation(e_buf[h % 3], bank[h % 2][:, :], ACT.Exp).then_inc(e_ready, 1)
            for a in range(NT):
                act.wait_ge(yz_ready, a + 1)
                nc.scalar.activation(buf(B_SQ, a * D, (a + 1) * D), toks(B_Y)[:, a, :], ACT.Square, scale=MEAN,
                                     accum_out=yg_ss[:, a:a + 1]).then_inc(squared, 1)
            for a in range(NT):
                turn_act(act, TURN_SSD, a, 0, B_SQ)
            ahead(act, LAST["ssd_proj"] + AHEAD - 1, split_act)
            for a in range(NT):
                turn_act(act, TURN_MIX, a, 0, B_T2)
            ahead(act, LAST["w_out"], split_act)

        def block_dve(dve):
            ahead(dve, FIRST["xbc"], split_dve)
            emitted[dve] = LAST["z"] + 1
            dve.wait_ge(blk_params, 16 * 7)
            dve.wait_ge(kv_evac, NT)
            for a in range(NT):
                op = nc.vector.tensor_tensor(dt_x[:, a, :], bank[2 + a][:, 2 * P:2 * P + 32], dt_bias[:, 0, :], ALU.add)
            op.then_inc(dt_read, 1)
            dve.wait_ge(dt_read, 1)
            nc.vector.scalar_tensor_tensor(dt_n, dt_x, -1.0, dt_x, ALU.mult, ALU.min).then_inc(dt_neg, 1)
            for c in range(XC):
                u = bank[4 + (c // 2) % 4][:, (c % 2) * T:(c % 2 + 1) * T]
                acc = xc_acc[c % 4]
                after_slots(dve, "xbc", c // 2 + 1)
                if c >= 4:
                    dve.wait_ge(xc_done, c - 3)
                link(dve, nc.vector.tensor_scalar(acc, u, col("conv_w_2", 2 * XC + c), col("conv_b_2", c), ALU.mult, ALU.add))
                for j in (0, 1, 3, 4):
                    shift = j - 2
                    dst = slice(max(0, -shift), T - max(0, shift))
                    src = slice(max(0, shift), T - max(0, -shift))
                    op = nc.vector.scalar_tensor_tensor(acc[:, dst], u[:, src], col("conv_w_2", j * XC + c), acc[:, dst],
                                                        ALU.mult, ALU.add)
                    if j < 4:
                        link(dve, op)
                op.then_inc(conv2_done, 1)
            dve.wait_ge(squared, 8 + 1)
            nh = GH + GKV
            link(dve, nc.vector.tensor_reduce(qk_ss, buf(B_P, 0, NT * HD).rearrange("p (h n) -> p h n", n=N), AX, ALU.add))
            nc.vector.tensor_scalar(qk_var, qk_ss, 1.0 / N, EPS, ALU.mult, ALU.add).then_inc(var_ready, 1)
            dve.wait_ge(rstd_ready, 4 + 1)
            qk_flat = buf(B_QK, 0, NT * HD).rearrange("p (h n) -> p h n", n=N)
            link(dve, nc.vector.tensor_tensor(qk_flat, qk_flat, spread(qk_rstd.unsqueeze(2), [P, NT * nh, N]), ALU.mult))
            link(dve, nc.vector.tensor_tensor(qk, qk, spread(qk_gain.unsqueeze(1), [P, NT, HD]), ALU.mult))
            for a in range(NT):
                src = qk[:, a, :].rearrange("p (h r n) -> p h r n", r=2, n=32)
                dst = qr[:, a, :].rearrange("p (h r n) -> p h r n", r=2, n=32)
                t0, t1 = (x.rearrange("p (h r n) -> p h r n", r=2, n=16) for x in rot_tmp)
                cos, sin = (spread(const(n, a * 32, (a + 1) * 32).rearrange("p (r n) -> p r n", r=2).unsqueeze(1),
                                   [P, nh, 2, 16]) for n in ("acos", "asin"))
                x1, x2 = src[:, :, :, 0:16], src[:, :, :, 16:32]
                for lo, f1, f2, op in ((0, cos, sin, ALU.subtract), (16, sin, cos, ALU.add)):
                    nc.vector.tensor_tensor(t0, x1, f1, ALU.mult)
                    link(dve, nc.vector.tensor_tensor(t1, x2, f2, ALU.mult))
                    last = nc.vector.tensor_tensor(dst[:, :, :, lo:lo + 16], t0, t1, op)
                    if lo == 0:
                        link(dve, last)
                last.then_inc(qk_roped, 1)
                dve.wait_ge(qk_roped, a + 1)
            dve.wait_ge(split_ready, LAST["z"] - SPLIT0 + 1)
            ahead(dve, LAST["gates"] + AHEAD, split_dve)
            dve.wait_ge(dt_ln, 1)
            dve.wait_ge(a_exp, 1)
            link(dve, nc.vector.scalar_tensor_tensor(dt, dt_x, 0.0, dt_l, ALU.max, ALU.add))
            for a in range(NT):
                op = nc.vector.scalar_tensor_tensor(adt[:, a, :], a_log[:, 0, :], -1.0, dt[:, a, :], ALU.mult, ALU.mult)
            op.then_inc(adt_ready, 1)
            for g in range(2):
                dve.wait_ge(cb_mm, g + 1)
                blocks = bank[g][:, :].rearrange("p (n l) -> p n l", l=P)
                for i, mask in ((0, "upto"), (2, "from")):
                    nc.vector.tensor_tensor(cb[g][:, i:i + 2, :], blocks[:, 0:4:3, :],
                                            spread(const(mask).unsqueeze(1), [P, 2, P]), ALU.mult)
                nc.vector.tensor_copy(cb[g][:, 4:6, :], blocks[:, 1:3, :]).then_inc(cb_in, 1)
            dve.wait_ge(qk_turned, 1)
            nc.vector.tensor_copy(buf(B_QT, 0, HALF), bank[6][:, :]).then_inc(qk_in, 1)
            nc.vector.tensor_copy(buf(B_QT, HALF, 2 * HALF), bank[7][:, :]).then_inc(qk_in, 1)
            nc.vector.tensor_copy(kgT, bank[0][:, 0:T]).then_inc(qk_in, 1)
            dve.wait_ge(xs_in, 4)
            nc.vector.tensor_tensor(toks(B_XB).rearrange("p a (h n) -> p a h n", n=N), toks(B_XS).rearrange("p a (h n) -> p a h n", n=N),
                                    spread(dt[:, :, H:2 * H].unsqueeze(3), [P, NT, H, N]), ALU.mult).then_inc(xd_b_ready, 1)

            def left_sides(h):
                if h >= 2:
                    dve.wait_ge(seg_mm, h - 1)
                l = seg_lhs[h % 2]
                f, b = adt[:, :, h:h + 1], adt[:, :, H + h:H + h + 1]
                for n, (mask, c) in enumerate((("after", f[:, 0]), ("after", f[:, 1]), ("before", b[:, 0]), ("before", b[:, 1]))):
                    op = nc.vector.tensor_scalar(l[:, n, :], const(mask), c, None, ALU.mult)
                op.then_inc(lhs_ready, 1)

            dve.wait_ge(adt_ready, 1)
            left_sides(0)

            def maxima(i):
                dve.wait_ge(s_mm, H + i + 1)
                link(dve, nc.vector.tensor_reduce(g_max[:, 2 * i:2 * i + 2], bank[S_BANK[i % 4]][:, :].rearrange("p (a t) -> p a t", t=T),
                                                  AX, ALU.max))
                nc.vector.tensor_scalar(g_nmax[:, 2 * i:2 * i + 2], g_max[:, 2 * i:2 * i + 2], -GQA_SCALE, None,
                                        ALU.mult).then_inc(sm_max, 1)

            def normalize(i):
                dve.wait_ge(sm_exp, H + i + 1)
                link(dve, nc.vector.reciprocal(g_inv[:, 2 * i:2 * i + 2], g_sum[:, 2 * i:2 * i + 2]))
                for a in range(NT):
                    p = gp_buf[i % 3][:, a * T:(a + 1) * T]
                    op = nc.vector.tensor_scalar(p, p, g_inv[:, 2 * i + a:2 * i + a + 1], None, ALU.mult)
                op.then_inc(p_ready, 1)

            for i in range(GH):
                maxima(i)
                if i >= 1:
                    normalize(i - 1)
            normalize(GH - 1)
            for b in range(2):
                dve.wait_ge(ot_hi, 4 + b + 1)
                at = slice(b * HALF, (b + 1) * HALF)
                nc.vector.tensor_tensor(buf(B_OT_LO, mem=arena12)[:, at], bank[4 + b][:, :], buf(B_OT, mem=arena12)[:, at].bitcast(F32), ALU.subtract).then_inc(ot_in, 1)

            def matrices(h):
                dve.wait_ge(e_ready, h + 1)
                nc.vector.tensor_tensor(e_buf[h % 3], e_buf[h % 3], buf(B_CB, (h // 8) * 768, (h // 8) * 768 + HALF),
                                        ALU.mult).then_inc(m_ready, 1)

            def carried_on(d):
                for g in range(2):
                    dve.wait_ge(off_mm, 2 * d + g + 1)
                    decay = carry_decay[:, (2 * d + 1) * H + 8 * g:(2 * d + 1) * H + 8 * (g + 1)]
                    nc.vector.tensor_tensor(buf(B_P, d * D + g * HALF, d * D + (g + 1) * HALF).rearrange("p (h n) -> p h n", n=N),
                                            bank[2 + g][:, :].rearrange("p (h n) -> p h n", n=N),
                                            spread(decay.unsqueeze(2), [P, 8, N]), ALU.mult).then_inc(off_scaled, 1)

            for h in range(H):
                if h + 1 < H:
                    left_sides(h + 1)
                matrices(h)
                if h in (7, 11):
                    carried_on(h // 4 - 1)
                if h == 13:
                    ahead(dve, FIRST["ssd_proj"] + 1, split_dve)
            dve.wait_ge(ssd_mm, H)
            dve.wait_ge(dx_ready, 1 + NT)
            y = toks(B_Y)
            for a in range(NT):
                for q in range(2):
                    cells = slice(q * HALF, (q + 1) * HALF)
                    op = nc.vector.tensor_tensor(y[:, a, cells], bank[4 + 2 * a + q][:, :], toks(B_DX)[:, a, cells], ALU.add)
                link(dve, op)
                nc.vector.tensor_tensor(y[:, a, :], y[:, a, :], toks(B_Z)[:, a, :], ALU.mult).then_inc(yz_ready, 1)
            for a in range(NT):
                dve.wait_ge(squared, 9 + a + 1)
                nc.vector.tensor_scalar(yg_var[:, a:a + 1], yg_ss[:, a:a + 1], EPS, None, ALU.add).then_inc(var_ready, 1)
            dve.wait_ge(yg_gain_landed, 16)
            for a in range(NT):
                dve.wait_ge(rstd_ready, 5 + a + 1)
                nc.vector.scalar_tensor_tensor(y[:, a, :], y[:, a, :], yg_rstd[:, a:a + 1], yg_gain, ALU.mult,
                                               ALU.mult).then_inc(yn_ready, 1)
            after_slots(dve, "attn_proj")
            for j in range(4):
                nc.vector.tensor_tensor(buf(B_MIX, j * HALF, (j + 1) * HALF), bank[j][:, :], buf(B_GA, j * HALF, (j + 1) * HALF),
                                        ALU.mult).then_inc(attn_gated, 1)
            for a in range(NT):
                turn_dve(dve, TURN_SSD, a, 0, B_SQ, B_SQ_LO)
            ahead(dve, LAST["ssd_proj"] + AHEAD - 1, split_dve)
            dve.wait_ge(attn_gated, 4)
            for a in range(NT):
                if a == 0:
                    dve.wait_ge(ssd_rows, 1)
                else:
                    after_slots(dve, "ssd_proj")
                for half in range(2):
                    j = 2 * a + half
                    op = nc.vector.tensor_tensor(buf(B_GATED, j * HALF, (j + 1) * HALF), bank[4 + j][:, :],
                                                 buf(B_GS, j * HALF, (j + 1) * HALF), ALU.mult)
                link(dve, op)
                nc.vector.tensor_tensor(toks(B_MIX)[:, a, :], toks(B_MIX)[:, a, :], toks(B_GATED)[:, a, :], ALU.add).then_inc(mix_ready, 1)
            for a in range(NT):
                turn_dve(dve, TURN_MIX, a, 0, B_T2, B_T2_LO)
            ahead(dve, LAST["w_out"], split_dve)

        def block_params_sp(sp):
            sp.wait_ge(x_updated, 4 * 4)
            gain = qk_gain.rearrange("p (h n) -> p h n", n=N)
            sp.dma_start(gain[:, 0:GH, :], spread(A["q_norm_2"][0].partition_broadcast(P).unsqueeze(1), [P, GH, N])).then_inc(blk_params, 16)
            sp.dma_start(gain[:, GH:, :], spread(A["k_norm_2"][0].partition_broadcast(P).unsqueeze(1), [P, GKV, N])).then_inc(blk_params, 16)
            for dst, names in ((dt_bias, ("dt_bias_f_2", "dt_bias_b_2")), (a_log, ("a_log_f_2", "a_log_b_2"))):
                for i, name in enumerate(names):
                    sp.dma_start(dst[:, 0, i * H:(i + 1) * H], A[name][0].partition_broadcast(P)).then_inc(blk_params, 16)
            sp.dma_start(d_skip, A["d_skip_2"][0].partition_broadcast(P)).then_inc(blk_params, 16)

        def block_pool(pool):
            pool.wait_ge(split_ready, FIRST["xbc"] - SPLIT0 + 1)
            for n in range(FIRST["xbc"] + 1, FIRST["z"] + 2):
                split_lo(pool, nc.gpsimd, n)
            pool.wait_ge(var_ready, 4 + 1)
            nc.gpsimd.tensor_tensor(qk_rstd, qk_var, minus_half[:, 0:NT * (GH + GKV)], ALU.pow).then_inc(rstd_ready, 1)
            for n in range(FIRST["z"] + 2, LAST["z"] + 1):
                split_lo(pool, nc.gpsimd, n)
            pool.wait_ge(adt_ready, 1)
            pool.wait_ge(xs_in, 4)
            xs = toks(B_XS).rearrange("p a (h n) -> p a h n", n=N)
            nc.gpsimd.tensor_tensor(toks(B_XF).rearrange("p a (h n) -> p a h n", n=N), xs,
                                    spread(dt[:, :, 0:H].unsqueeze(3), [P, NT, H, N]), ALU.mult).then_inc(xd_f_ready, 1)
            pool.wait_ge(blk_params, 16 * 7)
            pool.wait_ge(xd_b_ready, 1)
            nc.gpsimd.tensor_tensor(xs, xs, spread(d_skip.unsqueeze(1).unsqueeze(3), [P, NT, H, N]), ALU.mult).then_inc(dx_ready, 1)
            pool.wait_ge(carry_ready, 1)
            pool.wait_ge(xd_f_ready, 1)
            pool.wait_ge(ot_in, 4 + 2)
            for d, xd in enumerate((toks(B_XF)[:, 0, :], toks(B_XB)[:, 1, :])):
                nc.gpsimd.tensor_tensor(buf(B_P, d * D, (d + 1) * D).rearrange("p (h n) -> p h n", n=N),
                                        xd.rearrange("p (h n) -> p h n", n=N),
                                        spread(carry_decay[:, 2 * d * H:(2 * d + 1) * H].unsqueeze(2), [P, H, N]),
                                        ALU.mult).then_inc(carried, 1)
            pool.wait_ge(dx_ready, 1)
            for d in range(2):
                pool.wait_ge(off_scaled, 2 * (d + 1))
                dx = toks(B_DX)[:, 1 - d, :]
                nc.gpsimd.tensor_tensor(dx, dx, buf(B_P, d * D, (d + 1) * D), ALU.add).then_inc(dx_ready, 1)
            pool.wait_ge(seg_mm, H)
            pool.dma_start(yg_gain, A["ssd_norm_2"][0].partition_broadcast(P)).then_inc(yg_gain_landed, 16)
            for a in range(NT):
                pool.wait_ge(var_ready, 5 + a + 1)
                nc.gpsimd.tensor_tensor(yg_rstd[:, a:a + 1], yg_var[:, a:a + 1], minus_half[:, 0:1], ALU.pow).then_inc(rstd_ready, 1)

        def weights_sp(sp):
            def into(n, width=SLOT):
                if n >= RING:
                    sp.wait_ge(slot_done, n - RING + 1)
                return ring[:, n % RING, 0:width]

            def send(n, dst, src):
                sp.dma_start(dst, src).then_inc(landed[n % RING], 16)

            def rows_of(name, w, chunks):
                count = {k: c for k, c, _ in PLAN}[name]
                for s in range(count):
                    n = FIRST[name] + s
                    dst = into(n, chunks * w.shape[1]).rearrange("p (k n) -> p k n", k=chunks)
                    send(n, dst, w[s * chunks * P:(s + 1) * chunks * P, :].rearrange("(k p) n -> p k n", p=P))

            def columns_of(name, w, width):
                chunks = w.shape[0] // P
                for s in range({k: c for k, c, _ in PLAN}[name]):
                    n = FIRST[name] + s
                    dst = into(n, chunks * width).rearrange("p (k n) -> p k n", k=chunks)
                    send(n, dst, w[:, s * width:(s + 1) * width].rearrange("(k p) n -> p k n", p=P))

            def ffn(f, w_in, w_out):
                src = w_in.rearrange("(k p) (g n) -> p k g n", p=P, g=2)
                first = FIRST[f"ffn_in{f}"]

                def tile(it, j):
                    r = (first + j) % RING
                    sp.wait_ge(slot_done, it * RING + (first + j - RING + 1))
                    at = slice((it * RING + j) * P, (it * RING + j + 1) * P) if isinstance(it, int) else bass.ds(it * (RING * P) + j * P, P)
                    dst = ring[:, r, :].rearrange("p (k g n) -> p k g n", k=DC, g=2)
                    for g in range(2):
                        sp.dma_start(dst[:, :, g, :], src[:, :, g, at]).then_inc(landed[r], 16)

                rounds(sp, tile)
                for s in range(FC // 2):
                    n = FIRST[f"ffn_out{f}"] + s
                    dst = into(n).rearrange("p (k n) -> p k n", k=2)
                    for k in range(2):
                        send(n, dst[:, k, :], w_out[(2 * s + k) * P:(2 * s + k + 1) * P, :])

            n = FIRST["lora_wa"]
            dst = into(n, 2 * DC * 64).rearrange("p (g k n) -> p g k n", g=2, k=DC)
            for g, w in enumerate(("a_w1", "a_a1")):
                send(n, dst[:, g], A[w][0].rearrange("(k p) n -> p k n", p=P))
            columns_of("w_k", A["a_w_rkv"][0, 1], T)
            n = FIRST["lora_wa2"]
            dst = into(n)
            for g, w in enumerate(("a_w2", "a_a2")):
                send(n, dst[0:64, g * D:(g + 1) * D], A[w][0])
            columns_of("w_r", A["a_w_rkv"][0, 0], T)
            columns_of("lora_g", A["a_g1"][0], GATE_LORA)
            n = FIRST["lora_g2"]
            dst = into(n)
            send(n, dst[:, 0:D], A["a_g2"][0, 0:P])
            send(n, dst[0:GATE_LORA - P, D:2 * D], A["a_g2"][0, P:GATE_LORA])
            rows_of("w_v", A["a_w_rkv"][0, 2], 2)
            rwkv_blocks_sp(sp)
            rows_of("w_o", A["a_w_o"][0], 2)
            ffn(0, A["ffn_w_in"][0], A["ffn_w_out"][0])
            rows_of("kv_down", A["kv_w_down"], 4)
            rows_of("q_down", A["q_w_down"][0], 4)
            columns_of("kv_up", A["kv_w_up"], D)
            columns_of("q_up", A["q_w_up"][0], 4 * QK)
            rows_of("o_w", A["o_w"][0], 2)
            ffn(1, A["ffn_w_in"][1], A["ffn_w_out"][1])
            w_in = A["w_in_2"][0]
            at_z = GH * N + 2 * GKV * N
            at_x = at_z + D
            at_dt = at_x + XC * P
            at_g = at_dt + 2 * H
            for s in range(2):
                n = FIRST["kvdt"] + s
                dst = into(n, 4 * 288).rearrange("p (k n) -> p k n", k=4)
                part = w_in[s * HALF:(s + 1) * HALF, :].rearrange("(k p) n -> p k n", p=P)
                send(n, dst[:, :, 0:2 * P], part[:, :, GH * N:at_z])
                send(n, dst[:, :, 2 * P:288], part[:, :, at_dt:at_g])
            block_params_sp(sp)
            columns_of("xbc", w_in[:, at_x:at_dt], T)
            rows_of("q", w_in[:, 0:GH * N], 4)
            rows_of("z", w_in[:, at_z:at_x], 2)
            for g in range(2):
                for s in range(4):
                    n = FIRST["gates"] + 4 * g + s
                    send(n, into(n).rearrange("p (k n) -> p k n", k=2),
                         w_in[s * T:(s + 1) * T, at_g + g * D:at_g + (g + 1) * D].rearrange("(k p) n -> p k n", p=P))
            proj = A["w_attn_proj_2"][0].rearrange("(g j d) n -> g d j n", g=GKV, j=GJ)
            for s in range(2):
                n = FIRST["attn_proj"] + s
                dst = into(n).rearrange("p (k n) -> p k n", k=2)
                for g in range(GKV):
                    send(n, dst[g * N:(g + 1) * N], proj[g, :, 2 * s:2 * s + 2, :])
            rows_of("ssd_proj", A["w_ssd_proj_2"][0], 2)
            rows_of("w_out", A["w_out_2"][0], 2)
            ffn(2, A["w_gate_up_2"][0], A["w_down_2"][0])

        BETWEEN = [[(TURN_PRE1, 4, FFN_H, FFN_H_LO, None, XN)],
                   [(TURN_XKV, 4, M_XKV, M_XKV_LO, buf(GAIN_KV, 0, D), XN_KV), (TURN_PRE2, 0, M_H, M_H_LO, None, XN)],
                   [(TURN_PRE3, 4, FFN_H, FFN_H_LO, None, XN)], [(TURN_PRE4, 4, B_H, B_H_LO, None, XN)],
                   [(TURN_PRE5, 4, FFN_H, FFN_H_LO, None, XN)]]

        block = ctx.enter_context(nc.Block())

        @block.sync
        def _(sp):
            start_sp(sp)
            weights_sp(sp)
            for a in range(NT):
                sp.wait_ge(x_updated, 4 * 5 + 2 * (a + 1))
                sp.dma_start(out[0, a * P:(a + 1) * P, :], x_sb[:, a, :]).then_inc(out_stored, 16)
            sp.wait_ge(out_stored, 16 * NT)

        @block.gpsimd
        def _(pool):
            start_pool(pool)
            for a in range(NT):
                pre_root(pool, 0, a)
            load_gains(pool, 0, A["norm_g"][0, 1], A["norm_g"][0, 2])
            pool.wait_ge(const_landed, 16)
            rwkv_pool(pool)
            between_pool(pool, 0)
            load_gains(pool, 1, A["norm_g"][0, 3], A["norm_g"][1, 0])
            pool.dma_start(buf(GAIN_KV, 0, D), A["kv_norm_g"].partition_broadcast(P)).then_inc(kv_gain_landed, 16)
            ffn_pool(pool, 0)
            between_pool(pool, 1)
            load_gains(pool, 2, A["norm_g"][1, 1], A["norm_g"][1, 2])
            mla_pool(pool)
            between_pool(pool, 2)
            load_gains(pool, 3, A["norm_g"][1, 3], A["norm1_pre_2"][0])
            ffn_pool(pool, 1)
            between_pool(pool, 3)
            load_gains(pool, 4, A["norm1_post_2"][0], A["norm2_pre_2"][0])
            block_pool(pool)
            between_pool(pool, 4)
            load_gains(pool, 5, A["norm2_post_2"][0], None)
            ffn_pool(pool, 2)
            for a in range(NT):
                post_root(pool, 5, a)

        @block.tensor
        def _(pe):
            start_pe(pe)
            rwkv_pe(pe)
            ffn_pe(pe, 0, 1, TURN_PRE1)
            mla_pe(pe)
            ffn_pe(pe, 1, 3, TURN_PRE3)
            block_pe(pe)
            ffn_pe(pe, 2, 5, TURN_PRE5)

        @block.scalar
        def _(act):
            start_act(act)
            for a in range(NT):
                x_squares(act, 0, a)
            for a in range(NT):
                turn_act(act, TURN_PRE0, a, 4, W_HT)
            act.wait_ge(cols_ready, 1)
            rwkv_act(act)
            between_act(act, 0, BETWEEN[0], LAST["w_o"])
            ffn_act(act, 0)
            ahead(act, LAST["ffn_out0"], split_act)
            between_act(act, 1, BETWEEN[1], LAST["ffn_out0"])
            mla_act(act)
            between_act(act, 2, BETWEEN[2], LAST["o_w"])
            ffn_act(act, 1)
            ahead(act, LAST["ffn_out1"], split_act)
            between_act(act, 3, BETWEEN[3], LAST["ffn_out1"])
            block_act(act)
            between_act(act, 4, BETWEEN[4], LAST["w_out"])
            ffn_act(act, 2)
            ahead(act, LAST["ffn_out2"], split_act)
            for a in range(NT):
                post_squares(act, 5, a)

        @block.vector
        def _(dve):
            start_dve(dve)
            rwkv_dve(dve)
            between_dve(dve, 0, BETWEEN[0], LAST["w_o"])
            ffn_dve(dve, 0)
            ahead(dve, LAST["ffn_out0"], split_dve)
            between_dve(dve, 1, BETWEEN[1], LAST["ffn_out0"])
            mla_dve(dve)
            between_dve(dve, 2, BETWEEN[2], LAST["o_w"])
            ffn_dve(dve, 1)
            ahead(dve, LAST["ffn_out1"], split_dve)
            between_dve(dve, 3, BETWEEN[3], LAST["ffn_out1"])
            block_dve(dve)
            between_dve(dve, 4, BETWEEN[4], LAST["w_out"])
            ffn_dve(dve, 2)
            ahead(dve, LAST["ffn_out2"], split_dve)
            for a in range(NT):
                post_scale(dve, 5, a)
                x_update(dve, 5, a)


INPUTS = ["x", "norm_g", "ffn_w_in", "ffn_conv_w", "ffn_conv_b", "ffn_w_out", "a_mu", "a_w_rkv", "a_w0", "a_w1", "a_w2",
          "a_a0", "a_a1", "a_a2", "a_g1", "a_g2", "a_k_k", "a_k_a", "a_r_k", "a_lnx_w", "a_lnx_b", "a_w_o", "kv_norm_g",
          "kv_w_down", "kv_a_norm_g", "kv_w_up", "q_w_down", "q_norm_g", "q_w_up", "o_w", "w_in_2", "q_norm_2", "k_norm_2",
          "conv_w_2", "conv_b_2", "dt_bias_f_2", "dt_bias_b_2", "a_log_f_2", "a_log_b_2", "d_skip_2", "ssd_norm_2",
          "w_attn_proj_2", "w_ssd_proj_2", "w_out_2", "norm1_pre_2", "norm1_post_2", "norm2_pre_2", "norm2_post_2",
          "w_gate_up_2", "w_down_2"]


def kernel(**inputs):
    import concourse.bacc as bacc
    from concourse.bass_utils import run_bass_kernel_spmd

    nc = bacc.Bacc("TRN2", target_bir_lowering=False, num_devices=1)
    arrays, args = {}, {}
    for name in INPUTS:
        a = np.ascontiguousarray(inputs[name])
        arrays[f"in_{name}"] = a
        args[name] = nc.dram_tensor(f"in_{name}", a.shape, mybir.dt.from_np(a.dtype), kind="ExternalInput").ap()
    arrays["constants"] = np.ascontiguousarray(np.concatenate(list(CONSTANTS.values()), axis=1))
    const_dram = nc.dram_tensor("constants", (P, CONST_W), F32, kind="ExternalInput").ap()
    out = nc.dram_tensor("out", (1, T, D), F32, kind="ExternalOutput").ap()
    build(nc, args, const_dram, out)
    r = run_bass_kernel_spmd(nc, [arrays], core_ids=[0])
    return r.results[0]["out"]
```

```python
from contextlib import ExitStack

import numpy as np

import concourse.bass as bass
from concourse import mybir

F32 = mybir.dt.float32
F32R = mybir.dt.float32r
ALU = mybir.AluOpType
ACT = mybir.ActivationFunctionType
AX = mybir.AxisListType.X

P = 128
T = 256
NT = T // P
D = 1024
DC = D // P
HALF = 512
F = 2816
FC = F // P
H = 16
N = 64
HP = H // 2
NOPE, ROPE = 64, 32
QK = NOPE + ROPE
Q_LORA, KV_LORA = 384, 256
GATE_LORA = 160
GH, GKV, GJ = 8, 2, 4
XC = 12
EPS = 1e-6
LNX_EPS = 64e-5
KAPPA = float(np.exp(-0.5))
BS = 32
NB = P // BS
MLA_SCALE = float(QK) ** -0.5
GQA_SCALE = float(N) ** -0.5
NEG = -1e30

RING = 4
SLOT = 2048
ARENA = [(0, 4), (4, 5), (9, 4), (13, 5)]

PLAN = [("lora_wa", 1, 2), ("w_k", 4, 1), ("lora_wa2", 1, 2), ("w_r", 4, 1), ("lora_g", 1, 1), ("lora_g2", 1, 2),
        ("w_v", 4, 1), ("w_o", 4, 1), ("ffn_in0", FC, 2), ("ffn_out0", FC // 2, 2),
        ("kv_down", 2, 1), ("q_down", 2, 1), ("kv_up", 2, 1), ("q_up", 4, 1), ("o_w", 4, 1),
        ("ffn_in1", FC, 2), ("ffn_out1", FC // 2, 2),
        ("kvdt", 2, 2), ("xbc", 6, 1), ("q", 2, 1), ("z", 4, 1), ("gates", 8, 1),
        ("attn_proj", 2, 2), ("ssd_proj", 4, 1), ("w_out", 4, 1), ("ffn_in2", FC, 2), ("ffn_out2", FC // 2, 2)]
WIDTH = {"kv_down": 4 * 288, "q_down": 4 * Q_LORA, "q_up": 12 * QK, "kvdt": 4 * 288}
FIRST = {}
LANDED = []
SLOT_WIDTH = []
_count = [0] * RING
for _name, _n, _dmas in PLAN:
    FIRST[_name] = len(LANDED)
    for _ in range(_n):
        _r = len(LANDED) % RING
        _count[_r] += 16 * _dmas
        LANDED.append(_count[_r])
        SLOT_WIDTH.append(WIDTH.get(_name, SLOT))
LAST = {_name: FIRST[_name] + _n - 1 for _name, _n, _ in PLAN}
SPLIT_NO = {}
for _name, _n, _ in PLAN:
    if _name in ("w_k", "w_r", "w_v") or FIRST[_name] >= FIRST["w_o"]:
        for _s in range(_n):
            SPLIT_NO[FIRST[_name] + _s] = len(SPLIT_NO)
AHEAD = RING - 1

ROW_TILES = [[("norm_g", 64), ("a_mu", 48), ("a_w0", 8), ("a_a0", 8)],
             [("a_k_k", 8), ("a_k_a", 8), ("a_r_k", 8), ("kv_norm_g", 8), ("kv_a_norm_g", 2), ("q_norm_g", 3),
              ("norm1_pre_2", 8), ("norm2_pre_2", 8), ("ssd_norm_2", 8), ("conv_w_2", 60)],
             [("conv_b_2", 12), ("ffn_conv_w0", 66), ("ffn_conv_b", 44)],
             [("ffn_conv_w1", 66)]]
COL = {}
for _q, _tile in enumerate(ROW_TILES):
    _at = 0
    for _name, _n in _tile:
        COL[_name] = _q * P + _at
        _at += _n
PARAM_DMAS = sum(len(t) for t in ROW_TILES)


def constants():
    s, t = np.arange(P)[:, None], np.arange(P)[None, :]
    tok = np.arange(T, dtype=np.float32)
    inv = (1.0 / (10000.0 ** (np.arange(0, ROPE, 2, dtype=np.float32) / ROPE))).astype(np.float32)
    ang = tok[:, None] * inv[None, :]
    c, sn = np.cos(ang), np.sin(ang)
    perm = np.zeros((P, QK))
    cosT, sinT = np.zeros((P, T)), np.zeros((P, T))
    half = ROPE // 2
    for i in range(half):
        perm[NOPE + half + i, NOPE + i] = 1
        perm[NOPE + i, NOPE + half + i] = 1
        cosT[NOPE + i] = cosT[NOPE + half + i] = c[:, i]
        sinT[NOPE + i], sinT[NOPE + half + i] = -sn[:, i], sn[:, i]
    ktok = lambda a: a.reshape(NT, P, half).transpose(1, 0, 2).reshape(P, -1)
    maskb = np.where((t // 64) <= (s // 64), 0.0, NEG)
    inv2 = (10000.0 ** (-np.arange(0, 32, 2, dtype=np.float32) / 32)).astype(np.float32)
    a2 = np.stack([(tok // 64)[:, None] * inv2, (tok % 64)[:, None] * inv2], 1)
    axial = lambda a: a.reshape(NT, P, 32).transpose(1, 0, 2).reshape(P, -1)
    return {
        "ident": s == t, "before": s < t, "upto": s <= t, "after": s > t, "from": s >= t,
        "off": (s < t) & (s // BS != t // BS), "ones": np.ones((P, P)),
        "head_of": s // N == np.arange(2)[None, :], "perm": perm, "cosT": cosT, "sinT": sinT,
        "kcos": ktok(c), "ksin": ktok(sn), "maskb": np.concatenate([maskb, 0 * maskb, maskb], 1),
        "acos": axial(np.cos(a2)), "asin": axial(np.sin(a2)),
    }


CONSTANTS = {k: np.asarray(v, np.float32) for k, v in constants().items()}
CONST_AT, _at = {}, 0
for _k, _v in CONSTANTS.items():
    CONST_AT[_k] = _at
    _at += _v.shape[1]
CONST_W = _at


def build(nc, A, const_dram, out):
    with ExitStack() as ctx:
        def sb(name, shape, dtype=F32, stack=ctx):
            return stack.enter_context(nc.sbuf_tensor(name, shape, dtype))

        def sem(name):
            return ctx.enter_context(nc.semaphore(name))

        with ExitStack() as first:
            ring = sb("ring", [P, RING, SLOT], F32, first)
            arena = [sb(f"arena{i}", [P, n, SLOT], F32, first) for i, n in ARENA]
        ring12 = sb("ring12", [P, RING, SLOT], F32R)
        arena12 = [sb(f"arena12_{i}", [P, n, SLOT], F32R) for i, n in ARENA]
        x_sb = sb("x_sb", [P, NT, D])
        cst = sb("cst", [P, CONST_W])
        cols = sb("cols", [P, 4 * P])
        gpost, gpre = sb("gpost", [P, D]), sb("gpre", [P, D])
        unread = sb("unread", [P, 2, HALF], mybir.dt.bfloat16)
        stat = sb("stat", [P, 704])
        bank = [ctx.enter_context(nc.psum_tensor(f"bank{i}", [P, HALF], F32)) for i in range(8)]

        stat_used = [0]

        def small(n):
            stat_used[0] += n
            assert stat_used[0] <= 704
            return stat[:, stat_used[0] - n:stat_used[0]]

        def const(name, lo=0, hi=None):
            w = CONSTANTS[name].shape[1]
            return cst[:, CONST_AT[name] + lo:CONST_AT[name] + (w if hi is None else hi)]

        def col(name, i):
            return cols[:, COL[name] + i:COL[name] + i + 1]

        def bufs(i, n, mem=arena):
            tensor = [m for m, (first, count) in zip(mem, ARENA) if first <= i < first + count][0]
            at = [i - first for first, count in ARENA if first <= i < first + count][0]
            return tensor[:, at:at + n, :].rearrange("p b s -> p (b s)")

        def buf(i, lo=0, hi=SLOT, mem=arena):
            return bufs(i, 1, mem)[:, lo:hi]

        def chan(i, mem=arena):
            return buf(i, mem=mem).rearrange("p (c t) -> p c t", t=T)

        def toks(i):
            return buf(i).rearrange("p (a d) -> p a d", a=NT)

        def heads(i):
            return buf(i).rearrange("p (h t) -> p h t", t=P)

        def spread(ap, shape):
            return ap.broadcast_to(shape)

        ident = const("ident")
        po_ss, po_var, po_rstd, pr_ss, pr_var, pr_rstd = (small(n) for n in (4, 2, 2, 4, 2, 2))
        minus_half = small(32)

        landed = [sem(f"landed{r}") for r in range(RING)]
        slot_done = sem("slot_done")
        hi_ready, split_ready = sem("hi_ready"), sem("split_ready")
        x_landed = [sem("x_landed0"), sem("x_landed1")]
        const_landed, rows_zeroed, rows_landed = (sem(n) for n in ("const_landed", "rows_zeroed", "rows_landed"))
        cols_turned, cols_ready, consts_set = sem("cols_turned"), sem("cols_ready"), sem("consts_set")
        gpost_landed, gpre_landed, kv_gain_landed = (sem(n) for n in ("gpost_landed", "gpre_landed", "kv_gain_landed"))
        x_updated, out_stored = sem("x_updated"), sem("out_stored")
        dve_step = sem("dve_step")
        rows_done, post_mul, post_ss, post_var, post_rstd, pre_ss, pre_var, pre_rstd, xn_ready = (
            sem(n) for n in ("rows_done", "post_mul", "post_ss", "post_var", "post_rstd", "pre_ss", "pre_var", "pre_rstd",
                             "xn_ready"))
        squared, var_ready, rstd_ready = (sem(n) for n in ("squared", "var_ready", "rstd_ready"))
        turned, turn_a, turn_v = sem("turned"), sem("turn_a"), sem("turn_v")
        conv_step, act_done, ffn_prod, ffn_hi, ffn_done = (
            sem(n) for n in ("conv_step", "ffn_act_done", "ffn_prod", "ffn_hi", "ffn_done"))

        TURN_PRE0, TURN_PRE1, TURN_XKV, TURN_PRE2, TURN_PRE3, TURN_PRE4, TURN_SSD, TURN_MIX, TURN_PRE5 = range(9)

        def half_turns(turn, a):
            if turn in (TURN_XKV, TURN_PRE2):
                return 2 * TURN_XKV + 2 * a + (turn == TURN_PRE2)
            return 2 * turn + a

        HI = 13
        HI_OF = {"w_k": (5, 6, 8, 9), "w_r": (3, 13, 2, 3), "w_v": (0, 2, 15, 0), "w_o": (17, 4, 5, 0)}
        EARLY_HI = {FIRST[name] + s: i for name, at in HI_OF.items() for s, i in enumerate(at)}
        XN = 17
        XN_FFN0 = 11
        XN_KV, GAIN_KV = 9, 12
        MEAN = D ** -0.5

        def after_slots(eng, name, n=None):
            eng.wait_ge(slot_done, LAST[name] + 1 if n is None else FIRST[name] + n)

        def hi_of(n):
            return EARLY_HI.get(n, HI + n % RING)

        def weights(pe, n):
            pe.wait_ge(landed[n % RING], LANDED[n])
            return ring[:, n % RING, :]

        def split_weights(pe, n):
            pe.wait_ge(split_ready, SPLIT_NO[n] + 1)
            return buf(hi_of(n), mem=arena12), ring12[:, n % RING, :]

        def product(dst, stationary, moving, start, stop):
            nc.tensor.matmul(dst, stationary[0], moving[0], start=start, stop=False)
            nc.tensor.matmul(dst, stationary[0], moving[1], start=False, stop=False)
            return nc.tensor.matmul(dst, stationary[1], moving[0], start=False, stop=stop)

        def both(views, *at):
            return tuple(v[at] for v in views)

        def chan2(hi, lo):
            return chan(hi, arena12), chan(lo, arena12)

        def wide2(pe, first, nslots, act2, base, turn=None, before=None, rows=False, told=None,
                  between=None):
            def part(s, w, a):
                for kk in range(2):
                    k = 2 * s + kk
                    if turn is not None and k % 4 == 0:
                        turned_out(pe, turn, a, k // 4)
                    x = both(act2, slice(None), k, slice(a * P, (a + 1) * P))
                    for half in range(2):
                        at = slice(kk * D + half * HALF, kk * D + (half + 1) * HALF)
                        mm = product(bank[base + 2 * a + half][:, :], x, both(w, slice(None), at), k == 0, k == 2 * nslots - 1)
                return mm

            groups = [(s,) for s in range(nslots)]
            if turn is not None or rows:
                groups = [tuple(range(nslots))]
            for group in groups:
                if between is not None:
                    between(group[0])
                for a in range(NT):
                    if before is not None and group[0] == 0:
                        before(a)
                    for s in group:
                        mm = part(s, split_weights(pe, first + s), a)
                        if a == NT - 1:
                            mm.then_inc(slot_done, 1)
                    if a == 0 and group[-1] == nslots - 1 and (rows or told is not None):
                        mm.then_inc(rows_done if rows else told, 1)

        def turn_pe(src, base, a):
            for q in range(2):
                for c in range(4 * q, 4 * q + 4):
                    mm = nc.tensor.transpose(bank[base + 2 * a + q][:, c % 4 * P:(c % 4 + 1) * P], src[:, c * P:(c + 1) * P], ident)
                mm.then_inc(turned, 1)

        def xn_turn(pe, n, a, xn=XN, base=4):
            pe.wait_ge(xn_ready, n + 1)
            turn_pe(toks(xn)[:, a, :], base, a)

        def turned_out(eng, turn, a=NT - 1, q=1):
            eng.wait_ge(turn_v, half_turns(turn, a) * 2 + q + 1)
            if turn == TURN_PRE0:
                eng.wait_ge(turn_a, half_turns(turn, a) * 2 + q + 1)

        emitted = {}

        def ahead(eng, last, split):
            for n in range(emitted.get(eng, 0), last + 1):
                if n in SPLIT_NO:
                    split(eng, n)
            emitted[eng] = max(emitted.get(eng, 0), last + 1)

        def split_act(act, n, rounds_on=0):
            r, w = n % RING, SLOT_WIDTH[n]
            act.wait_ge(landed[r], LANDED[n] + rounds_on * 32)
            nc.scalar.activation(buf(hi_of(n), 0, w, arena12), ring[:, r, 0:w], ACT.Copy).then_inc(hi_ready, 1)

        def split_lo(eng, on, n, rounds_on=0):
            r, w = n % RING, SLOT_WIDTH[n]
            eng.wait_ge(hi_ready, SPLIT_NO[n] + 1 + rounds_on * RING)
            on.tensor_tensor(ring12[:, r, 0:w], ring[:, r, 0:w], buf(hi_of(n), 0, w, arena12).bitcast(F32),
                             ALU.subtract).then_inc(split_ready, 1)

        def split_dve(dve, n, rounds_on=0):
            split_lo(dve, nc.vector, n, rounds_on)

        def split_pool(pool, n):
            split_lo(pool, nc.gpsimd, n)

        def turn_act(act, turn, a, base, hi):
            whole = turn == TURN_PRE0
            for q in range(1 if whole else 2):
                act.wait_ge(turned, half_turns(turn, a) * 2 + q + 1)
                nc.scalar.activation(chan(hi, arena if whole else arena12)[:, 4 * q:4 * q + 4, a * P:(a + 1) * P],
                                     bank[base + 2 * a + q][:, :].rearrange("p (c t) -> p c t", t=P),
                                     ACT.Copy).then_inc(turn_a, 2 if whole else 1)

        def turn_dve(dve, turn, a, base, hi, lo=None):
            for q in range(2) if lo is not None else (1,):
                src = bank[base + 2 * a + q][:, :].rearrange("p (c t) -> p c t", t=P)
                at = (slice(None), slice(4 * q, 4 * q + 4), slice(a * P, (a + 1) * P))
                if lo is None:
                    dve.wait_ge(turned, half_turns(turn, a) * 2 + q + 1)
                    nc.vector.tensor_copy(chan(hi)[at], src).then_inc(turn_v, 2)
                else:
                    dve.wait_ge(turn_a, half_turns(turn, a) * 2 + q + 1)
                    nc.vector.tensor_tensor(chan(lo, arena12)[at], src, chan(hi, arena12)[at].bitcast(F32),
                                            ALU.subtract).then_inc(turn_v, 1)

        steps = [0]

        def step(ins):
            steps[0] += 1
            ins.then_inc(dve_step, 1)
            return steps[0]

        def link(dve, ins):
            dve.wait_ge(dve_step, step(ins))

        POST = ["w_o", "ffn_out0", "o_w", "ffn_out1", "w_out", "ffn_out2"]

        def rows_ready(eng, i, a):
            if a == 0:
                eng.wait_ge(rows_done, i + 1)
            else:
                after_slots(eng, POST[i])

        def post_squares(act, i, a):
            rows_ready(act, i, a)
            if i == len(POST) - 1 and a == 1:
                act.wait_ge(post_ss, 4 * i + 2)
            else:
                act.wait_ge(pre_ss, 4 * i + 2 * a + 4)
            nc.scalar.activation(unread[:, 0, :], bank[4 + 2 * a][:, :], ACT.Square, scale=MEAN,
                                 accum_out=po_ss[:, 2 * a:2 * a + 1]).then_inc(post_ss, 1)
            act.wait_ge(post_mul, 4 * i + 2 * a + 1)
            nc.scalar.activation(unread[:, 1, :], bank[5 + 2 * a][:, :], ACT.Square, scale=MEAN,
                                 accum_out=po_ss[:, 2 * a + 1:2 * a + 2]).then_inc(post_ss, 1)

        def post_scale(dve, i, a):
            tmp = toks(XN if i else XN_FFN0)[:, a, :]
            dve.wait_ge(gpost_landed, 16 * (i + 1))
            rows_ready(dve, i, a)
            nc.vector.tensor_tensor(tmp[:, HALF:D], bank[5 + 2 * a][:, :], gpost[:, HALF:D], ALU.mult).then_inc(post_mul, 1)
            dve.wait_ge(post_ss, 4 * i + 2 * a + 1)
            nc.vector.tensor_tensor(tmp[:, 0:HALF], bank[4 + 2 * a][:, :], gpost[:, 0:HALF], ALU.mult).then_inc(post_mul, 1)
            dve.wait_ge(post_ss, 4 * i + 2 * a + 2)
            nc.vector.scalar_tensor_tensor(po_var[:, a:a + 1], po_ss[:, 2 * a:2 * a + 1], EPS, po_ss[:, 2 * a + 1:2 * a + 2],
                                           ALU.add, ALU.add).then_inc(post_var, 1)

        def post_root(pool, i, a):
            pool.wait_ge(post_var, NT * i + a + 1)
            nc.gpsimd.tensor_tensor(po_rstd[:, a:a + 1], po_var[:, a:a + 1], minus_half[:, 0:1], ALU.pow).then_inc(post_rstd, 1)

        def x_update(dve, i, a):
            dve.wait_ge(post_mul, 4 * i + 2 * a + 2)
            dve.wait_ge(post_rstd, NT * i + a + 1)
            tmp = toks(XN if i else XN_FFN0)
            for half in range(2):
                at = slice(half * HALF, (half + 1) * HALF)
                nc.vector.scalar_tensor_tensor(x_sb[:, a, at], tmp[:, a, at], po_rstd[:, a:a + 1], x_sb[:, a, at],
                                               ALU.mult, ALU.add).then_inc(x_updated, 1)

        def x_squares(act, i, a):
            for half in range(2):
                if i == 0:
                    act.wait_ge(x_landed[a], 16)
                else:
                    act.wait_ge(x_updated, 4 * (i - 1) + 2 * a + half + 1)
                if i or a:
                    act.wait_ge(pre_ss, 4 * i + 2 * a + half - 1)
                nc.scalar.activation(unread[:, half, :], x_sb[:, a, half * HALF:(half + 1) * HALF], ACT.Square, scale=MEAN,
                                     accum_out=pr_ss[:, 2 * a + half:2 * a + half + 1]).then_inc(pre_ss, 1)

        def pre_mean(dve, i, a):
            dve.wait_ge(pre_ss, 4 * i + 2 * a + 2)
            nc.vector.scalar_tensor_tensor(pr_var[:, a:a + 1], pr_ss[:, 2 * a:2 * a + 1], EPS, pr_ss[:, 2 * a + 1:2 * a + 2],
                                           ALU.add, ALU.add).then_inc(pre_var, 1)

        def pre_root(pool, i, a):
            pool.wait_ge(pre_var, NT * i + a + 1)
            nc.gpsimd.tensor_tensor(pr_rstd[:, a:a + 1], pr_var[:, a:a + 1], minus_half[:, 0:1], ALU.pow).then_inc(pre_rstd, 1)

        def x_scaled(dve, i, a, gain=None, dst=XN):
            dve.wait_ge(pre_rstd, NT * i + a + 1)
            if gain is None:
                gain = gpre[:, :]
                dve.wait_ge(gpre_landed, 16 * (i + 1))
            else:
                dve.wait_ge(kv_gain_landed, 16)
            nc.vector.scalar_tensor_tensor(toks(dst)[:, a, :], x_sb[:, a, :], pr_rstd[:, a:a + 1], gain,
                                           ALU.mult, ALU.mult).then_inc(xn_ready, 1)

        XN_OF = [0, 2, 4, 8, 10, 12, 14]

        def between_act(act, i, turns, last):
            post_squares(act, i, 0)
            x_squares(act, i + 1, 0)
            ahead(act, last + 1, split_act)
            post_squares(act, i, 1)
            for turn, base, hi, lo, gain, xn in turns:
                turn_act(act, turn, 0, base, hi)
            ahead(act, last + 2, split_act)
            x_squares(act, i + 1, 1)
            if len(turns) > 1:
                ahead(act, last + 4, split_act)
            for turn, base, hi, lo, gain, xn in turns:
                turn_act(act, turn, 1, base, hi)

        def between_dve(dve, i, turns, last):
            post_scale(dve, i, 0)
            x_update(dve, i, 0)
            pre_mean(dve, i + 1, 0)
            for turn, base, hi, lo, gain, xn in turns:
                x_scaled(dve, i + 1, 0, gain, xn)
            emitted[dve] = last + 2
            post_scale(dve, i, 1)
            x_update(dve, i, 1)
            for turn, base, hi, lo, gain, xn in turns:
                turn_dve(dve, turn, 0, base, hi, lo)
            pre_mean(dve, i + 1, 1)
            dve.wait_ge(split_ready, SPLIT_NO[last + 1] + 1)
            if len(turns) > 1:
                ahead(dve, last + 4, split_dve)
            for turn, base, hi, lo, gain, xn in turns:
                x_scaled(dve, i + 1, 1, gain, xn)
            for turn, base, hi, lo, gain, xn in turns:
                turn_dve(dve, turn, 1, base, hi, lo)

        def between_pool(pool, i):
            n = LAST[POST[i]] + 1
            post_root(pool, i, 0)
            pre_root(pool, i + 1, 0)
            pool.wait_ge(split_ready, SPLIT_NO[n])
            pool.wait_ge(hi_ready, SPLIT_NO[n] + 1)
            r, w, hi = n % RING, SLOT_WIDTH[n], buf(hi_of(n), mem=arena12).bitcast(F32)
            halves = [slice(0, w // 2), slice(w // 2, w)]
            nc.gpsimd.tensor_tensor(ring12[:, r, halves[0]], ring[:, r, halves[0]], hi[:, halves[0]], ALU.subtract)
            post_root(pool, i, 1)
            nc.gpsimd.tensor_tensor(ring12[:, r, halves[1]], ring[:, r, halves[1]], hi[:, halves[1]],
                                    ALU.subtract).then_inc(split_ready, 1)
            pre_root(pool, i + 1, 1)

        def load_gains(pool, i, post, pre):
            pool.wait_ge(xn_ready, XN_OF[i + 1])
            if i > 0:
                pool.wait_ge(post_mul, 4 * i)
            if pre is not None:
                pool.dma_start(gpre[:, :], pre.partition_broadcast(P)).then_inc(gpre_landed, 16)
            pool.dma_start(gpost[:, :], post.partition_broadcast(P)).then_inc(gpost_landed, 16)

        FFN_H, FFN_H_LO, FFN_F, FFN_F_LO, FFN_CONV, FFN_P = 0, 5, 1, 6, 4, 9
        fT_hi, fT_lo = (bufs(i, 3, arena12) for i in (FFN_F, FFN_F_LO))
        conv_acc = [buf(FFN_CONV, j * T, (j + 1) * T) for j in range(RING)]
        gate_act = [buf(FFN_CONV, (RING + j) * T, (RING + j + 1) * T) for j in range(RING)]
        gated = [buf(FFN_P, j * T, (j + 1) * T) for j in range(RING)]
        LOOPS = FC // RING

        def rounds(eng, tile):
            for j in range(RING):
                tile(0, j)
            with eng.Fori(1, LOOPS) as it:
                for j in range(RING):
                    tile(it, j)
            for j in range(FC - LOOPS * RING):
                tile(LOOPS, j)

        def tile_cells(whole, it, j):
            if isinstance(it, int):
                return whole[:, (it * RING + j) * T:(it * RING + j + 1) * T]
            return whole[:, bass.ds(it * (RING * T) + j * T, T)]

        def ffn_pe(pe, f, i, turn):
            first = FIRST[f"ffn_in{f}"]
            h2 = chan2(FFN_H, FFN_H_LO)

            for a in range(NT):
                xn_turn(pe, XN_OF[i] + a, a, XN if f else XN_FFN0)

            def tile(it, j):
                r = (first + j) % RING
                pe.wait_ge(split_ready, SPLIT_NO[first + j] + 1 + it * RING)
                if not (isinstance(it, int) and it == 0):
                    pe.wait_ge(ffn_prod, f * FC + it * RING + (j - RING + 1))
                w = [v.rearrange("p (k g n) -> p k g n", k=DC, g=2) for v in (buf(HI + r, mem=arena12), ring12[:, r, :])]
                for g in range(2):
                    for k in range(DC):
                        if isinstance(it, int) and it == j == g == 0 and k % 4 == 0:
                            turned_out(pe, turn, 0, k // 4)
                            turned_out(pe, turn, 1, k // 4)
                        mm = product(bank[j][:, g * T:(g + 1) * T], both(w, slice(None), k, g), both(h2, slice(None), k),
                                     k == 0, k == DC - 1)
                mm.then_inc(slot_done, 1)

            rounds(pe, tile)

            def rows(k, a):
                w = split_weights(pe, FIRST[f"ffn_out{f}"] + k // 2)
                pe.wait_ge(ffn_done, f * FC + k + 1)
                at = slice(k * T + a * P, k * T + (a + 1) * P)
                for half in range(2):
                    cells = slice((k % 2) * D + half * HALF, (k % 2) * D + (half + 1) * HALF)
                    mm = product(bank[4 + 2 * a + half][:, :], (fT_hi[:, at], fT_lo[:, at]), both(w, slice(None), cells),
                                 k == 0, k == FC - 1)
                return mm

            last = 2 * (RING - 1)
            for k in range(FC - last):
                for a in range(NT):
                    mm = rows(k, a)
                if k % 2 == 1:
                    mm.then_inc(slot_done, 1)
            for a in range(NT):
                for k in range(FC - last, FC):
                    mm = rows(k, a)
                    if a == NT - 1 and k % 2 == 1:
                        mm.then_inc(slot_done, 1)
                if a == 0:
                    mm.then_inc(rows_done, 1)

        def ffn_act(act, f):
            first = FIRST[f"ffn_in{f}"]

            def tile(it, j):
                split_act(act, first + AHEAD + j, it)
                if f < 2:
                    act.wait_ge(conv_step, 3 * f * FC + it * (3 * RING) + 3 * (j + 1))
                    nc.scalar.activation(gate_act[j], conv_acc[j], ACT.Gelu_apprx_tanh).then_inc(act_done, 1)
                else:
                    act.wait_ge(slot_done, first + it * RING + (j + 1))
                    nc.scalar.activation(gate_act[j], bank[j][:, 0:T], ACT.Silu).then_inc(act_done, 1)

            ahead(act, first + AHEAD - 1, split_act)
            rounds(act, tile)
            emitted[act] = first + FC + AHEAD

        def ffn_dve(dve, f):
            first = FIRST[f"ffn_in{f}"]

            def at(it, j, name):
                if isinstance(it, int):
                    return col(name[0], name[1] + it * RING + j)
                return cols[:, bass.ds(it * RING + (COL[name[0]] + name[1] + j), 1)]

            def tile(it, j):
                gate, up = bank[j][:, 0:T], bank[j][:, T:2 * T]
                if f < 2:
                    tap = [(f"ffn_conv_w{f}", i * FC) for i in range(3)]
                    dve.wait_ge(slot_done, first + it * RING + (j + 1))
                    nc.vector.tensor_scalar(conv_acc[j], gate, at(it, j, tap[2]), at(it, j, ("ffn_conv_b", f * FC)),
                                            ALU.mult, ALU.add).then_inc(conv_step, 1)
                    for i in (1, 0):
                        back = 2 - i
                        dve.wait_ge(conv_step, 3 * f * FC + it * (3 * RING) + 3 * j + back)
                        nc.vector.scalar_tensor_tensor(conv_acc[j][:, back:T], gate[:, 0:T - back], at(it, j, tap[i]),
                                                       conv_acc[j][:, back:T], ALU.mult, ALU.add).then_inc(conv_step, 1)
                split_dve(dve, first + AHEAD + j, it)
                dve.wait_ge(act_done, f * FC + it * RING + (j + 1))
                if not (isinstance(it, int) and it == 0):
                    dve.wait_ge(ffn_done, f * FC + it * RING + (j - RING + 1))
                nc.vector.tensor_tensor(gated[j], gate_act[j], up, ALU.mult).then_inc(ffn_prod, 1)

            ahead(dve, first + AHEAD - 1, split_dve)
            rounds(dve, tile)
            emitted[dve] = first + FC + AHEAD

        def ffn_pool(pool, f):
            def tile(it, j):
                pool.wait_ge(ffn_prod, f * FC + it * RING + (j + 1))
                nc.gpsimd.tensor_copy(tile_cells(fT_hi, it, j), gated[j]).then_inc(ffn_hi, 1)
                pool.wait_ge(ffn_hi, f * FC + it * RING + (j + 1))
                nc.gpsimd.tensor_tensor(tile_cells(fT_lo, it, j), gated[j], tile_cells(fT_hi, it, j).bitcast(F32),
                                        ALU.subtract).then_inc(ffn_done, 1)

            rounds(pool, tile)

        ROWS = 15
        rows = buf(ROWS, 0, 4 * P).rearrange("p (q n) -> p q n", n=P)

        def row_view(name):
            if name[-1] in "01" and name.startswith("ffn_conv_w"):
                return A["ffn_conv_w"][int(name[-1])].rearrange("j (c p) -> (j c) p", p=P)
            a = A[name]
            if name == "a_r_k":
                return a.rearrange("o (c g) n -> (o c) (g n)", g=2)
            if len(a.shape) == 1:
                return a.rearrange("(c p) -> c p", p=P)
            if len(a.shape) == 2:
                return a.rearrange("o (c p) -> (o c) p", p=P)
            return a.rearrange("o j (c p) -> (o j c) p", p=P)

        def start_act(act):
            for a in range(NT):
                act.dma_start(x_sb[:, a, :], A["x"][0, a * P:(a + 1) * P, :]).then_inc(x_landed[a], 16)
            act.dma_start(cst[:, :], const_dram).then_inc(const_landed, 16)

        def start_sp(sp):
            sp.wait_ge(rows_zeroed, 1)
            for q, tile in enumerate(ROW_TILES):
                for name, n in tile:
                    lo = COL[name] - q * P
                    sp.dma_start(rows[lo:lo + n, q, :], row_view(name)).then_inc(rows_landed, 16)

        def start_pool(pool):
            nc.gpsimd.memset(minus_half, -0.5).then_inc(consts_set, 1)
            pool.dma_start(gpre[:, :], A["norm_g"][0, 0].partition_broadcast(P)).then_inc(gpre_landed, 16)
            pool.wait_ge(consts_set, 1)

        def start_pe(pe):
            pe.wait_ge(const_landed, 16)
            for a in range(NT):
                xn_turn(pe, a, a)
            pe.wait_ge(rows_landed, 16 * PARAM_DMAS)
            for q in range(4):
                mm = nc.tensor.transpose(bank[0][:, q * P:(q + 1) * P], rows[:, q, :], ident)
            mm.then_inc(cols_turned, 1)

        def start_dve(dve):
            nc.vector.memset(buf(ROWS, 0, 4 * P), 0.0).then_inc(rows_zeroed, 1)
            for a in range(NT):
                pre_mean(dve, 0, a)
                x_scaled(dve, 0, a)
            for a in range(NT):
                turn_dve(dve, TURN_PRE0, a, 4, W_HT)
            dve.wait_ge(cols_turned, 1)
            nc.vector.tensor_copy(cols[:, :], bank[0][:, :]).then_inc(cols_ready, 1)
            dve.wait_ge(const_landed, 16)
            dve.wait_ge(cols_ready, 1)

        W_HT, W_DX = 0, 1
        W_XS = {"w": 3, "a": 13, "r": 14, "k": 2, "g": 15, "v": 16}
        MIXES = [("w", 3), ("a", 4), ("k", 1), ("r", 0), ("g", 5), ("v", 2)]
        MIXED = {name: i + 1 for i, (name, _) in enumerate(MIXES)}
        W_K, W_SIG, W_CUM, W_A, W_EP, W_EM, W_KK, W_LORA, W_G, W_R = 4, 5, 6, 7, 8, 9, 10, 11, 12, 17
        W_RINV, W_T1, W_V = 0, 1, 11
        W_XS_HI = {"k": 17, "r": 12, "v": 3}
        XS_SPLIT = {name: i + 1 for i, name in enumerate(W_XS_HI)}
        W_REMOVE, W_ADD, W_KEY, W_QUERY = W_SIG, W_A, W_EM, W_EP
        W_N, W_Z, W_LK, W_RK, W_RB = (13, 14), (2, 3), (0, 1), (15, 16), (6, 10)
        W_SOLVE, W_TOK = 1, 17
        W_RHS0, W_RHS1, W_SUM1, W_U1, W_U0 = 5, 4, 7, 0, 1
        W_LNX, W_YC, W_YSQ, W_C, W_OT, W_OT_LO = 9, 13, 14, 2, 3, 6
        HALVES = [slice(hf * D, (hf + 1) * D) for hf in range(2)]
        nd = buf(W_SOLVE, 0, BS * BS).rearrange("p (s t) -> p s t", t=BS)
        yd = buf(W_SOLVE, BS * BS, 2 * BS * BS).rearrange("p (s t) -> p s t", t=BS)
        n_dram = nc.dram_tensor("n_blocks", (NT, H, NB, BS, BS), F32, kind="Internal").ap()
        y_dram = nc.dram_tensor("y_blocks", (NT, H, NB, BS, BS), F32, kind="Internal").ap()
        rhs0, sum0, u0 = buf(W_RHS0, 0, D), buf(W_RHS0, D, 2 * D), buf(W_U0, 0, D)
        s1 = buf(W_U0, D, D + HP * N)
        u1, q_turned = buf(W_SUM1, 0, D), buf(W_RHS0, 0, D).rearrange("p (c t) -> p c t", t=P)
        sides = lambda i: buf(i).rearrange("p (x h n) -> p x h n", x=2, n=N)
        mid, last_e, s_scale = small(16), small(8), small(8)
        solve_tmp = small(256)
        kk_inv = small(NT * H)
        bon, y_sum, y_mean, y_sq, y_var, y_rstd = (small(32) for _ in range(6))

        (mix_done, lora_hidden, gate_hidden, k_evac, decay_sig, iclr_sig, r_evac, g_evac, v_evac) = (
            sem(n) for n in ("mix_done", "lora_hidden", "gate_hidden", "k_evac", "decay_sig", "iclr_sig", "r_evac",
                             "g_evac", "v_evac"))
        (kk_ready, kk_summed, kk_wide, kk_turned, cum_ready, decay_exp, removal_ready, keys_ready, queries_ready, bonus_ready,
         bonus_summed, bonus_copied, n_mm, n_masked, prod_mm, prod_evac, lk_masked, rk_masked) = (
            sem(n) for n in ("kk_ready", "kk_summed", "kk_wide", "kk_turned", "cum_ready", "decay_exp", "removal_ready", "keys_ready",
                             "queries_ready", "bonus_ready", "bonus_summed", "bonus_copied", "n_mm", "n_masked",
                             "prod_mm", "prod_evac", "lk_masked", "rk_masked"))
        (n_saved, nd_landed, solved, y_saved, z_zeroed, z_landed, n_cut, tok_mm, tok_evac, u_mm, u_rhs, u_sol,
         state_mm, state_ready, q_mm, q_in, u1_mm, u1_ready, ymm, lnx_landed, yc_ready, c_step, c_ready, o_ready, o_mm,
         o_in, o_split) = (
            sem(n) for n in ("n_saved", "nd_landed", "solved", "y_saved", "z_zeroed", "z_landed", "n_cut", "tok_mm",
                             "tok_evac", "u_mm", "u_rhs", "u_sol", "state_mm", "state_ready", "q_mm", "q_in", "u1_mm",
                             "u1_ready", "y_mm", "lnx_landed", "yc_ready", "c_step", "c_ready", "o_ready", "o_mm",
                             "o_in", "o_split"))
        xs_hi, xs_split = sem("xs_hi"), sem("xs_split")
        ROUNDS = 2 * NB
        before_round = lambda s: 0 if s == 0 else 4 + 6 * (s - 1)
        sums_before = lambda s: 4 + 6 * (s // 2 - 1) if s else 0
        sols_before = lambda s: 6 * (s // 2)
        PAIR_BANKS = NT * HP
        bank_heads = lambda l: [l % 2 + 2 * (2 * (l % 8 // 2) + i) for i in range(2)]
        Y_BANK = ((5, 0), (6, 7))

        def xs_split_act(act, name):
            act.wait_ge(mix_done, MIXED[name])
            nc.scalar.activation(buf(W_XS_HI[name], mem=arena12), buf(W_XS[name]), ACT.Copy).then_inc(xs_hi, 1)

        def xs_split_lo(eng, on, name):
            eng.wait_ge(xs_hi, XS_SPLIT[name])
            on.tensor_tensor(buf(W_XS[name], mem=arena12), buf(W_XS[name]), buf(W_XS_HI[name], mem=arena12).bitcast(F32),
                             ALU.subtract).then_inc(xs_split, 1)

        def rwkv_pe(pe):
            xs = {name: chan(i) for name, i in W_XS.items()}
            lora = buf(W_LORA)

            xs2 = {name: chan2(W_XS_HI[name], W_XS[name]) for name in W_XS_HI}

            def columns(name, x2, base, s):
                w2 = [w.rearrange("p (k n) -> p k n", n=T) for w in split_weights(pe, FIRST[name] + s)]
                for n in range(2):
                    for k in range(DC):
                        mm = product(bank[base + s][:, n * T:(n + 1) * T], both(w2, slice(None), k, slice(n * P, (n + 1) * P)),
                                     both(x2, slice(None), k), k == 0, k == DC - 1)
                mm.then_inc(slot_done, 1)

            w = weights(pe, FIRST["lora_wa"])[:, 0:2 * DC * 64].rearrange("p (g k n) -> p g k n", g=2, k=DC)
            for g, name in enumerate(("w", "a")):
                pe.wait_ge(mix_done, MIXED[name])
                for k in range(DC):
                    mm = nc.tensor.matmul(bank[g][0:64, 0:T], w[:, g, k, :], xs[name][:, k, :],
                                          start=(k == 0), stop=(k == DC - 1))
            mm.then_inc(slot_done, 1)
            pe.wait_ge(xs_split, XS_SPLIT["k"])
            for s in range(4):
                columns("w_k", xs2["k"], 4, s)
            w = weights(pe, FIRST["lora_wa2"])
            pe.wait_ge(lora_hidden, 2)
            for g in range(2):
                for c in range(DC):
                    if g == 1 and c % 2 == 0:
                        pe.wait_ge(k_evac, c // 2 + 1)
                    mm = nc.tensor.matmul(bank[4 * g + c // 2][:, (c % 2) * T:(c % 2 + 1) * T],
                                          w[0:64, g * D + c * P:g * D + (c + 1) * P], lora[0:64, g * T:(g + 1) * T],
                                          start=True, stop=True)
            mm.then_inc(slot_done, 1)
            pe.wait_ge(xs_split, XS_SPLIT["r"])
            for s in range(4):
                pe.wait_ge(decay_sig, s + 1)
                columns("w_r", xs2["r"], 0, s)
                if s == 0:
                    pe.wait_ge(iclr_sig, 1)
                    for c in range(DC):
                        pe.wait_ge(squared, c // 4 + 1)
                        for a in range(NT):
                            mm = nc.tensor.matmul(bank[4][:, a * H + 2 * c:a * H + 2 * c + 2],
                                                  chan(W_RINV)[:, c, a * P:(a + 1) * P], const("head_of"), start=True, stop=True)
                    mm.then_inc(kk_summed, 1)
                if s == 2:
                    pe.wait_ge(iclr_sig, 4)
                    pe.wait_ge(kk_wide, 1)
                    for c in range(DC):
                        for a in range(NT):
                            mm = nc.tensor.transpose(bank[4 + c // 2][:, c % 2 * T + a * P:c % 2 * T + (a + 1) * P],
                                                     toks(W_RINV)[:, a, c * P:(c + 1) * P], ident)
                        if c % 4 == 3:
                            mm.then_inc(kk_turned, 1)
            w = weights(pe, FIRST["lora_g"])[:, 0:DC * GATE_LORA].rearrange("p (k n) -> p k n", n=GATE_LORA)
            pe.wait_ge(mix_done, MIXED["g"])
            pe.wait_ge(r_evac, 1)
            for lo, hi in ((0, P), (P, GATE_LORA)):
                at = 0 if lo == 0 else T
                for k in range(DC):
                    mm = nc.tensor.matmul(bank[0][0:hi - lo, at:at + T], w[:, k, lo:hi], xs["g"][:, k, :],
                                          start=(k == 0), stop=(k == DC - 1))
            mm.then_inc(slot_done, 1)
            w = weights(pe, FIRST["lora_g2"])
            pe.wait_ge(r_evac, 4)
            pe.wait_ge(gate_hidden, 2)
            for a in range(NT):
                for half in range(2):
                    dst = bank[2 * a + half][:, :]
                    nc.tensor.matmul(dst, lora[:, 2 * T + a * P:2 * T + (a + 1) * P],
                                     w[:, half * HALF:(half + 1) * HALF], start=True, stop=False)
                    mm = nc.tensor.matmul(dst, lora[0:32, 3 * T + a * P:3 * T + (a + 1) * P],
                                          w[0:32, D + half * HALF:D + (half + 1) * HALF], start=False, stop=True)
            mm.then_inc(slot_done, 1)

            remove, add, key, query = (chan(i) for i in (W_REMOVE, W_ADD, W_KEY, W_QUERY))
            both_sides = bufs(W_REMOVE, 4).rearrange("p (b c t) -> p b c t", b=4, t=T)[:, 0:4:W_QUERY - W_REMOVE]

            def pairs(l, left, a):
                for i, h in enumerate(bank_heads(l)):
                    lo = (h % 2) * N
                    at = (slice(lo, lo + N), h // 2, slice(a * P, (a + 1) * P))
                    mm = nc.tensor.matmul(bank[4 + l % 4][:, i * T:(i + 1) * T].rearrange("p (x t) -> p x t", t=P), left[at],
                                          both_sides[lo:lo + N, :, h // 2, a * P:(a + 1) * P], start=True, stop=True)
                return mm

            pe.wait_ge(removal_ready, 2)
            pe.wait_ge(queries_ready, 1)
            for l in range(PAIR_BANKS):
                if l >= 4:
                    pe.wait_ge(n_masked, 2 * (l - 3))
                pairs(l, add, l // 8).then_inc(n_mm, 1)

            pe.wait_ge(xs_split, XS_SPLIT["v"])
            pe.wait_ge(g_evac, 4)
            for s in range(4):
                w2 = split_weights(pe, FIRST["w_v"] + s)
                for a in range(NT):
                    for k in (2 * s, 2 * s + 1):
                        for half in range(2):
                            at = slice(k % 2 * D + half * HALF, k % 2 * D + (half + 1) * HALF)
                            mm = product(bank[2 * a + half][:, :], both(xs2["v"], slice(None), k, slice(a * P, (a + 1) * P)),
                                         both(w2, slice(None), at), k == 0, k == DC - 1)
                mm.then_inc(slot_done, 1)
                if s == 0:
                    pe.wait_ge(n_masked, 2 * PAIR_BANKS)
                    pe.wait_ge(keys_ready, 1)
                    for j in range(4):
                        for i in range(4):
                            c = 4 * (j % 2) + i
                            mm = nc.tensor.transpose(bank[4 + j][:, i * P:(i + 1) * P], (add, key)[j // 2][:, c, 0:P], ident)
                        mm.then_inc(tok_mm, 1)
                if s == 1:
                    for j in range(2):
                        pe.wait_ge(tok_evac, j + 1)
                        for i in range(4):
                            mm = nc.tensor.transpose(bank[4 + j][:, i * P:(i + 1) * P], remove[:, 4 * j + i, P:T], ident)
                        mm.then_inc(tok_mm, 1)
                    pe.wait_ge(bonus_ready, 1)
                    pe.wait_ge(tok_evac, 3)
                    for a in range(NT):
                        for c in range(DC):
                            mm = nc.tensor.matmul(bank[6][:, a * H + 2 * c:a * H + 2 * c + 2],
                                                  chan(W_K)[:, c, a * P:(a + 1) * P], const("head_of"), start=True, stop=True)
                    mm.then_inc(bonus_summed, 1)
            pe.wait_ge(bonus_copied, 1)
            pe.wait_ge(tok_evac, 6)
            for l in range(PAIR_BANKS):
                if l >= 4:
                    pe.wait_ge(prod_evac, l - 3)
                pairs(l, key, l // 8).then_inc(prod_mm, 1)

            v = toks(W_V)
            z, n_off, lk, rb, rk = ([heads(m) for m in two] for two in (W_Z, W_N, W_LK, W_RB, W_RK))
            for s in range(ROUNDS):
                if s == 1:
                    pe.wait_ge(z_landed, 16 * NT * NB)
                if s == 2:
                    pe.wait_ge(n_cut, NT)
                for g in range(4 if s == 0 else 6):
                    a = 0 if g < 2 else 1
                    if s == 0:
                        pe.wait_ge(v_evac, 4)
                        pe.wait_ge(lk_masked, g + 1)
                    elif s % 2 == 1:
                        pe.wait_ge(u_rhs, 4 if s == 1 and g >= 2 else sums_before(s - 1) + g + 1)
                    else:
                        pe.wait_ge(u_sol, sols_before(s - 1) + g + 1)
                    wide_sides = a == 1 and s > 0
                    for i in range(4 if wide_sides else 8):
                        h = 4 * (g - 2) + i if wide_sides else 8 * (g % 2) + i
                        hv = slice(h * N, (h + 1) * N)
                        if s == 0:
                            left, right = lk, v[:, a, hv]
                        elif s % 2 == 0:
                            left, right = n_off, sides(W_U1)[:, :, h, :] if a else u0[:, hv]
                        else:
                            left, right = z, (sides(W_RHS1 if s == 1 else W_SUM1)[:, :, h, :] if a else
                                              (rhs0 if s == 1 else sum0)[:, hv])
                        w = 2 * N if wide_sides else N
                        mm = nc.tensor.matmul(bank[g][:, i * w:(i + 1) * w], left[a][:, h, :], right, start=True, stop=True)
                    mm.then_inc(u_mm, 1)
            bh, kh = buf(W_TOK, 0, D), buf(W_TOK, D, 2 * D)
            pe.wait_ge(u_sol, sols_before(ROUNDS - 1) + 2)
            for h in range(H):
                lo, c, hv = (h % 2) * N, h // 2, slice(h * N, (h + 1) * N)
                cells = bank[0][lo:lo + N, c * N:(c + 1) * N]
                nc.tensor.matmul(cells, bh[:, hv], u0[:, hv], start=True, stop=False)
                mm = nc.tensor.matmul(cells, kh[:, hv], v[:, 0, hv], start=False, stop=True)
            mm.then_inc(state_mm, 1)
            pe.wait_ge(u_sol, sols_before(ROUNDS - 1) + 6)
            for c in range(DC):
                mm = nc.tensor.transpose(bank[1 + c // 4][:, c % 4 * P:(c % 4 + 1) * P],
                                         buf(W_U1, D + c * P, D + (c + 1) * P), ident)
            mm.then_inc(q_mm, 1)
            def o_turn(a):
                pe.wait_ge(o_ready, a + 1)
                for c in range(DC):
                    mm = nc.tensor.transpose(bank[2 * a + c // 4][:, c % 4 * P:(c % 4 + 1) * P],
                                             toks(W_YC)[:, a, c * P:(c + 1) * P], ident)
                mm.then_inc(o_mm, 1)

            def y_bank(a, q):
                for c in range(HP):
                    if a == q == 1 and c == HP // 2:
                        o_turn(0)
                    h = 2 * c + q
                    cells, hv = bank[Y_BANK[a][q]][:, c * N:(c + 1) * N], slice(h * N, (h + 1) * N)
                    nc.tensor.matmul(cells, rb[a][:, h, :], (u0, u1)[a][:, hv], start=True, stop=False)
                    mm = nc.tensor.matmul(cells, rk[a][:, h, :], v[:, a, hv], start=False, stop=(a == 0))
                    if a == 1:
                        mm = nc.tensor.matmul(cells, query[q * N:(q + 1) * N, c, P:2 * P],
                                              s1[q * N:(q + 1) * N, c * N:(c + 1) * N], start=False, stop=True)
                mm.then_inc(ymm, 1)

            pe.wait_ge(rk_masked, NT)
            y_bank(0, 0)
            pe.wait_ge(q_in, 2)
            pe.wait_ge(state_ready, 1)
            for q in range(2):
                for c in range(HP):
                    mm = nc.tensor.matmul(bank[3 + q][:, c * N:(c + 1) * N], q_turned[q * N:(q + 1) * N, c, :],
                                          s1[q * N:(q + 1) * N, c * N:(c + 1) * N], start=True, stop=True)
            mm.then_inc(u1_mm, 1)
            y_bank(0, 1)
            pe.wait_ge(u1_ready, 2)
            y_bank(1, 0)
            y_bank(1, 1)
            def o_tile(a):
                if a > 0:
                    o_turn(a)
                pe.wait_ge(o_split, 2 * (a + 1))

            wide2(pe, FIRST["w_o"], 4, chan2(W_OT, W_OT_LO), 4, before=o_tile, rows=True)

        def rwkv_act(act):
            lora = buf(W_LORA)
            ahead(act, FIRST["w_k"] + 1, split_act)
            xs_split_act(act, "k")
            ahead(act, FIRST["w_k"] + 2, split_act)
            xs_split_act(act, "r")
            after_slots(act, "lora_wa")
            nc.scalar.activation(lora[0:64, 0:T], bank[0][0:64, 0:T], ACT.Tanh).then_inc(lora_hidden, 1)
            nc.scalar.activation(lora[0:64, T:2 * T], bank[1][0:64, 0:T], ACT.Copy).then_inc(lora_hidden, 1)
            ahead(act, LAST["w_k"], split_act)
            for s in range(4):
                after_slots(act, "w_k", s + 1)
                nc.scalar.activation(buf(W_K, s * HALF, (s + 1) * HALF), bank[4 + s][:, :], ACT.Copy).then_inc(k_evac, 1)
                if s == 1 or s == 2:
                    ahead(act, FIRST["w_r"] + s - 1, split_act)
            for hf in range(2):
                act.wait_ge(kk_ready, hf + 1)
                nc.scalar.activation(buf(W_RINV)[:, HALVES[hf]], buf(W_KK)[:, HALVES[hf]], ACT.Square).then_inc(squared, 1)
            ahead(act, FIRST["w_r"] + 2, split_act)
            after_slots(act, "lora_wa2")
            for bias, dst, base, done in (("a_w0", W_SIG, 0, decay_sig), ("a_a0", W_A, 4, iclr_sig)):
                for c in range(DC):
                    op = nc.scalar.activation(chan(dst)[:, c, :], bank[base + c // 2][:, (c % 2) * T:(c % 2 + 1) * T],
                                              ACT.Sigmoid, bias=col(bias, c))
                    if c % 2 == 1:
                        op.then_inc(done, 1)
            act.wait_ge(cum_ready, 1)
            nc.scalar.activation(buf(W_EP), buf(W_CUM), ACT.Exp, scale=-KAPPA).then_inc(decay_exp, 1)
            nc.scalar.activation(buf(W_EM), buf(W_CUM), ACT.Exp, scale=KAPPA).then_inc(decay_exp, 1)
            nc.scalar.activation(buf(W_SIG), buf(W_SIG), ACT.Exp, scale=-KAPPA).then_inc(decay_exp, 1)
            nc.scalar.activation(s_scale, last_e, ACT.Exp, scale=-KAPPA).then_inc(decay_exp, 1)
            for s in range(4):
                if s == 2:
                    act.wait_ge(rstd_ready, 1)
                    nc.scalar.activation(buf(W_RINV).rearrange("p (h n) -> p h n", n=N),
                                         spread(kk_inv.unsqueeze(2), [P, NT * H, N]), ACT.Copy).then_inc(kk_wide, 1)
                after_slots(act, "w_r", s + 1)
                nc.scalar.activation(buf(W_R, s * HALF, (s + 1) * HALF), bank[s][:, :], ACT.Copy).then_inc(r_evac, 1)
                if s == 0:
                    ahead(act, LAST["w_r"], split_act)
            xs_split_act(act, "v")
            ahead(act, FIRST["w_v"], split_act)
            after_slots(act, "lora_g")
            nc.scalar.activation(lora[:, 2 * T:3 * T], bank[0][:, 0:T], ACT.Sigmoid).then_inc(gate_hidden, 1)
            nc.scalar.activation(lora[0:32, 3 * T:4 * T], bank[0][0:32, T:2 * T], ACT.Sigmoid).then_inc(gate_hidden, 1)
            ahead(act, FIRST["w_v"] + 1, split_act)
            after_slots(act, "lora_g2")
            for j in range(4):
                nc.scalar.activation(buf(W_G, j * HALF, (j + 1) * HALF), bank[j][:, :], ACT.Copy).then_inc(g_evac, 1)
            ahead(act, FIRST["w_v"] + 2, split_act)
            after_slots(act, "w_v", 1)
            ahead(act, LAST["w_v"], split_act)
            act.wait_ge(bonus_ready, 1)
            for j in range(6):
                if j == 4:
                    act.wait_ge(bonus_summed, 1)
                    nc.scalar.activation(bon, bank[6][:, 0:NT * H], ACT.Copy).then_inc(bonus_copied, 1)
                act.wait_ge(tok_mm, j + 1)
                dst = buf(W_TOK, j * HALF, (j + 1) * HALF) if j < 4 else buf(W_RHS1, D + (j - 4) * HALF, D + (j - 3) * HALF)
                nc.scalar.activation(dst, bank[4 + j % 4][:, :], ACT.Copy).then_inc(tok_evac, 1)
            after_slots(act, "w_v")
            for j in range(4):
                nc.scalar.activation(buf(W_V, j * HALF, (j + 1) * HALF), bank[j][:, :], ACT.Copy).then_inc(v_evac, 1)
            for l in range(PAIR_BANKS):
                a, first = l // 8, bank_heads(l)[0]
                act.wait_ge(prod_mm, l + 1)
                if l == 8:
                    act.wait_ge(y_saved, 16)
                src = bank[4 + l % 4][:, :].rearrange("p (h x t) -> p h x t", x=2, t=P)
                nc.scalar.activation(heads(W_LK[a])[:, first:first + 3:2, :], src[:, :, 0, :], ACT.Copy)
                nc.scalar.activation(heads(W_RK[a])[:, first:first + 3:2, :], src[:, :, 1, :], ACT.Copy).then_inc(prod_evac, 1)
            for s in range(1, ROUNDS, 2):
                for g in range(6):
                    act.wait_ge(u_mm, before_round(s) + g + 1)
                    if g < 2:
                        dst, src = u0[:, g * HALF:(g + 1) * HALF], bank[g][:, :]
                    else:
                        dst = sides(W_U1)[:, :, 4 * (g - 2):4 * (g - 1), :]
                        src = bank[g][:, :].rearrange("p (h x n) -> p x h n", x=2, n=N)
                    nc.scalar.activation(dst, src, ACT.Copy).then_inc(u_sol, 1)
            act.wait_ge(q_mm, 1)
            for j in range(2):
                nc.scalar.activation(q_turned[:, 4 * j:4 * j + 4, :], bank[1 + j][:, :].rearrange("p (c t) -> p c t", t=P),
                                     ACT.Copy).then_inc(q_in, 1)
            act.wait_ge(state_mm, 1)
            ahead(act, FIRST["w_o"] + 1, split_act)
            act.wait_ge(u1_mm, 1)
            ahead(act, FIRST["w_o"] + 2, split_act)
            act.wait_ge(u1_ready, 2)
            ahead(act, LAST["w_o"], split_act)
            for a in range(NT):
                act.wait_ge(yc_ready, a + 1)
                nc.scalar.activation(toks(W_YSQ)[:, a, :], toks(W_YC)[:, a, :], ACT.Square).then_inc(squared, 1)
                act.wait_ge(o_mm, a + 1)
                for q in range(2):
                    nc.scalar.activation(chan(W_OT, arena12)[:, 4 * q:4 * q + 4, a * P:(a + 1) * P],
                                         bank[2 * a + q][:, :].rearrange("p (c t) -> p c t", t=P), ACT.Copy).then_inc(o_in, 1)

        def rwkv_dve(dve):
            hT, dx = chan(W_HT), chan(W_DX)
            turned_out(dve, TURN_PRE0)
            nc.vector.tensor_scalar(dx[:, :, 0:1], hT[:, :, 0:1], -1.0, None, ALU.mult)
            link(dve, nc.vector.tensor_tensor(dx[:, :, 1:T], hT[:, :, 0:T - 1], hT[:, :, 1:T], ALU.subtract))
            for name, row in MIXES:
                for c in range(DC):
                    op = nc.vector.scalar_tensor_tensor(chan(W_XS[name])[:, c, :], dx[:, c, :], col("a_mu", row * DC + c),
                                                        hT[:, c, :], ALU.mult, ALU.add)
                    if name == "r" and c == DC // 2 - 1:
                        xs_split_lo(dve, nc.vector, "k")
                op.then_inc(mix_done, 1)
            xs_split_lo(dve, nc.vector, "r")
            kT, kk, sig, cum, aT = chan(W_K), chan(W_KK), chan(W_SIG), chan(W_CUM), chan(W_A)
            for hf in range(2):
                dve.wait_ge(k_evac, 2 * hf + 2)
                for c in range(4 * hf, 4 * hf + 4):
                    op = nc.vector.tensor_scalar(kk[:, c, :], kT[:, c, :], col("a_k_k", c), None, ALU.mult)
                op.then_inc(kk_ready, 1)
            dve.wait_ge(decay_sig, 4)
            for c in range(DC):
                for a in range(NT):
                    t = slice(a * P, (a + 1) * P)
                    op = nc.vector.tensor_tensor_scan(cum[:, c, t], const("ones"), sig[:, c, t], 0.0, ALU.mult, ALU.add)
            link(dve, op)
            tiles = buf(W_CUM).rearrange("p (n t) -> p n t", t=P)
            link(dve, nc.vector.tensor_copy(mid, tiles[:, :, P // 2 - 1]))
            link(dve, nc.vector.tensor_tensor(tiles, tiles, spread(mid.unsqueeze(2), [P, 16, P]), ALU.subtract))
            nc.vector.tensor_tensor(last_e, tiles[:, 0:16:2, P - 1], mid[:, 1:16:2], ALU.add)
            nc.vector.tensor_tensor(buf(W_SIG), buf(W_CUM), buf(W_SIG), ALU.subtract).then_inc(cum_ready, 1)
            dve.wait_ge(kk_summed, 1)
            nc.vector.tensor_scalar(kk_inv, bank[4][:, 0:NT * H], 1e-24, None, ALU.max).then_inc(var_ready, 1)
            dve.wait_ge(mix_done, len(MIXES))
            dve.wait_ge(iclr_sig, 4)
            for c in range(DC):
                op = nc.vector.tensor_scalar(chan(W_T1)[:, c, :], aT[:, c, :], 1.0, col("a_k_a", c), ALU.subtract, ALU.mult)
            link(dve, op)
            dve.wait_ge(kk_ready, 2)
            k_new = step(nc.vector.scalar_tensor_tensor(buf(W_K), buf(W_T1), 1.0, buf(W_K), ALU.add, ALU.mult))
            dve.wait_ge(decay_exp, 4)
            for hf in range(2):
                at = HALVES[hf]
                dve.wait_ge(kk_turned, hf + 1)
                for j in (2 * hf, 2 * hf + 1):
                    cells = buf(W_KK, j * HALF, (j + 1) * HALF)
                    op = nc.vector.tensor_tensor(cells, cells, bank[4 + j][:, :], ALU.mult)
                link(dve, op)
                link(dve, nc.vector.tensor_tensor(buf(W_A)[:, at], buf(W_A)[:, at], buf(W_KK)[:, at], ALU.mult))
                link(dve, nc.vector.tensor_tensor(buf(W_ADD)[:, at], buf(W_A)[:, at], buf(W_EM)[:, at], ALU.mult))
                nc.vector.scalar_tensor_tensor(buf(W_REMOVE)[:, at], buf(W_KK)[:, at], -1.0, buf(W_SIG)[:, at],
                                               ALU.mult, ALU.mult).then_inc(removal_ready, 1)

            dve.wait_ge(r_evac, 4)
            nc.vector.tensor_tensor(buf(W_QUERY), buf(W_R), buf(W_EP), ALU.mult).then_inc(queries_ready, 1)

            for l in range(PAIR_BANKS):
                a, first = l // 8, bank_heads(l)[0]
                src = bank[4 + l % 4][:, :].rearrange("p (h x t) -> p h x t", x=2, t=P)
                dve.wait_ge(n_mm, l + 1)
                for x, (dst, mask) in enumerate(((W_N, "before"), (W_RB, "upto"))):
                    nc.vector.tensor_tensor(heads(dst[a])[:, first:first + 3:2, :], src[:, :, x, :],
                                            spread(const(mask).unsqueeze(1), [P, 2, P]), ALU.mult).then_inc(n_masked, 1)
            dve.wait_ge(dve_step, k_new)
            nc.vector.tensor_tensor(buf(W_KEY), buf(W_K), buf(W_EM), ALU.mult).then_inc(keys_ready, 1)
            dve.wait_ge(keys_ready, 1)
            for c in range(DC):
                op = nc.vector.scalar_tensor_tensor(kT[:, c, :], chan(W_R)[:, c, :], col("a_r_k", c), kT[:, c, :],
                                                    ALU.mult, ALU.mult)
            op.then_inc(bonus_ready, 1)
            dve.wait_ge(removal_ready, 2)
            link(dve, nc.vector.memset(buf(W_SOLVE, BS * BS, 2 * BS * BS), 0.0))
            link(dve, nc.vector.memset(buf(W_SOLVE, BS * BS, 2 * BS * BS)[:, 0:BS * BS:BS + 1], 1.0))
            dve.wait_ge(nd_landed, 16)
            for j in range(BS - 1):
                m, w = j + 1, BS - 1 - j
                outer = solve_tmp[:, 0:m * w].rearrange("p (s t) -> p s t", t=w)
                link(dve, nc.vector.tensor_tensor(outer, spread(yd[:, 0:m, j:j + 1], [P, m, w]),
                                                  spread(nd[:, j:j + 1, j + 1:BS], [P, m, w]), ALU.mult))
                op = nc.vector.tensor_tensor(yd[:, 0:m, j + 1:BS], yd[:, 0:m, j + 1:BS], outer, ALU.add)
                if j < BS - 2:
                    link(dve, op)
            op.then_inc(solved, 1)
            for g in range(4):
                at = slice(g % 2 * 8, g % 2 * 8 + 8)
                dve.wait_ge(prod_evac, 4 * (g + 1))
                nc.vector.tensor_tensor(heads(W_LK[g // 2])[:, at], heads(W_LK[g // 2])[:, at],
                                        spread(const("before").unsqueeze(1), [P, 8, P]), ALU.mult).then_inc(lk_masked, 1)
            for s in range(0, ROUNDS, 2):
                for g in range(4 if s == 0 else 6):
                    dve.wait_ge(u_mm, before_round(s) + g + 1)
                    cells = slice(g % 2 * HALF, (g % 2 + 1) * HALF)
                    if s == 0:
                        if g == 0:
                            dve.wait_ge(tok_mm, 6)
                        if g == 2:
                            dve.wait_ge(bonus_summed, 1)
                        op = nc.vector.tensor_copy((rhs0 if g < 2 else buf(W_RHS1, 0, D))[:, cells], bank[g][:, :])
                    elif g < 2:
                        op = nc.vector.tensor_tensor(sum0[:, cells], bank[g][:, :], rhs0[:, cells], ALU.add)
                    else:
                        at = (slice(None), slice(None), slice(4 * (g - 2), 4 * (g - 1)))
                        op = nc.vector.tensor_tensor(sides(W_SUM1)[at], bank[g][:, :].rearrange("p (h x n) -> p x h n", x=2, n=N),
                                                     sides(W_RHS1)[at], ALU.add)
                    op.then_inc(u_rhs, 1)
            dve.wait_ge(state_mm, 1)
            nc.vector.tensor_tensor(s1.rearrange("p (c n) -> p c n", n=N), bank[0][:, :].rearrange("p (c n) -> p c n", n=N),
                                    spread(s_scale.unsqueeze(2), [P, HP, N]), ALU.mult).then_inc(state_ready, 1)
            emitted[dve] = FIRST["w_o"]
            dve.wait_ge(split_ready, SPLIT_NO[LAST["w_v"]] + 1)
            ahead(dve, FIRST["w_o"] + 1, split_dve)
            dve.wait_ge(u1_mm, 1)
            for q in range(2):
                by_parity = lambda ap: ap.rearrange("p (c g n) -> p g c n", g=2, n=N)[:, q]
                nc.vector.tensor_tensor(by_parity(u1), bank[3 + q][:, :].rearrange("p (c n) -> p c n", n=N),
                                        by_parity(buf(W_U1, 0, D)), ALU.add).then_inc(u1_ready, 1)
            ahead(dve, FIRST["w_o"] + 2, split_dve)
            dve.wait_ge(u_mm, before_round(ROUNDS))
            for a in range(NT):
                yc = toks(W_YC)[:, a, :]
                stat = slice(a * H, (a + 1) * H)
                for q in range(2):
                    dve.wait_ge(ymm, 2 * a + q + 1)
                    op = nc.vector.tensor_reduce(y_sum[:, a * H + q:(a + 1) * H:2], bank[Y_BANK[a][q]][:, :].rearrange(
                        "p (c n) -> p c n", n=N), AX, ALU.add)
                link(dve, op)
                link(dve, nc.vector.tensor_scalar(y_mean[:, stat], y_sum[:, stat], -1.0 / N, None, ALU.mult))
                for q in range(2):
                    op = nc.vector.tensor_tensor(yc.rearrange("p (c g n) -> p g c n", g=2, n=N)[:, q],
                                                 bank[Y_BANK[a][q]][:, :].rearrange("p (c n) -> p c n", n=N),
                                                 spread(y_mean[:, a * H + q:(a + 1) * H:2].unsqueeze(2), [P, HP, N]), ALU.add)
                op.then_inc(yc_ready, 1)
                dve.wait_ge(squared, 2 + a + 1)
                link(dve, nc.vector.tensor_reduce(y_sq[:, stat], toks(W_YSQ)[:, a, :].rearrange("p (h n) -> p h n", n=N),
                                                  AX, ALU.add))
                nc.vector.tensor_scalar(y_var[:, stat], y_sq[:, stat], 1.0 / N, LNX_EPS, ALU.mult, ALU.add).then_inc(var_ready, 1)
                dve.wait_ge(yc_ready, a + 1)
                dve.wait_ge(rstd_ready, 1 + a + 1)
                y32 = yc.rearrange("p (h n) -> p h n", n=N)
                link(dve, nc.vector.tensor_tensor(y32, y32, spread(y_rstd[:, stat].unsqueeze(2), [P, H, N]), ALU.mult))
                dve.wait_ge(c_ready, a + 1)
                link(dve, nc.vector.tensor_tensor(yc, yc, toks(W_G)[:, a, :], ALU.mult))
                nc.vector.tensor_tensor(yc, yc, toks(W_C)[:, a, :], ALU.add).then_inc(o_ready, 1)
                ahead(dve, LAST["w_o"], split_dve)
                for q in range(2):
                    dve.wait_ge(o_in, 2 * a + q + 1)
                    at = (slice(None), slice(4 * q, 4 * q + 4), slice(a * P, (a + 1) * P))
                    nc.vector.tensor_tensor(chan(W_OT_LO, arena12)[at], bank[2 * a + q][:, :].rearrange("p (c t) -> p c t", t=P),
                                            chan(W_OT, arena12)[at].bitcast(F32), ALU.subtract).then_inc(o_split, 1)

        def rwkv_pool(pool):
            ahead(pool, FIRST["w_r"] + 2, split_pool)
            pool.wait_ge(var_ready, 1)
            nc.gpsimd.tensor_tensor(kk_inv, kk_inv, minus_half, ALU.pow).then_inc(rstd_ready, 1)
            ahead(pool, LAST["w_r"], split_pool)
            pool.wait_ge(xs_split, XS_SPLIT["r"])
            xs_split_lo(pool, nc.gpsimd, "v")
            ahead(pool, LAST["w_v"], split_pool)
            pool.wait_ge(n_saved, 16 * NT * NB)
            for m in W_N:
                nc.gpsimd.tensor_tensor(heads(m), heads(m), spread(const("off").unsqueeze(1), [P, H, P]),
                                        ALU.mult).then_inc(n_cut, 1)
            after_slots(pool, "w_v")
            for m in W_Z:
                nc.gpsimd.memset(buf(m), 0.0).then_inc(z_zeroed, 1)
            for a in range(NT):
                pool.wait_ge(prod_evac, 8 * (a + 1))
                nc.gpsimd.tensor_tensor(heads(W_RK[a]), heads(W_RK[a]), spread(const("upto").unsqueeze(1), [P, H, P]),
                                        ALU.mult).then_inc(rk_masked, 1)
            pool.wait_ge(prod_mm, PAIR_BANKS)
            pool.dma_start(buf(W_LNX, 0, D), A["a_lnx_w"][0].partition_broadcast(P)).then_inc(lnx_landed, 16)
            pool.dma_start(buf(W_LNX, D, 2 * D), A["a_lnx_b"][0].partition_broadcast(P)).then_inc(lnx_landed, 16)
            pool.wait_ge(lnx_landed, 32)
            pool.wait_ge(bonus_copied, 1)
            pool.wait_ge(u_mm, before_round(ROUNDS))
            steps_done = 0
            for a in range(NT):
                c, g = toks(W_C)[:, a, :], toks(W_G)[:, a, :]
                nc.gpsimd.tensor_tensor(c.rearrange("p (h n) -> p h n", n=N), toks(W_V)[:, a, :].rearrange("p (h n) -> p h n", n=N),
                                        spread(bon[:, a * H:(a + 1) * H].unsqueeze(2), [P, H, N]), ALU.mult).then_inc(c_step, 1)
                for in1, op in ((buf(W_LNX, D, 2 * D), ALU.add), (g, ALU.mult)):
                    steps_done += 1
                    pool.wait_ge(c_step, steps_done)
                    nc.gpsimd.tensor_tensor(c, c, in1, op).then_inc(c_step, 1)
                steps_done += 1
                pool.wait_ge(c_step, steps_done)
                nc.gpsimd.tensor_tensor(g, g, buf(W_LNX, 0, D), ALU.mult).then_inc(c_ready, 1)
                if a == 0:
                    pool.wait_ge(var_ready, 1 + 1)
                    nc.gpsimd.tensor_tensor(y_rstd[:, 0:H], y_var[:, 0:H], minus_half[:, 0:H], ALU.pow).then_inc(rstd_ready, 1)
            pool.wait_ge(var_ready, 1 + 2)
            nc.gpsimd.tensor_tensor(y_rstd[:, H:2 * H], y_var[:, H:2 * H], minus_half[:, 0:H], ALU.pow).then_inc(rstd_ready, 1)

        def rwkv_blocks_sp(sp):
            for a in range(NT):
                for b in range(NB):
                    if b == 0:
                        sp.wait_ge(n_masked, PAIR_BANKS * (a + 1))
                    sp.dma_start(n_dram[a, :, b].rearrange("h s t -> s h t"),
                                 heads(W_N[a])[b * BS:(b + 1) * BS, :, b * BS:(b + 1) * BS]).then_inc(n_saved, 16)
            sp.wait_ge(n_saved, 16 * NT * NB)
            sp.wait_ge(kk_turned, 2)
            sp.dma_start(buf(W_SOLVE, 0, BS * BS), n_dram.rearrange("a h b s t -> (a h b) (s t)")).then_inc(nd_landed, 16)
            sp.wait_ge(solved, 1)
            sp.dma_start(y_dram.rearrange("a h b s t -> (a h b) (s t)"), buf(W_SOLVE, BS * BS, 2 * BS * BS)).then_inc(y_saved, 16)
            sp.wait_ge(y_saved, 16)
            sp.wait_ge(z_zeroed, NT)
            for a in range(NT):
                for b in range(NB):
                    sp.dma_start(heads(W_Z[a])[b * BS:(b + 1) * BS, :, b * BS:(b + 1) * BS],
                                 y_dram[a, :, b].rearrange("h s t -> s h t")).then_inc(z_landed, 16)

        M_H, M_XKV, M_TOK, M_LATT, M_K, M_Q, M_V, M_ROT, M_S, M_PT, M_OT = 0, 1, 2, 3, 4, 6, 8, 9, 10, 11, 12
        M_H_LO, M_XKV_LO, M_LATT_LO, M_OT_LO = 10, 11, 0, 1
        ckv = buf(M_TOK, 0, NT * KV_LORA).rearrange("p (a n) -> p a n", a=NT)
        cq = buf(M_TOK, 512, 512 + NT * Q_LORA).rearrange("p (a n) -> p a n", a=NT)
        kr = buf(M_TOK, 1280, 1280 + NT * QK).rearrange("p (a n) -> p a n", a=NT)
        kraw = buf(M_TOK, 1472, 1472 + NT * ROPE).rearrange("p (a n) -> p a n", a=NT)
        krt = [buf(M_TOK, 1536 + 32 * i, 1568 + 32 * i).rearrange("p (a n) -> p a n", a=NT) for i in range(4)]
        down = ((bank[4], bank[6]), (bank[5], bank[7]))
        lat = chan2(M_LATT, M_LATT_LO)
        kT = bufs(M_K, 2).rearrange("p (h t) -> p h t", t=T)
        qT = bufs(M_Q, 2).rearrange("p (h t) -> p h t", t=T)
        S_BUFS = 5
        s_buf = [buf(M_S, i * 384, (i + 1) * 384) for i in range(S_BUFS)]
        pt_buf = [buf(M_PT, i * 384, (i + 1) * 384) for i in range(2)]
        lat_sum, lat_var, lat_rstd = small(4), small(4), small(4)
        sm_nmax, sm_sum, sm_inv = small(2 * H), small(2 * H), small(2 * H)
        (lat_ready, lat_turned, lat_hi, lat_in, krope_in, nope_evac, vh_evac, q_evac, perm_mm, q_sin, q_cos, q_roped, s_mm, sm_max,
         sm_exp, p_ready, pt_mm, pt_evac, pv_mm, inv_ready, p_ready_act) = (
            sem(n) for n in ("lat_ready", "lat_turned", "lat_hi", "lat_in", "krope_in", "nope_evac", "vh_evac",
                             "q_evac", "perm_mm", "q_sin", "q_cos", "q_roped", "mla_s_mm", "mla_max", "mla_exp", "mla_p_ready",
                             "mla_pt_mm", "mla_pt_evac", "mla_pv_mm", "mla_inv_ready", "mla_p_ready_act"))

        rot = slice(NOPE, QK)

        def rope_table(name):
            return spread(cst[rot, CONST_AT[name]:CONST_AT[name] + T].unsqueeze(1), [ROPE, 2, T])

        def swapped_q(g):
            return buf(M_ROT, g % 4 * HALF, (g % 4 + 1) * HALF)[rot, :].rearrange("p (h t) -> p h t", t=T)

        def mla_pe(pe):
            downs = (("kv_down", chan2(M_XKV, M_XKV_LO), TURN_XKV, KV_LORA + ROPE),
                     ("q_down", chan2(M_H, M_H_LO), TURN_PRE2, Q_LORA))
            for a in range(NT):
                xn_turn(pe, XN_OF[2] + 2 * a, a, XN_KV, 4)
                xn_turn(pe, XN_OF[2] + 2 * a + 1, a, XN, 0)
                for n, (name, src, turn, width) in enumerate(downs):
                    for s in range(2):
                        w = split_weights(pe, FIRST[name] + s)
                        turned_out(pe, turn, a, s)
                        for kk in range(4):
                            k = 4 * s + kk
                            mm = product(down[n][a][:, 0:width], both(src, slice(None), k, slice(a * P, (a + 1) * P)),
                                         both(w, slice(None), slice(kk * width, (kk + 1) * width)), k == 0, k == DC - 1)
                        if a == NT - 1:
                            mm.then_inc(slot_done, 1)
            pe.wait_ge(lat_ready, 1)
            for a in range(NT):
                for c in range(2):
                    nc.tensor.transpose(bank[0][:, c * T + a * P:c * T + (a + 1) * P], ckv[:, a, c * P:(c + 1) * P], ident)
                for c in range(3):
                    nc.tensor.transpose(bank[1 + c // 2][:, (c % 2) * T + a * P:(c % 2) * T + (a + 1) * P],
                                        cq[:, a, c * P:(c + 1) * P], ident)
                mm = nc.tensor.transpose(bank[3][0:QK, a * P:(a + 1) * P], kr[:, a, :], ident)
            mm.then_inc(lat_turned, 1)
            pe.wait_ge(lat_in, 5)
            for s in range(2):
                w = [v.rearrange("p (k h n) -> p k h n", k=2, n=2 * N) for v in split_weights(pe, FIRST["kv_up"] + s)]
                for i in range(8):
                    if s == 0 and i == 6:
                        pe.wait_ge(krope_in, 1)
                    if s == 1 and i % 2 == 0:
                        pe.wait_ge(nope_evac, i // 2 + 1)
                    for k in range(2):
                        mm = product(bank[i // 2][0:NOPE, (i % 2) * T:(i % 2 + 1) * T],
                                     both(w, slice(None), k, i, slice(0, NOPE)), both(lat, slice(None), k), k == 0, k == 1)
                for a in range(NT):
                    for k in range(2):
                        mm = product(bank[4 + 2 * s + a][:, :].rearrange("p (h n) -> p h n", n=N),
                                     both(lat, slice(None), k, slice(a * P, (a + 1) * P)),
                                     both(w, slice(None), k, slice(None), slice(NOPE, 2 * N)), k == 0, k == 1)
                mm.then_inc(slot_done, 1)
            def swapped(g):
                pe.wait_ge(q_evac, g + 1)
                if g >= 4:
                    pe.wait_ge(q_sin, g - 3)
                nc.tensor.matmul(bank[4 + g % 4][0:QK, :], const("perm")[0:QK, :], qT[0:QK, 2 * g:2 * g + 2, :],
                                 start=True, stop=True).then_inc(perm_mm, 1)

            pe.wait_ge(nope_evac, 8)
            pe.wait_ge(vh_evac, 4)
            for s in range(4):
                w = [v[:, 0:3 * 4 * QK].rearrange("p (k n) -> p k n", k=3) for v in split_weights(pe, FIRST["q_up"] + s)]
                for i in range(4):
                    g = 2 * s + i // 2
                    if g >= 4 and i % 2 == 0:
                        pe.wait_ge(q_evac, g - 3)
                    for k in range(3):
                        mm = product(bank[g % 4][0:QK, (i % 2) * T:(i % 2 + 1) * T],
                                     both(w, slice(None), k, slice(i * QK, (i + 1) * QK)), both(lat, slice(None), 2 + k),
                                     k == 0, k == 2)
                mm.then_inc(slot_done, 1)
                if s > 0:
                    swapped(2 * s - 2)
                    swapped(2 * s - 1)
            swapped(6)
            swapped(7)
            pe.wait_ge(q_evac, 8)
            v = toks(M_V)

            def scores(h):
                if h >= 2:
                    pe.wait_ge(sm_max, h - 1)
                pe.wait_ge(q_roped, h // 2 + 1)
                for a, cells in enumerate((slice(0, P), slice(P, 3 * P))):
                    mm = nc.tensor.matmul(bank[h % 2][:, cells], qT[0:QK, h, a * P:(a + 1) * P],
                                          kT[0:QK, h, 0:(a + 1) * P], start=True, stop=True)
                mm.then_inc(s_mm, 1)

            def turn_p(h):
                pe.wait_ge((p_ready, p_ready_act)[h % 2], h // 2 + 1)
                if h >= 2:
                    pe.wait_ge(pt_evac, h - 1)
                for i in range(3):
                    mm = nc.tensor.transpose(bank[2 + h % 2][:, i * P:(i + 1) * P], s_buf[h % S_BUFS][:, i * P:(i + 1) * P], ident)
                mm.then_inc(pt_mm, 1)

            def values(h):
                pe.wait_ge(pt_evac, h + 1)
                c, rows_, hv = h // 2, slice((h % 2) * N, (h % 2 + 1) * N), slice(h * N, (h + 1) * N)
                dst = bank[4 + c // 2][rows_, (c % 2) * T:(c % 2 + 1) * T]
                pt = pt_buf[h % 2]
                nc.tensor.matmul(dst, v[:, 0, hv], pt[:, 0:T], start=True, stop=False)
                nc.tensor.matmul(dst[:, P:T], v[:, 1, hv], pt[:, T:3 * P], start=False, stop=True).then_inc(pv_mm, 1)

            scores(0)
            scores(1)
            for h in range(H):
                if h == 1:
                    pe.wait_ge(q_sin, 8)
                if h + 2 < H:
                    scores(h + 2)
                if h >= 1:
                    turn_p(h - 1)
                if h >= 2:
                    values(h - 2)
            turn_p(H - 1)
            values(H - 2)
            values(H - 1)
            pe.wait_ge(o_split, 4 + 4)
            wide2(pe, FIRST["o_w"], 4, chan2(M_OT, M_OT_LO), 4, rows=True)

        def mla_act(act):
            after_slots(act, "kv_down")
            for i in range(4):
                if i == 2:
                    after_slots(act, "q_down")
                n = (KV_LORA, Q_LORA)[i // 2]
                nc.scalar.activation(buf(XN, i * HALF, i * HALF + n), down[i // 2][i % 2][:, 0:n], ACT.Square,
                                     accum_out=lat_sum[:, i:i + 1]).then_inc(squared, 1)
            ahead(act, FIRST["kv_up"], split_act)
            act.wait_ge(lat_turned, 1)
            for c in range(5):
                nc.scalar.activation(lat[0][:, c, :], bank[c // 2][:, (c % 2) * T:(c % 2 + 1) * T], ACT.Copy,
                                     scale=col("kv_a_norm_g", c) if c < 2 else col("q_norm_g", c - 2)).then_inc(lat_hi, 1)
            nc.scalar.activation(kT[NOPE:QK, :, :], spread(bank[3][NOPE:QK, 0:T].unsqueeze(1), [ROPE, H, T]),
                                 ACT.Copy).then_inc(krope_in, 1)
            ahead(act, FIRST["q_up"] + 1, split_act)
            for s in range(2):
                after_slots(act, "kv_up", s + 1)
                for j in range(4):
                    h = 8 * s + 2 * j
                    nc.scalar.activation(kT[0:NOPE, h:h + 2, :], bank[j][0:NOPE, :].rearrange("p (h t) -> p h t", t=T),
                                         ACT.Copy).then_inc(nope_evac, 1)
                ahead(act, FIRST["q_up"] + 2 + s, split_act)
            for g in range(8):
                after_slots(act, "q_up", g // 2 + 1)
                nc.scalar.activation(qT[0:QK, 2 * g:2 * g + 2, :], bank[g % 4][0:QK, :].rearrange("p (h t) -> p h t", t=T),
                                     ACT.Copy).then_inc(q_evac, 1)

            def exps(h):
                act.wait_ge(sm_max, h + 1)
                for a, (lo, hi) in enumerate(((0, P), (P, 3 * P))):
                    op = nc.scalar.activation(s_buf[h % S_BUFS][:, lo:hi], s_buf[h % S_BUFS][:, lo:hi], ACT.Exp,
                                              bias=sm_nmax[:, 2 * h + a:2 * h + a + 1],
                                              accum_out=sm_sum[:, 2 * h + a:2 * h + a + 1])
                op.then_inc(sm_exp, 1)

            def normalize(h):
                act.wait_ge(inv_ready, h // 2 + 1)
                for a, (lo, hi) in enumerate(((0, P), (P, 3 * P))):
                    op = nc.scalar.activation(s_buf[h % S_BUFS][:, lo:hi], s_buf[h % S_BUFS][:, lo:hi], ACT.Copy,
                                              scale=sm_inv[:, 2 * h + a:2 * h + a + 1])
                op.then_inc(p_ready_act, 1)

            def evac(h):
                act.wait_ge(pt_mm, h + 1)
                if h >= 2:
                    act.wait_ge(pv_mm, h - 1)
                nc.scalar.activation(pt_buf[h % 2], bank[2 + h % 2][:, 0:3 * P], ACT.Copy).then_inc(pt_evac, 1)

            def outputs(b):
                act.wait_ge(pv_mm, 4 * (b + 1))
                nc.scalar.activation(buf(M_OT, b * HALF, (b + 1) * HALF, arena12), bank[4 + b][:, :], ACT.Copy).then_inc(o_in, 1)

            ahead(act, FIRST["o_w"] + 2, split_act)
            for h in range(H):
                exps(h)
                if h >= 2 and h % 2 == 0:
                    normalize(h - 1)
                if h >= 2:
                    evac(h - 2)
                if h >= 6 and h % 4 == 2:
                    outputs(h // 4 - 1)
            normalize(H - 1)
            evac(H - 2)
            evac(H - 1)
            outputs(3)
            ahead(act, LAST["o_w"], split_act)

        def mla_dve(dve):
            nc.vector.memset(kr[:, :, 0:NOPE], 0.0)
            dve.wait_ge(squared, 4 + 4)
            link(dve, nc.vector.tensor_scalar(lat_var[:, 0:2], lat_sum[:, 0:2], 1.0 / KV_LORA, EPS, ALU.mult, ALU.add))
            nc.vector.tensor_scalar(lat_var[:, 2:4], lat_sum[:, 2:4], 1.0 / Q_LORA, EPS, ALU.mult, ALU.add).then_inc(var_ready, 1)
            for a in range(NT):
                op = nc.vector.tensor_copy(kraw[:, a, :], down[0][a][:, KV_LORA:KV_LORA + ROPE])
            link(dve, op)
            half = ROPE // 2
            x1, x2 = kraw[:, :, 0:half], kraw[:, :, half:ROPE]
            cos, sin = (const(n).rearrange("p (a n) -> p a n", a=NT) for n in ("kcos", "ksin"))
            for i, (x, f) in enumerate(((x1, cos), (x2, sin), (x1, sin), (x2, cos))):
                op = nc.vector.tensor_tensor(krt[i], x, f, ALU.mult)
            link(dve, op)
            nc.vector.tensor_tensor(kr[:, :, NOPE:NOPE + half], krt[0], krt[1], ALU.subtract)
            nc.vector.tensor_tensor(kr[:, :, NOPE + half:QK], krt[2], krt[3], ALU.add)
            dve.wait_ge(rstd_ready, 3 + 1)
            for i in range(4):
                n, dst = ((KV_LORA, ckv), (Q_LORA, cq))[i // 2]
                op = nc.vector.tensor_scalar(dst[:, i % 2, :], down[i // 2][i % 2][:, 0:n], lat_rstd[:, i:i + 1], None, ALU.mult)
            op.then_inc(lat_ready, 1)
            ahead(dve, FIRST["kv_up"], split_dve)
            for c in range(5):
                dve.wait_ge(lat_hi, min(c // 2 * 2 + 2, 5))
                nc.vector.scalar_tensor_tensor(lat[1][:, c, :], bank[c // 2][:, (c % 2) * T:(c % 2 + 1) * T],
                                               col("kv_a_norm_g", c) if c < 2 else col("q_norm_g", c - 2), lat[0][:, c, :].bitcast(F32),
                                               ALU.mult, ALU.subtract).then_inc(lat_in, 1)
            ahead(dve, FIRST["q_up"] + 1, split_dve)
            for s in range(2):
                after_slots(dve, "kv_up", s + 1)
                for a in range(NT):
                    nc.vector.tensor_copy(toks(M_V)[:, a, s * HALF:(s + 1) * HALF], bank[4 + 2 * s + a][:, :]).then_inc(vh_evac, 1)
                ahead(dve, FIRST["q_up"] + 2 + s, split_dve)
            def maxima(h):
                dve.wait_ge(s_mm, h + 1)
                if h >= S_BUFS:
                    dve.wait_ge(pt_mm, h - S_BUFS + 1)
                s = s_buf[h % S_BUFS]
                link(dve, nc.vector.scalar_tensor_tensor(s, bank[h % 2][:, 0:3 * P], MLA_SCALE, const("maskb"), ALU.mult, ALU.add))
                nc.vector.tensor_reduce(sm_nmax[:, 2 * h:2 * h + 1], s[:, 0:P], AX, ALU.max, negate=True)
                nc.vector.tensor_reduce(sm_nmax[:, 2 * h + 1:2 * h + 2], s[:, P:3 * P], AX, ALU.max, negate=True).then_inc(sm_max, 1)

            def normalize(h):
                dve.wait_ge(sm_exp, h + 1)
                inverse = nc.vector.reciprocal(sm_inv[:, 2 * h:2 * h + 2], sm_sum[:, 2 * h:2 * h + 2])
                if h % 2 == 1:
                    inverse.then_inc(inv_ready, 1)
                    return
                link(dve, inverse)
                for a, (lo, hi) in enumerate(((0, P), (P, 3 * P))):
                    op = nc.vector.tensor_scalar(s_buf[h % S_BUFS][:, lo:hi], s_buf[h % S_BUFS][:, lo:hi],
                                                 sm_inv[:, 2 * h + a:2 * h + a + 1], None, ALU.mult)
                op.then_inc(p_ready, 1)

            def outputs(b):
                dve.wait_ge(o_in, 4 + b + 1)
                at = slice(b * HALF, (b + 1) * HALF)
                nc.vector.tensor_tensor(buf(M_OT_LO, mem=arena12)[:, at], bank[4 + b][:, :], buf(M_OT, mem=arena12)[:, at].bitcast(F32), ALU.subtract).then_inc(o_split, 1)

            def swapped_sin(g):
                dve.wait_ge(perm_mm, g + 1)
                if g >= 4:
                    dve.wait_ge(q_roped, g - 3)
                nc.vector.tensor_tensor(swapped_q(g), bank[4 + g % 4][rot, :].rearrange("p (h t) -> p h t", t=T),
                                        rope_table("sinT"), ALU.mult).then_inc(q_sin, 1)

            for g in range(8):
                swapped_sin(g)
            for h in range(H):
                maxima(h)
                if h >= 1:
                    normalize(h - 1)
                if h >= 7 and h % 4 == 3:
                    outputs(h // 4 - 1)
            normalize(H - 1)
            outputs(3)
            emitted[dve] = LAST["o_w"] + 1
            dve.wait_ge(split_ready, SPLIT_NO[LAST["o_w"]] + 1)

        def mla_pool(pool):
            pool.wait_ge(var_ready, 3 + 1)
            nc.gpsimd.tensor_tensor(lat_rstd, lat_var, minus_half[:, 0:4], ALU.pow).then_inc(rstd_ready, 1)
            for g in range(8):
                q = qT[rot, 2 * g:2 * g + 2, :]
                pool.wait_ge(perm_mm, g + 1)
                nc.gpsimd.tensor_tensor(q, q, rope_table("cosT"), ALU.mult).then_inc(q_cos, 1)
                pool.wait_ge(q_cos, g + 1)
                pool.wait_ge(q_sin, g + 1)
                nc.gpsimd.tensor_tensor(q, q, swapped_q(g), ALU.add).then_inc(q_roped, 1)
            pool.wait_ge(q_roped, 8)
            pool.wait_ge(split_ready, SPLIT_NO[LAST["q_up"]] + 1)
            for n in range(FIRST["o_w"], LAST["o_w"] + 1):
                split_lo(pool, nc.gpsimd, n)

        B_H, B_XC, B_XS, B_Z, B_GA, B_GS, B_QK, B_QR, B_QT, B_P, B_OT = 0, 1, 3, 4, 5, 6, 7, 8, 9, 10, 12
        B_H_LO, B_OT_LO, B_SQ_LO, B_T2_LO = 11, 9, 0, 9
        B_CB, B_XF, B_XB, B_LHS, B_E, B_Y, B_SQ = 11, 0, 2, 8, 17, 1, 2
        HD = (GH + GKV) * N
        xcT = bufs(B_XC, 2)[:, 0:XC * T].rearrange("p (c t) -> p c t", t=T)
        xc_acc = [buf(B_XC + 1, 1024 + i * T, 1024 + (i + 1) * T) for i in range(4)]
        qk = buf(B_QK, 0, NT * HD).rearrange("p (a n) -> p a n", a=NT)
        vg = buf(B_QK, NT * HD, NT * HD + NT * P).rearrange("p (a n) -> p a n", a=NT)
        qr = buf(B_QR, 0, NT * HD).rearrange("p (a n) -> p a n", a=NT)
        rot_tmp = [buf(B_QR, NT * HD + i * HD // 2, NT * HD + (i + 1) * HD // 2) for i in range(2)]
        qgT = buf(B_QT, 0, GJ * T).rearrange("p (j t) -> p j t", t=T)
        kgT = buf(B_QT, GJ * T, (GJ + 1) * T)
        qk_gain = buf(B_QT, (GJ + 1) * T, (GJ + 1) * T + HD)
        gp_buf = [buf(B_P, 0, HALF), buf(B_P, HALF, 2 * HALF), buf(B_E, 0, HALF)]
        gpt_buf = [buf(B_P, (2 + i) * HALF, (3 + i) * HALF) for i in range(2)]
        cb = [buf(B_CB, g * 768, (g + 1) * 768).rearrange("p (n l) -> p n l", l=P) for g in range(2)]
        seg_lhs = [buf(B_LHS, i * HALF, (i + 1) * HALF).rearrange("p (n l) -> p n l", l=P) for i in range(2)]
        e_buf = [buf(B_E, i * HALF, (i + 1) * HALF) for i in range(3)]
        carry_decay = buf(B_E, 3 * HALF, 3 * HALF + 4 * H)
        arena_small = buf(B_OT, GJ * T, SLOT)
        (dt_bias, a_log, dt_x, dt_n, dt_e, dt_l, dt, adt) = (
            arena_small[:, i * 64:(i + 1) * 64].rearrange("p (a h) -> p a h", a=NT) for i in range(8))
        d_skip = arena_small[:, 512:512 + H]
        qk_ss, qk_var, qk_rstd = (arena_small[:, 540 + 20 * i:560 + 20 * i] for i in range(3))
        g_max, g_nmax, g_sum, g_inv = (arena_small[:, 600 + 16 * i:616 + 16 * i] for i in range(4))
        yg_gain = buf(B_LHS, 0, D)
        yg_ss, yg_var, yg_rstd = (arena_small[:, 670 + 2 * i:672 + 2 * i] for i in range(3))
        (blk_params, kv_evac, dt_read, conv2_done, xc_done, qg_evac, z_evac, gate_evac, dt_neg, dt_exp, dt_ln, a_exp,
         adt_ready, qk_roped, qk_turned, qk_in, cb_mm, cb_in, xs_turned, xs_in, xd_f_ready, xd_b_ready) = (
            sem(n) for n in ("blk_params", "kv_evac", "dt_read", "conv2_done", "xc_done", "qg_evac", "z_evac",
                             "gate_evac", "dt_neg", "dt_exp", "dt_ln", "a_exp", "adt_ready", "qk_roped", "qk_turned",
                             "qk_in", "cb_mm", "cb_in", "xs_turned", "xs_in", "xd_f_ready", "xd_b_ready"))
        (carry_mm, carry_ready, carried, off_mm, off_scaled, lhs_ready, seg_mm, e_ready, m_ready, ssd_mm, dx_ready, yz_ready, yn_ready, yg_gain_landed, ssd_rows,
         attn_gated, mix_ready) = (
            sem(n) for n in ("carry_mm", "carry_ready", "carried", "off_mm", "off_scaled", "lhs_ready", "seg_mm", "e_ready", "m_ready", "ssd_mm", "dx_ready", "yz_ready", "yn_ready",
                             "yg_gain_landed", "ssd_rows", "attn_gated", "mix_ready"))
        B_MIX, B_T2, B_DX, B_GATED = 11, 10, 3, 3

        def block_pe(pe):
            h2 = chan2(B_H, B_H_LO)

            def tile(k, a):
                return both(h2, slice(None), k, slice(a * P, (a + 1) * P))

            for a in range(NT):
                xn_turn(pe, XN_OF[4] + a, a)
            turned_out(pe, TURN_PRE4)
            for s in range(2):
                w = [v[:, 0:4 * 288].rearrange("p (k n) -> p k n", n=288) for v in split_weights(pe, FIRST["kvdt"] + s)]
                for kk in range(4):
                    k = 4 * s + kk
                    for a in range(NT):
                        mm = product(bank[2 + a][:, 0:288], tile(k, a), both(w, slice(None), kk), k == 0, k == DC - 1)
                mm.then_inc(slot_done, 1)
            for s in range(6):
                w = [v.rearrange("p (k n) -> p k n", n=T) for v in split_weights(pe, FIRST["xbc"] + s)]
                if s >= 4:
                    pe.wait_ge(conv2_done, 2 * (s - 3))
                for n in range(2):
                    for k in range(DC):
                        mm = product(bank[4 + s % 4][:, n * T:(n + 1) * T], both(w, slice(None), k, slice(n * P, (n + 1) * P)),
                                     both(h2, slice(None), k), k == 0, k == DC - 1)
                mm.then_inc(slot_done, 1)
            for s in range(2):
                w = [v.rearrange("p (k n) -> p k n", n=HALF) for v in split_weights(pe, FIRST["q"] + s)]
                for kk in range(4):
                    k = 4 * s + kk
                    for a in range(NT):
                        mm = product(bank[a][:, :], tile(k, a), both(w, slice(None), kk), k == 0, k == DC - 1)
                mm.then_inc(slot_done, 1)
            pe.wait_ge(conv2_done, XC)
            wide2(pe, FIRST["z"], 4, h2, 4)
            pe.wait_ge(qk_roped, NT)
            pe.wait_ge(kv_evac, NT)
            pe.wait_ge(dt_read, 1)
            for a in range(NT):
                for j in range(GJ):
                    nc.tensor.transpose(bank[j // 2][:, (j % 2) * T + a * P:(j % 2) * T + (a + 1) * P], qr[:, a, j * P:(j + 1) * P], ident)
                mm = nc.tensor.transpose(bank[2][:, a * P:(a + 1) * P], qr[:, a, GH * N:HD], ident)
            mm.then_inc(qk_turned, 1)

            def scores(i):
                j, g = i // GKV, i % GKV
                if i >= 2:
                    pe.wait_ge(sm_exp, H + i - 1)
                for a in range(NT):
                    mm = nc.tensor.matmul(bank[g][:, a * T:(a + 1) * T], qgT[g * N:(g + 1) * N, j, a * P:(a + 1) * P],
                                          kgT[g * N:(g + 1) * N, :], start=True, stop=True)
                mm.then_inc(s_mm, 1)

            def turn_p(i):
                pe.wait_ge(p_ready, H // 2 + i + 1)
                if i >= 1:
                    pe.wait_ge(pt_evac, H + i)
                for b in range(NT):
                    for a in range(NT):
                        mm = nc.tensor.transpose(bank[2][:, b * T + a * P:b * T + (a + 1) * P],
                                                 gp_buf[i % 3][:, a * T + b * P:a * T + (b + 1) * P], ident)
                mm.then_inc(pt_mm, 1)

            def values(i):
                j, g = i // GKV, i % GKV
                pe.wait_ge(pt_evac, H + i + 1)
                if i == 4:
                    pe.wait_ge(o_split, 8 + 1)
                for b in range(NT):
                    mm = nc.tensor.matmul(bank[3][g * N:(g + 1) * N, (j % 2) * T:(j % 2 + 1) * T],
                                          vg[:, b, g * N:(g + 1) * N], gpt_buf[i % 2][:, b * T:(b + 1) * T],
                                          start=(b == 0), stop=(b == NT - 1))
                mm.then_inc(pv_mm, 1)

            def attention_step(k):
                if k < GH:
                    scores(k)
                if 1 <= k <= GH:
                    turn_p(k - 1)
                if k >= 2:
                    values(k - 2)

            def second_gate(s):
                attention_step(4 + s)
                if s == 0:
                    pe.wait_ge(gate_evac, 4)

            pe.wait_ge(qk_in, 3)
            pe.wait_ge(z_evac, 4)
            wide2(pe, FIRST["gates"], 4, h2, 4, between=attention_step)
            wide2(pe, FIRST["gates"] + 4, 4, h2, 4, between=second_gate)
            attention_step(GH)
            pe.wait_ge(xc_done, XC)
            pe.wait_ge(sm_exp, H + GH)
            for g in range(2):
                for b in range(NT):
                    mm = nc.tensor.matmul(bank[g][:, b * T:(b + 1) * T], xcT[:, 8 + g, b * P:(b + 1) * P], xcT[:, 10 + g, :],
                                          start=True, stop=True)
                mm.then_inc(cb_mm, 1)
            attention_step(GH + 1)
            for j in range(4):
                pe.wait_ge(gate_evac, 5 + j)
                for i in range(4):
                    a, c = j // 2, 4 * (j % 2) + i
                    mm = nc.tensor.transpose(bank[4 + j][:, i * P:(i + 1) * P], xcT[:, c, a * P:(a + 1) * P], ident)
                mm.then_inc(xs_turned, 1)

            pe.wait_ge(adt_ready, 1)
            for i, (mask, cells) in enumerate((("after", adt[:, 0, 0:H]), ("upto", adt[:, 1, 0:H]),
                                               ("before", adt[:, 1, H:2 * H]), ("from", adt[:, 0, H:2 * H]))):
                mm = nc.tensor.matmul(bank[2][:, i * H:(i + 1) * H], const(mask), cells, start=True, stop=True)
            mm.then_inc(carry_mm, 1)
            pe.wait_ge(cb_in, 2)
            pe.wait_ge(xs_in, 4)
            pe.wait_ge(o_split, 8 + 2)
            xf, xb = toks(B_XF), toks(B_XB)

            def segments(h):
                pe.wait_ge(lhs_ready, h + 1)
                if h >= 2:
                    pe.wait_ge(e_ready, h - 1)
                for n, right in enumerate(("upto", "upto", "from", "from")):
                    mm = nc.tensor.matmul(bank[h % 2][:, n * P:(n + 1) * P], seg_lhs[h % 2][:, n, :], const(right), start=True, stop=True)
                mm.then_inc(seg_mm, 1)

            def mix_tokens(h):
                pe.wait_ge(m_ready, h + 1)
                hv = slice(h * N, (h + 1) * N)
                for a in range(NT):
                    for i, xd in enumerate((xf, xb)):
                        mm = nc.tensor.matmul(bank[4 + 2 * a + h // 8][:, (h % 8) * N:(h % 8 + 1) * N],
                                              e_buf[h % 3][:, (2 * i + a) * P:(2 * i + a + 1) * P], xd[:, a, hv],
                                              start=(i == 0), stop=(i == 1))
                mm.then_inc(ssd_mm, 1)

            def carry(d):
                pe.wait_ge(carried, d + 1)
                if d == 0:
                    pe.wait_ge(carry_ready, 1)
                else:
                    pe.wait_ge(off_scaled, 2)
                for g in range(2):
                    nc.tensor.matmul(bank[2 + g][:, :], cb[g][:, 4 + d, :], buf(B_P, d * D + g * HALF, d * D + (g + 1) * HALF),
                                     start=True, stop=True).then_inc(off_mm, 1)

            for h in range(H):
                segments(h)
                if h == 2:
                    pe.wait_ge(xd_f_ready, 1)
                    pe.wait_ge(xd_b_ready, 1)
                if h >= 2:
                    mix_tokens(h - 2)
                if h == 5:
                    carry(0)
                if h == 9:
                    carry(1)
            mix_tokens(H - 2)
            mix_tokens(H - 1)
            pe.wait_ge(e_ready, H)
            pe.wait_ge(off_scaled, 4)
            wide2(pe, FIRST["attn_proj"], 2, chan2(B_OT, B_OT_LO), 0)
            pe.wait_ge(attn_gated, 4)

            def y_turn(a):
                pe.wait_ge(yn_ready, a + 1)
                turn_pe(toks(B_Y)[:, a, :], 0, a)

            def mix_turn(a):
                pe.wait_ge(mix_ready, a + 1)
                turn_pe(toks(B_MIX)[:, a, :], 0, a)

            wide2(pe, FIRST["ssd_proj"], 4, chan2(B_SQ, B_SQ_LO), 4, TURN_SSD, y_turn, told=ssd_rows)
            wide2(pe, FIRST["w_out"], 4, chan2(B_T2, B_T2_LO), 4, TURN_MIX, mix_turn, rows=True)

        def block_act(act):
            ahead(act, FIRST["xbc"] + 1, split_act)
            after_slots(act, "kvdt")
            for a in range(NT):
                nc.scalar.activation(qk[:, a, GH * N:HD], bank[2 + a][:, 0:P], ACT.Copy)
                nc.scalar.activation(vg[:, a, :], bank[2 + a][:, P:2 * P], ACT.Copy).then_inc(kv_evac, 1)
            ahead(act, FIRST["xbc"] + AHEAD, split_act)
            for c in range(XC):
                act.wait_ge(conv2_done, c + 1)
                nc.scalar.activation(xcT[:, c, :], xc_acc[c % 4], ACT.Silu).then_inc(xc_done, 1)
                if c % 2 == 1:
                    ahead(act, FIRST["xbc"] + c // 2 + 1 + AHEAD, split_act)
            ahead(act, LAST["q"] + 2, split_act)
            after_slots(act, "q")
            for a in range(NT):
                nc.scalar.activation(qk[:, a, 0:GH * N].rearrange("p (j g d) -> p g j d", g=GKV, d=N),
                                     bank[a][:, :].rearrange("p (g j d) -> p g j d", g=GKV, d=N), ACT.Copy).then_inc(qg_evac, 1)
            act.wait_ge(qg_evac, NT)
            act.wait_ge(kv_evac, NT)
            nc.scalar.activation(buf(B_P, 0, NT * HD), buf(B_QK, 0, NT * HD), ACT.Square).then_inc(squared, 1)
            ahead(act, LAST["z"] + AHEAD, split_act)
            after_slots(act, "z")
            for j in range(4):
                nc.scalar.activation(buf(B_Z, j * HALF, (j + 1) * HALF), bank[4 + j][:, :], ACT.Silu).then_inc(z_evac, 1)
            act.wait_ge(blk_params, 16 * 7)
            act.wait_ge(dt_neg, 1)
            nc.scalar.activation(dt_e, dt_n, ACT.Exp).then_inc(dt_exp, 1)
            act.wait_ge(dt_exp, 1)
            nc.scalar.activation(dt_l, dt_e, ACT.Ln, bias=1.0).then_inc(dt_ln, 1)
            nc.scalar.activation(a_log[:, 0, :], a_log[:, 0, :], ACT.Exp).then_inc(a_exp, 1)

            def exps(i):
                act.wait_ge(sm_max, H + i + 1)
                if i >= 3:
                    act.wait_ge(pt_mm, H + i - 2)
                for a in range(NT):
                    op = nc.scalar.activation(gp_buf[i % 3][:, a * T:(a + 1) * T], bank[i % GKV][:, a * T:(a + 1) * T], ACT.Exp,
                                              bias=g_nmax[:, 2 * i + a:2 * i + a + 1], scale=GQA_SCALE,
                                              accum_out=g_sum[:, 2 * i + a:2 * i + a + 1])
                op.then_inc(sm_exp, 1)

            def evac(i):
                act.wait_ge(pt_mm, H + i + 1)
                if i >= 2:
                    act.wait_ge(pv_mm, H + i - 1)
                nc.scalar.activation(gpt_buf[i % 2], bank[2][:, :], ACT.Copy).then_inc(pt_evac, 1)

            def gate(g):
                after_slots(act, "gates", 4 * (g + 1))
                for j in range(4):
                    nc.scalar.activation(buf((B_GA, B_GS)[g], j * HALF, (j + 1) * HALF), bank[4 + j][:, :], ACT.Sigmoid).then_inc(gate_evac, 1)

            def outputs(b):
                act.wait_ge(pv_mm, H + 4 * (b + 1))
                nc.scalar.activation(buf(B_OT, b * HALF, (b + 1) * HALF, arena12), bank[3][:, :], ACT.Copy).then_inc(o_in, 1)

            for k in range(GH):
                if k == 4:
                    gate(0)
                exps(k)
                if k >= 1:
                    evac(k - 1)
                if k == 5:
                    outputs(0)
                ahead(act, FIRST["gates"] + k + 2, split_act)
            evac(GH - 1)
            gate(1)
            for j in range(4):
                act.wait_ge(xs_turned, j + 1)
                nc.scalar.activation(buf(B_XS, j * HALF, (j + 1) * HALF), bank[4 + j][:, :], ACT.Copy).then_inc(xs_in, 1)
            outputs(1)
            act.wait_ge(carry_mm, 1)
            nc.scalar.activation(carry_decay, bank[2][:, 0:4 * H], ACT.Exp).then_inc(carry_ready, 1)
            for h in range(H):
                if h in (2, 12):
                    ahead(act, FIRST["ssd_proj"] + h // 12, split_act)
                act.wait_ge(seg_mm, h + 1)
                if h >= 3:
                    act.wait_ge(ssd_mm, h - 2)
                nc.scalar.activation(e_buf[h % 3], bank[h % 2][:, :], ACT.Exp).then_inc(e_ready, 1)
            for a in range(NT):
                act.wait_ge(yz_ready, a + 1)
                nc.scalar.activation(buf(B_SQ, a * D, (a + 1) * D), toks(B_Y)[:, a, :], ACT.Square, scale=MEAN,
                                     accum_out=yg_ss[:, a:a + 1]).then_inc(squared, 1)
            turn_act(act, TURN_SSD, 0, 0, B_SQ)
            ahead(act, LAST["ssd_proj"], split_act)
            turn_act(act, TURN_SSD, 1, 0, B_SQ)
            ahead(act, LAST["ssd_proj"] + 1, split_act)
            turn_act(act, TURN_MIX, 0, 0, B_T2)
            ahead(act, LAST["w_out"], split_act)
            turn_act(act, TURN_MIX, 1, 0, B_T2)

        def block_dve(dve):
            ahead(dve, FIRST["xbc"], split_dve)
            emitted[dve] = LAST["z"] + 1
            dve.wait_ge(blk_params, 16 * 7)
            dve.wait_ge(kv_evac, NT)
            for a in range(NT):
                op = nc.vector.tensor_tensor(dt_x[:, a, :], bank[2 + a][:, 2 * P:2 * P + 32], dt_bias[:, 0, :], ALU.add)
            op.then_inc(dt_read, 1)
            dve.wait_ge(dt_read, 1)
            nc.vector.scalar_tensor_tensor(dt_n, dt_x, -1.0, dt_x, ALU.mult, ALU.min).then_inc(dt_neg, 1)
            for c in range(XC):
                u = bank[4 + (c // 2) % 4][:, (c % 2) * T:(c % 2 + 1) * T]
                acc = xc_acc[c % 4]
                after_slots(dve, "xbc", c // 2 + 1)
                if c >= 4:
                    dve.wait_ge(xc_done, c - 3)
                link(dve, nc.vector.tensor_scalar(acc, u, col("conv_w_2", 2 * XC + c), col("conv_b_2", c), ALU.mult, ALU.add))
                for j in (0, 1, 3, 4):
                    shift = j - 2
                    dst = slice(max(0, -shift), T - max(0, shift))
                    src = slice(max(0, shift), T - max(0, -shift))
                    op = nc.vector.scalar_tensor_tensor(acc[:, dst], u[:, src], col("conv_w_2", j * XC + c), acc[:, dst],
                                                        ALU.mult, ALU.add)
                    if j < 4:
                        link(dve, op)
                op.then_inc(conv2_done, 1)
            dve.wait_ge(squared, 8 + 1)
            nh = GH + GKV
            link(dve, nc.vector.tensor_reduce(qk_ss, buf(B_P, 0, NT * HD).rearrange("p (h n) -> p h n", n=N), AX, ALU.add))
            nc.vector.tensor_scalar(qk_var, qk_ss, 1.0 / N, EPS, ALU.mult, ALU.add).then_inc(var_ready, 1)
            dve.wait_ge(rstd_ready, 4 + 1)
            qk_flat = buf(B_QK, 0, NT * HD).rearrange("p (h n) -> p h n", n=N)
            link(dve, nc.vector.tensor_tensor(qk_flat, qk_flat, spread(qk_rstd.unsqueeze(2), [P, NT * nh, N]), ALU.mult))
            link(dve, nc.vector.tensor_tensor(qk, qk, spread(qk_gain.unsqueeze(1), [P, NT, HD]), ALU.mult))
            for a in range(NT):
                src = qk[:, a, :].rearrange("p (h r n) -> p h r n", r=2, n=32)
                dst = qr[:, a, :].rearrange("p (h r n) -> p h r n", r=2, n=32)
                t0, t1 = (x.rearrange("p (h r n) -> p h r n", r=2, n=16) for x in rot_tmp)
                cos, sin = (spread(const(n, a * 32, (a + 1) * 32).rearrange("p (r n) -> p r n", r=2).unsqueeze(1),
                                   [P, nh, 2, 16]) for n in ("acos", "asin"))
                x1, x2 = src[:, :, :, 0:16], src[:, :, :, 16:32]
                for lo, f1, f2, op in ((0, cos, sin, ALU.subtract), (16, sin, cos, ALU.add)):
                    nc.vector.tensor_tensor(t0, x1, f1, ALU.mult)
                    link(dve, nc.vector.tensor_tensor(t1, x2, f2, ALU.mult))
                    last = nc.vector.tensor_tensor(dst[:, :, :, lo:lo + 16], t0, t1, op)
                    if lo == 0:
                        link(dve, last)
                last.then_inc(qk_roped, 1)
                dve.wait_ge(qk_roped, a + 1)
            dve.wait_ge(split_ready, SPLIT_NO[LAST["z"]] + 1)
            ahead(dve, FIRST["gates"] + 1, split_dve)
            dve.wait_ge(qk_turned, 1)
            nc.vector.tensor_copy(buf(B_QT, 0, HALF), bank[0][:, :]).then_inc(qk_in, 1)
            nc.vector.tensor_copy(buf(B_QT, HALF, 2 * HALF), bank[1][:, :]).then_inc(qk_in, 1)
            nc.vector.tensor_copy(kgT, bank[2][:, 0:T]).then_inc(qk_in, 1)
            dve.wait_ge(dt_ln, 1)
            dve.wait_ge(a_exp, 1)
            link(dve, nc.vector.scalar_tensor_tensor(dt, dt_x, 0.0, dt_l, ALU.max, ALU.add))
            for a in range(NT):
                op = nc.vector.scalar_tensor_tensor(adt[:, a, :], a_log[:, 0, :], -1.0, dt[:, a, :], ALU.mult, ALU.mult)
            op.then_inc(adt_ready, 1)

            def maxima(i):
                dve.wait_ge(s_mm, H + i + 1)
                link(dve, nc.vector.tensor_reduce(g_max[:, 2 * i:2 * i + 2], bank[i % GKV][:, :].rearrange("p (a t) -> p a t", t=T),
                                                  AX, ALU.max))
                nc.vector.tensor_scalar(g_nmax[:, 2 * i:2 * i + 2], g_max[:, 2 * i:2 * i + 2], -GQA_SCALE, None,
                                        ALU.mult).then_inc(sm_max, 1)

            def normalize(i):
                dve.wait_ge(sm_exp, H + i + 1)
                link(dve, nc.vector.reciprocal(g_inv[:, 2 * i:2 * i + 2], g_sum[:, 2 * i:2 * i + 2]))
                for a in range(NT):
                    p = gp_buf[i % 3][:, a * T:(a + 1) * T]
                    op = nc.vector.tensor_scalar(p, p, g_inv[:, 2 * i + a:2 * i + a + 1], None, ALU.mult)
                op.then_inc(p_ready, 1)

            def outputs(b):
                dve.wait_ge(o_in, 8 + b + 1)
                at = slice(b * HALF, (b + 1) * HALF)
                nc.vector.tensor_tensor(buf(B_OT_LO, mem=arena12)[:, at], bank[3][:, :], buf(B_OT, mem=arena12)[:, at].bitcast(F32),
                                        ALU.subtract).then_inc(o_split, 1)

            for k in range(GH):
                maxima(k)
                normalize(k)
                if k == 5:
                    outputs(0)
                ahead(dve, FIRST["gates"] + k + 2, split_dve)
            for g in range(2):
                dve.wait_ge(cb_mm, g + 1)
                blocks = bank[g][:, :].rearrange("p (n l) -> p n l", l=P)
                for i, mask in ((0, "upto"), (2, "from")):
                    nc.vector.tensor_tensor(cb[g][:, i:i + 2, :], blocks[:, 0:4:3, :],
                                            spread(const(mask).unsqueeze(1), [P, 2, P]), ALU.mult)
                nc.vector.tensor_copy(cb[g][:, 4:6, :], blocks[:, 1:3, :]).then_inc(cb_in, 1)
            def left_sides(h):
                if h >= 2:
                    dve.wait_ge(seg_mm, h - 1)
                l = seg_lhs[h % 2]
                f, b = adt[:, :, h:h + 1], adt[:, :, H + h:H + h + 1]
                for n, (mask, c) in enumerate((("after", f[:, 0]), ("after", f[:, 1]), ("before", b[:, 0]), ("before", b[:, 1]))):
                    op = nc.vector.tensor_scalar(l[:, n, :], const(mask), c, None, ALU.mult)
                op.then_inc(lhs_ready, 1)

            dve.wait_ge(adt_ready, 1)
            left_sides(0)

            outputs(1)
            dve.wait_ge(xs_in, 4)
            nc.vector.tensor_tensor(toks(B_XB).rearrange("p a (h n) -> p a h n", n=N), toks(B_XS).rearrange("p a (h n) -> p a h n", n=N),
                                    spread(dt[:, :, H:2 * H].unsqueeze(3), [P, NT, H, N]), ALU.mult).then_inc(xd_b_ready, 1)

            emitted[dve] = FIRST["ssd_proj"] + 1

            def matrices(h):
                dve.wait_ge(e_ready, h + 1)
                nc.vector.tensor_tensor(e_buf[h % 3], e_buf[h % 3], buf(B_CB, (h // 8) * 768, (h // 8) * 768 + HALF),
                                        ALU.mult).then_inc(m_ready, 1)

            def carried_on(d):
                for g in range(2):
                    dve.wait_ge(off_mm, 2 * d + g + 1)
                    decay = carry_decay[:, (2 * d + 1) * H + 8 * g:(2 * d + 1) * H + 8 * (g + 1)]
                    nc.vector.tensor_tensor(buf(B_P, d * D + g * HALF, d * D + (g + 1) * HALF).rearrange("p (h n) -> p h n", n=N),
                                            bank[2 + g][:, :].rearrange("p (h n) -> p h n", n=N),
                                            spread(decay.unsqueeze(2), [P, 8, N]), ALU.mult).then_inc(off_scaled, 1)

            for h in range(H):
                if h + 1 < H:
                    left_sides(h + 1)
                matrices(h)
                if h in (7, 11):
                    carried_on(h // 4 - 1)
            dve.wait_ge(ssd_mm, H)
            dve.wait_ge(dx_ready, 1 + NT)
            y = toks(B_Y)
            for a in range(NT):
                for q in range(2):
                    cells = slice(q * HALF, (q + 1) * HALF)
                    op = nc.vector.tensor_tensor(y[:, a, cells], bank[4 + 2 * a + q][:, :], toks(B_DX)[:, a, cells], ALU.add)
                link(dve, op)
                nc.vector.tensor_tensor(y[:, a, :], y[:, a, :], toks(B_Z)[:, a, :], ALU.mult).then_inc(yz_ready, 1)
            dve.wait_ge(split_ready, SPLIT_NO[FIRST["ssd_proj"]] + 1)
            ahead(dve, FIRST["ssd_proj"] + 1, split_dve)
            for a in range(NT):
                dve.wait_ge(squared, 9 + a + 1)
                nc.vector.tensor_scalar(yg_var[:, a:a + 1], yg_ss[:, a:a + 1], EPS, None, ALU.add).then_inc(var_ready, 1)
            dve.wait_ge(yg_gain_landed, 16)
            for a in range(NT):
                dve.wait_ge(rstd_ready, 5 + a + 1)
                nc.vector.scalar_tensor_tensor(y[:, a, :], y[:, a, :], yg_rstd[:, a:a + 1], yg_gain, ALU.mult,
                                               ALU.mult).then_inc(yn_ready, 1)
            after_slots(dve, "attn_proj")
            for j in range(4):
                nc.vector.tensor_tensor(buf(B_MIX, j * HALF, (j + 1) * HALF), bank[j][:, :], buf(B_GA, j * HALF, (j + 1) * HALF),
                                        ALU.mult).then_inc(attn_gated, 1)
            turn_dve(dve, TURN_SSD, 0, 0, B_SQ, B_SQ_LO)
            ahead(dve, LAST["ssd_proj"], split_dve)
            turn_dve(dve, TURN_SSD, 1, 0, B_SQ, B_SQ_LO)
            dve.wait_ge(attn_gated, 4)
            for a in range(NT):
                if a == 0:
                    dve.wait_ge(ssd_rows, 1)
                else:
                    ahead(dve, LAST["ssd_proj"] + 1, split_dve)
                    after_slots(dve, "ssd_proj")
                for half in range(2):
                    j = 2 * a + half
                    op = nc.vector.tensor_tensor(buf(B_GATED, j * HALF, (j + 1) * HALF), bank[4 + j][:, :],
                                                 buf(B_GS, j * HALF, (j + 1) * HALF), ALU.mult)
                link(dve, op)
                nc.vector.tensor_tensor(toks(B_MIX)[:, a, :], toks(B_MIX)[:, a, :], toks(B_GATED)[:, a, :], ALU.add).then_inc(mix_ready, 1)
            turn_dve(dve, TURN_MIX, 0, 0, B_T2, B_T2_LO)
            ahead(dve, LAST["w_out"], split_dve)
            turn_dve(dve, TURN_MIX, 1, 0, B_T2, B_T2_LO)

        def block_params_sp(sp):
            sp.wait_ge(x_updated, 4 * 4)
            gain = qk_gain.rearrange("p (h n) -> p h n", n=N)
            sp.dma_start(gain[:, 0:GH, :], spread(A["q_norm_2"][0].partition_broadcast(P).unsqueeze(1), [P, GH, N])).then_inc(blk_params, 16)
            sp.dma_start(gain[:, GH:, :], spread(A["k_norm_2"][0].partition_broadcast(P).unsqueeze(1), [P, GKV, N])).then_inc(blk_params, 16)
            for dst, names in ((dt_bias, ("dt_bias_f_2", "dt_bias_b_2")), (a_log, ("a_log_f_2", "a_log_b_2"))):
                for i, name in enumerate(names):
                    sp.dma_start(dst[:, 0, i * H:(i + 1) * H], A[name][0].partition_broadcast(P)).then_inc(blk_params, 16)
            sp.dma_start(d_skip, A["d_skip_2"][0].partition_broadcast(P)).then_inc(blk_params, 16)

        def block_pool(pool):
            pool.wait_ge(split_ready, SPLIT_NO[FIRST["xbc"]] + 1)
            for n in range(FIRST["xbc"] + 1, FIRST["z"] + 2):
                split_lo(pool, nc.gpsimd, n)
            pool.wait_ge(var_ready, 4 + 1)
            nc.gpsimd.tensor_tensor(qk_rstd, qk_var, minus_half[:, 0:NT * (GH + GKV)], ALU.pow).then_inc(rstd_ready, 1)
            for n in range(FIRST["z"] + 2, LAST["z"] + 1):
                split_lo(pool, nc.gpsimd, n)
            pool.wait_ge(adt_ready, 1)
            pool.wait_ge(xs_in, 4)
            xs = toks(B_XS).rearrange("p a (h n) -> p a h n", n=N)
            nc.gpsimd.tensor_tensor(toks(B_XF).rearrange("p a (h n) -> p a h n", n=N), xs,
                                    spread(dt[:, :, 0:H].unsqueeze(3), [P, NT, H, N]), ALU.mult).then_inc(xd_f_ready, 1)
            pool.wait_ge(blk_params, 16 * 7)
            pool.wait_ge(xd_b_ready, 1)
            nc.gpsimd.tensor_tensor(xs, xs, spread(d_skip.unsqueeze(1).unsqueeze(3), [P, NT, H, N]), ALU.mult).then_inc(dx_ready, 1)
            pool.wait_ge(carry_ready, 1)
            pool.wait_ge(xd_f_ready, 1)
            pool.wait_ge(o_split, 8 + 2)
            for d, xd in enumerate((toks(B_XF)[:, 0, :], toks(B_XB)[:, 1, :])):
                nc.gpsimd.tensor_tensor(buf(B_P, d * D, (d + 1) * D).rearrange("p (h n) -> p h n", n=N),
                                        xd.rearrange("p (h n) -> p h n", n=N),
                                        spread(carry_decay[:, 2 * d * H:(2 * d + 1) * H].unsqueeze(2), [P, H, N]),
                                        ALU.mult).then_inc(carried, 1)
            pool.wait_ge(dx_ready, 1)
            pool.wait_ge(split_ready, SPLIT_NO[LAST["attn_proj"]] + 1)
            split_lo(pool, nc.gpsimd, FIRST["ssd_proj"])
            for d in range(2):
                pool.wait_ge(off_scaled, 2 * (d + 1))
                dx = toks(B_DX)[:, 1 - d, :]
                nc.gpsimd.tensor_tensor(dx, dx, buf(B_P, d * D, (d + 1) * D), ALU.add).then_inc(dx_ready, 1)
            pool.wait_ge(seg_mm, H)
            pool.dma_start(yg_gain, A["ssd_norm_2"][0].partition_broadcast(P)).then_inc(yg_gain_landed, 16)
            for a in range(NT):
                pool.wait_ge(var_ready, 5 + a + 1)
                nc.gpsimd.tensor_tensor(yg_rstd[:, a:a + 1], yg_var[:, a:a + 1], minus_half[:, 0:1], ALU.pow).then_inc(rstd_ready, 1)

        def weights_sp(sp):
            def into(n, width=SLOT):
                if n >= RING:
                    sp.wait_ge(slot_done, n - RING + 1)
                return ring[:, n % RING, 0:width]

            def send(n, dst, src):
                sp.dma_start(dst, src).then_inc(landed[n % RING], 16)

            def rows_of(name, w, chunks):
                count = {k: c for k, c, _ in PLAN}[name]
                for s in range(count):
                    n = FIRST[name] + s
                    dst = into(n, chunks * w.shape[1]).rearrange("p (k n) -> p k n", k=chunks)
                    send(n, dst, w[s * chunks * P:(s + 1) * chunks * P, :].rearrange("(k p) n -> p k n", p=P))

            def columns_of(name, w, width):
                chunks = w.shape[0] // P
                for s in range({k: c for k, c, _ in PLAN}[name]):
                    n = FIRST[name] + s
                    dst = into(n, chunks * width).rearrange("p (k n) -> p k n", k=chunks)
                    send(n, dst, w[:, s * width:(s + 1) * width].rearrange("(k p) n -> p k n", p=P))

            def ffn(f, w_in, w_out):
                src = w_in.rearrange("(k p) (g n) -> p k g n", p=P, g=2)
                first = FIRST[f"ffn_in{f}"]

                def tile(it, j):
                    r = (first + j) % RING
                    sp.wait_ge(slot_done, it * RING + (first + j - RING + 1))
                    at = slice((it * RING + j) * P, (it * RING + j + 1) * P) if isinstance(it, int) else bass.ds(it * (RING * P) + j * P, P)
                    dst = ring[:, r, :].rearrange("p (k g n) -> p k g n", k=DC, g=2)
                    for g in range(2):
                        sp.dma_start(dst[:, :, g, :], src[:, :, g, at]).then_inc(landed[r], 16)

                rounds(sp, tile)
                for s in range(FC // 2):
                    n = FIRST[f"ffn_out{f}"] + s
                    dst = into(n).rearrange("p (k n) -> p k n", k=2)
                    for k in range(2):
                        send(n, dst[:, k, :], w_out[(2 * s + k) * P:(2 * s + k + 1) * P, :])

            n = FIRST["lora_wa"]
            dst = into(n, 2 * DC * 64).rearrange("p (g k n) -> p g k n", g=2, k=DC)
            for g, w in enumerate(("a_w1", "a_a1")):
                send(n, dst[:, g], A[w][0].rearrange("(k p) n -> p k n", p=P))
            columns_of("w_k", A["a_w_rkv"][0, 1], T)
            n = FIRST["lora_wa2"]
            dst = into(n)
            for g, w in enumerate(("a_w2", "a_a2")):
                send(n, dst[0:64, g * D:(g + 1) * D], A[w][0])
            columns_of("w_r", A["a_w_rkv"][0, 0], T)
            columns_of("lora_g", A["a_g1"][0], GATE_LORA)
            n = FIRST["lora_g2"]
            dst = into(n)
            send(n, dst[:, 0:D], A["a_g2"][0, 0:P])
            send(n, dst[0:GATE_LORA - P, D:2 * D], A["a_g2"][0, P:GATE_LORA])
            rows_of("w_v", A["a_w_rkv"][0, 2], 2)
            rwkv_blocks_sp(sp)
            rows_of("w_o", A["a_w_o"][0], 2)
            ffn(0, A["ffn_w_in"][0], A["ffn_w_out"][0])
            rows_of("kv_down", A["kv_w_down"], 4)
            rows_of("q_down", A["q_w_down"][0], 4)
            columns_of("kv_up", A["kv_w_up"], D)
            columns_of("q_up", A["q_w_up"][0], 4 * QK)
            rows_of("o_w", A["o_w"][0], 2)
            ffn(1, A["ffn_w_in"][1], A["ffn_w_out"][1])
            w_in = A["w_in_2"][0]
            at_z = GH * N + 2 * GKV * N
            at_x = at_z + D
            at_dt = at_x + XC * P
            at_g = at_dt + 2 * H
            for s in range(2):
                n = FIRST["kvdt"] + s
                dst = into(n, 4 * 288).rearrange("p (k n) -> p k n", k=4)
                part = w_in[s * HALF:(s + 1) * HALF, :].rearrange("(k p) n -> p k n", p=P)
                send(n, dst[:, :, 0:2 * P], part[:, :, GH * N:at_z])
                send(n, dst[:, :, 2 * P:288], part[:, :, at_dt:at_g])
            block_params_sp(sp)
            columns_of("xbc", w_in[:, at_x:at_dt], T)
            rows_of("q", w_in[:, 0:GH * N], 4)
            rows_of("z", w_in[:, at_z:at_x], 2)
            for g in range(2):
                for s in range(4):
                    n = FIRST["gates"] + 4 * g + s
                    send(n, into(n).rearrange("p (k n) -> p k n", k=2),
                         w_in[s * T:(s + 1) * T, at_g + g * D:at_g + (g + 1) * D].rearrange("(k p) n -> p k n", p=P))
            proj = A["w_attn_proj_2"][0].rearrange("(g j d) n -> g d j n", g=GKV, j=GJ)
            for s in range(2):
                n = FIRST["attn_proj"] + s
                dst = into(n).rearrange("p (k n) -> p k n", k=2)
                for g in range(GKV):
                    send(n, dst[g * N:(g + 1) * N], proj[g, :, 2 * s:2 * s + 2, :])
            rows_of("ssd_proj", A["w_ssd_proj_2"][0], 2)
            rows_of("w_out", A["w_out_2"][0], 2)
            ffn(2, A["w_gate_up_2"][0], A["w_down_2"][0])

        BETWEEN = [[(TURN_PRE1, 4, FFN_H, FFN_H_LO, None, XN_FFN0)],
                   [(TURN_XKV, 4, M_XKV, M_XKV_LO, buf(GAIN_KV, 0, D), XN_KV), (TURN_PRE2, 0, M_H, M_H_LO, None, XN)],
                   [(TURN_PRE3, 4, FFN_H, FFN_H_LO, None, XN)], [(TURN_PRE4, 4, B_H, B_H_LO, None, XN)],
                   [(TURN_PRE5, 4, FFN_H, FFN_H_LO, None, XN)]]

        block = ctx.enter_context(nc.Block())

        @block.sync
        def _(sp):
            start_sp(sp)
            weights_sp(sp)
            for a in range(NT):
                sp.wait_ge(x_updated, 4 * 5 + 2 * (a + 1))
                sp.dma_start(out[0, a * P:(a + 1) * P, :], x_sb[:, a, :]).then_inc(out_stored, 16)
            sp.wait_ge(out_stored, 16 * NT)

        @block.gpsimd
        def _(pool):
            start_pool(pool)
            for a in range(NT):
                pre_root(pool, 0, a)
            load_gains(pool, 0, A["norm_g"][0, 1], A["norm_g"][0, 2])
            pool.wait_ge(const_landed, 16)
            rwkv_pool(pool)
            between_pool(pool, 0)
            load_gains(pool, 1, A["norm_g"][0, 3], A["norm_g"][1, 0])
            pool.dma_start(buf(GAIN_KV, 0, D), A["kv_norm_g"].partition_broadcast(P)).then_inc(kv_gain_landed, 16)
            ffn_pool(pool, 0)
            between_pool(pool, 1)
            load_gains(pool, 2, A["norm_g"][1, 1], A["norm_g"][1, 2])
            mla_pool(pool)
            between_pool(pool, 2)
            load_gains(pool, 3, A["norm_g"][1, 3], A["norm1_pre_2"][0])
            ffn_pool(pool, 1)
            between_pool(pool, 3)
            load_gains(pool, 4, A["norm1_post_2"][0], A["norm2_pre_2"][0])
            block_pool(pool)
            between_pool(pool, 4)
            load_gains(pool, 5, A["norm2_post_2"][0], None)
            ffn_pool(pool, 2)
            for a in range(NT):
                post_root(pool, 5, a)

        @block.tensor
        def _(pe):
            start_pe(pe)
            rwkv_pe(pe)
            ffn_pe(pe, 0, 1, TURN_PRE1)
            mla_pe(pe)
            ffn_pe(pe, 1, 3, TURN_PRE3)
            block_pe(pe)
            ffn_pe(pe, 2, 5, TURN_PRE5)

        @block.scalar
        def _(act):
            start_act(act)
            for a in range(NT):
                x_squares(act, 0, a)
            for a in range(NT):
                turn_act(act, TURN_PRE0, a, 4, W_HT)
            act.wait_ge(cols_ready, 1)
            rwkv_act(act)
            between_act(act, 0, BETWEEN[0], LAST["w_o"])
            ffn_act(act, 0)
            ahead(act, LAST["ffn_out0"], split_act)
            between_act(act, 1, BETWEEN[1], LAST["ffn_out0"])
            mla_act(act)
            between_act(act, 2, BETWEEN[2], LAST["o_w"])
            ffn_act(act, 1)
            ahead(act, LAST["ffn_out1"], split_act)
            between_act(act, 3, BETWEEN[3], LAST["ffn_out1"])
            block_act(act)
            between_act(act, 4, BETWEEN[4], LAST["w_out"])
            ffn_act(act, 2)
            ahead(act, LAST["ffn_out2"], split_act)
            for a in range(NT):
                post_squares(act, 5, a)

        @block.vector
        def _(dve):
            start_dve(dve)
            rwkv_dve(dve)
            between_dve(dve, 0, BETWEEN[0], LAST["w_o"])
            ffn_dve(dve, 0)
            ahead(dve, LAST["ffn_out0"], split_dve)
            between_dve(dve, 1, BETWEEN[1], LAST["ffn_out0"])
            mla_dve(dve)
            between_dve(dve, 2, BETWEEN[2], LAST["o_w"])
            ffn_dve(dve, 1)
            ahead(dve, LAST["ffn_out1"], split_dve)
            between_dve(dve, 3, BETWEEN[3], LAST["ffn_out1"])
            block_dve(dve)
            between_dve(dve, 4, BETWEEN[4], LAST["w_out"])
            ffn_dve(dve, 2)
            ahead(dve, LAST["ffn_out2"], split_dve)
            for a in range(NT):
                post_scale(dve, 5, a)
                x_update(dve, 5, a)


INPUTS = ["x", "norm_g", "ffn_w_in", "ffn_conv_w", "ffn_conv_b", "ffn_w_out", "a_mu", "a_w_rkv", "a_w0", "a_w1", "a_w2",
          "a_a0", "a_a1", "a_a2", "a_g1", "a_g2", "a_k_k", "a_k_a", "a_r_k", "a_lnx_w", "a_lnx_b", "a_w_o", "kv_norm_g",
          "kv_w_down", "kv_a_norm_g", "kv_w_up", "q_w_down", "q_norm_g", "q_w_up", "o_w", "w_in_2", "q_norm_2", "k_norm_2",
          "conv_w_2", "conv_b_2", "dt_bias_f_2", "dt_bias_b_2", "a_log_f_2", "a_log_b_2", "d_skip_2", "ssd_norm_2",
          "w_attn_proj_2", "w_ssd_proj_2", "w_out_2", "norm1_pre_2", "norm1_post_2", "norm2_pre_2", "norm2_post_2",
          "w_gate_up_2", "w_down_2"]


def kernel(**inputs):
    import concourse.bacc as bacc
    from concourse.bass_utils import run_bass_kernel_spmd

    nc = bacc.Bacc("TRN2", target_bir_lowering=False, num_devices=1)
    arrays, args = {}, {}
    for name in INPUTS:
        a = np.ascontiguousarray(inputs[name])
        arrays[f"in_{name}"] = a
        args[name] = nc.dram_tensor(f"in_{name}", a.shape, mybir.dt.from_np(a.dtype), kind="ExternalInput").ap()
    arrays["constants"] = np.ascontiguousarray(np.concatenate(list(CONSTANTS.values()), axis=1))
    const_dram = nc.dram_tensor("constants", (P, CONST_W), F32, kind="ExternalInput").ap()
    out = nc.dram_tensor("out", (1, T, D), F32, kind="ExternalOutput").ap()
    build(nc, args, const_dram, out)
    r = run_bass_kernel_spmd(nc, [arrays], core_ids=[0])
    return r.results[0]["out"]
```
